# Optimizing a Trainium2 kernel written in Bass

```python
import jax
import jax.numpy as jnp
from jax import lax
import numpy as np
import math
import jax, jax.numpy as jnp

D_MODEL = 1024
BATCH = 1
SEQ = 256
DEPTH = 2

CHUNK = 64
Q_BLOCK = 128
HEAD_DIM = 64
NEG_INF = -1e30
LN_EPS = 1e-5
RMS_EPS = 1e-6

MLA_HEADS = 8
MLA_Q_RANK = 384
MLA_KV_RANK = 256
MLA_NOPE = 64
MLA_ROPE = 32
MLA_V = 64
ROPE_THETA = 10000.0

SWA_HEADS = 8
SWA_KV_HEADS = 2
SWA_WINDOW = 128
SWA_LEFT_CHUNKS = SWA_WINDOW // CHUNK

FOX_HEADS = 8

CK_HEADS = 8
CK_LEFT_CHUNKS = 8
REL_MAX = 256
REL_TABLE = REL_MAX + CHUNK

D_FF = -(-8 * D_MODEL // (3 * 256)) * 256

DEEPNORM_ALPHA = (2 * DEPTH) ** 0.25
DEEPNORM_BETA = (8 * DEPTH) ** -0.25

AB_SPLITS = (MLA_Q_RANK, MLA_KV_RANK, MLA_ROPE, SWA_HEADS * HEAD_DIM, SWA_KV_HEADS * HEAD_DIM, SWA_KV_HEADS * HEAD_DIM)
CD_SPLITS = (FOX_HEADS * HEAD_DIM,) * 3 + (FOX_HEADS,) + (CK_HEADS * HEAD_DIM,) * 3
AB_MIX = MLA_HEADS * MLA_V + SWA_HEADS * HEAD_DIM
CD_MIX = (FOX_HEADS + CK_HEADS) * HEAD_DIM


def _split_cols(x, widths):
    return jnp.split(x, [int(i) for i in np.cumsum(widths)[:-1]], axis=-1)

def _layer_norm(x, g, b):
    xf = x.astype(jnp.float32)
    mu = jnp.mean(xf, -1, keepdims=True)
    var = jnp.mean(jnp.square(xf - mu), -1, keepdims=True)
    y = (xf - mu) * lax.rsqrt(var + LN_EPS) * g.astype(jnp.float32) + b.astype(jnp.float32)
    return y.astype(x.dtype)

def _rms_norm(x, g):
    xf = x.astype(jnp.float32)
    y = xf * lax.rsqrt(jnp.mean(xf * xf, -1, keepdims=True) + RMS_EPS)
    return (y * g.astype(jnp.float32)).astype(x.dtype)

def _rope_tables(S):
    inv = ROPE_THETA ** (-jnp.arange(0, MLA_ROPE, 2, dtype=jnp.float32) / MLA_ROPE)
    ang = jnp.arange(S, dtype=jnp.float32)[:, None] * inv[None, :]
    return jnp.cos(ang), jnp.sin(ang)

def _apply_rope(x, cos, sin):
    x1, x2 = jnp.split(x.astype(jnp.float32), 2, axis=-1)
    return jnp.concatenate([x1 * cos - x2 * sin, x1 * sin + x2 * cos], -1).astype(x.dtype)

def _alibi_slopes(n):
    return jnp.exp2(-8.0 * jnp.arange(1, n + 1, dtype=jnp.float32) / n)

def _sweep_query_blocks(block_fn, *q_parts):
    B, S = q_parts[0].shape[:2]
    nb = S // Q_BLOCK
    blocked = tuple(jnp.moveaxis(p.reshape(B, nb, Q_BLOCK, *p.shape[2:]), 1, 0) for p in q_parts)
    out = lax.map(lambda a: block_fn(a[0], *a[1]), (jnp.arange(nb), blocked))
    return jnp.moveaxis(out, 0, 1).reshape(B, S, *out.shape[3:])

def _band(x, n_left):
    B, S = x.shape[:2]
    nc = S // CHUNK
    pad = [(0, 0), (n_left * CHUNK, 0)] + [(0, 0)] * (x.ndim - 2)
    xp = jnp.pad(x, pad).reshape(B, nc + n_left, CHUNK, *x.shape[2:])
    return jnp.concatenate([xp[:, j:j + nc] for j in range(n_left + 1)], axis=2)

def _band_geometry(nc, n_left):
    band = jnp.arange((n_left + 1) * CHUNK)
    key_off = band // CHUNK - n_left
    dist = jnp.arange(CHUNK)[:, None] - (key_off * CHUNK + band % CHUNK)[None, :]
    valid = (jnp.arange(nc)[:, None] + key_off[None, :]) >= 0
    return dist, valid

def _mla_attention(q_nope, q_rope, k_nope, k_rope, v):
    S = k_nope.shape[1]
    scale = (MLA_NOPE + MLA_ROPE) ** -0.5
    key_chunk = jnp.arange(S) // CHUNK

    def block(i, qn, qr):
        q_chunk = (i * Q_BLOCK + jnp.arange(Q_BLOCK)) // CHUNK
        logits = (jnp.einsum('bqhd,bkhd->bhqk', qn, k_nope, preferred_element_type=jnp.float32)
                  + jnp.einsum('bqhr,bkr->bhqk', qr, k_rope, preferred_element_type=jnp.float32)) * scale
        logits = jnp.where(key_chunk[None, :] <= q_chunk[:, None], logits, NEG_INF)
        p = jax.nn.softmax(logits, axis=-1).astype(v.dtype)
        return jnp.einsum('bhqk,bkhd->bqhd', p, v)

    return _sweep_query_blocks(block, q_nope, q_rope)

def _swa_sink_attention(q, k, v, sinks):
    B, S, _, d = q.shape
    nc = S // CHUNK
    G = SWA_HEADS // SWA_KV_HEADS
    qc = q.reshape(B, nc, CHUNK, SWA_KV_HEADS, G, d)
    kb, vb = _band(k, SWA_LEFT_CHUNKS), _band(v, SWA_LEFT_CHUNKS)
    dist, valid = _band_geometry(nc, SWA_LEFT_CHUNKS)
    alibi = -_alibi_slopes(SWA_HEADS).reshape(SWA_KV_HEADS, G, 1, 1) * jnp.abs(dist).astype(jnp.float32)
    logits = jnp.einsum('bcqkgd,bcskd->bckgqs', qc, kb, preferred_element_type=jnp.float32) * d ** -0.5 + alibi
    logits = jnp.where(valid[None, :, None, None, None, :], logits, NEG_INF)
    sink = jnp.broadcast_to(sinks.astype(jnp.float32).reshape(SWA_KV_HEADS, G, 1, 1), logits.shape[:-1] + (1,))
    p = jax.nn.softmax(jnp.concatenate([logits, sink], -1), axis=-1)[..., :-1].astype(v.dtype)
    return jnp.einsum('bckgqs,bcskd->bcqkgd', p, vb).reshape(B, S, SWA_HEADS, d)

def _forgetting_attention(q, k, v, f_logit, b_forget):
    S = k.shape[1]
    scale = q.shape[-1] ** -0.5
    cum_log_f = jnp.cumsum(jax.nn.log_sigmoid(f_logit.astype(jnp.float32) + b_forget.astype(jnp.float32)), axis=1)
    cum_k = jnp.swapaxes(cum_log_f, 1, 2)[:, :, None, :]
    key_pos = jnp.arange(S)

    def block(i, qb, cum_q):
        q_pos = i * Q_BLOCK + jnp.arange(Q_BLOCK)
        decay = jnp.swapaxes(cum_q, 1, 2)[..., None] - cum_k
        logits = jnp.einsum('bqhd,bkhd->bhqk', qb, k, preferred_element_type=jnp.float32) * scale + decay
        logits = jnp.where(key_pos[None, :] <= q_pos[:, None], logits, NEG_INF)
        p = jax.nn.softmax(logits, axis=-1).astype(v.dtype)
        return jnp.einsum('bhqk,bkhd->bqhd', p, v)

    return _sweep_query_blocks(block, q, cum_log_f)

def _chunk_relpos_attention(q, k, v, rel_bias):
    B, S, H, d = q.shape
    nc = S // CHUNK
    qc = q.reshape(B, nc, CHUNK, H, d)
    kb, vb = _band(k, CK_LEFT_CHUNKS), _band(v, CK_LEFT_CHUNKS)
    dist, valid = _band_geometry(nc, CK_LEFT_CHUNKS)
    idx = jnp.clip(dist, -(CHUNK - 1), REL_MAX) + (CHUNK - 1)
    bias = jnp.moveaxis(rel_bias[idx], -1, 0).astype(jnp.float32)
    logits = jnp.einsum('bcqhd,bcshd->bchqs', qc, kb, preferred_element_type=jnp.float32) * d ** -0.5 + bias
    logits = jnp.where(valid[None, :, None, None, :], logits, NEG_INF)
    p = jax.nn.softmax(logits, axis=-1).astype(v.dtype)
    return jnp.einsum('bchqs,bcshd->bcqhd', p, vb).reshape(B, S, H, d)

def _mixer_ab(h, w_in, q_norm, w_uq, kv_norm, w_ukv, sinks, w_out, cos, sin):
    B, S, _ = h.shape
    proj = jnp.einsum('bsd,df->bsf', h, w_in)
    c_q, c_kv, k_r, q_s, k_s, v_s = _split_cols(proj, AB_SPLITS)
    q = jnp.einsum('bsr,rf->bsf', _rms_norm(c_q, q_norm), w_uq).reshape(B, S, MLA_HEADS, MLA_NOPE + MLA_ROPE)
    q_nope = q[..., :MLA_NOPE]
    q_rope = _apply_rope(q[..., MLA_NOPE:], cos[None, :, None], sin[None, :, None])
    kv = jnp.einsum('bsr,rf->bsf', _rms_norm(c_kv, kv_norm), w_ukv).reshape(B, S, MLA_HEADS, MLA_NOPE + MLA_V)
    k_rope = _apply_rope(k_r, cos[None], sin[None])
    o_a = _mla_attention(q_nope, q_rope, kv[..., :MLA_NOPE], k_rope, kv[..., MLA_NOPE:])
    o_b = _swa_sink_attention(q_s.reshape(B, S, SWA_HEADS, HEAD_DIM),
                              k_s.reshape(B, S, SWA_KV_HEADS, HEAD_DIM),
                              v_s.reshape(B, S, SWA_KV_HEADS, HEAD_DIM), sinks)
    o = jnp.concatenate([o_a.reshape(B, S, -1), o_b.reshape(B, S, -1)], -1)
    return jnp.einsum('bsf,fd->bsd', o, w_out)

def _mixer_cd(h, w_in, b_forget, rel_bias, w_out):
    B, S, _ = h.shape
    proj = jnp.einsum('bsd,df->bsf', h, w_in)
    q_f, k_f, v_f, f_logit, q_c, k_c, v_c = _split_cols(proj, CD_SPLITS)
    o_c = _forgetting_attention(q_f.reshape(B, S, FOX_HEADS, HEAD_DIM), k_f.reshape(B, S, FOX_HEADS, HEAD_DIM),
                                v_f.reshape(B, S, FOX_HEADS, HEAD_DIM), f_logit, b_forget)
    o_d = _chunk_relpos_attention(q_c.reshape(B, S, CK_HEADS, HEAD_DIM), k_c.reshape(B, S, CK_HEADS, HEAD_DIM),
                                  v_c.reshape(B, S, CK_HEADS, HEAD_DIM), rel_bias)
    o = jnp.concatenate([o_c.reshape(B, S, -1), o_d.reshape(B, S, -1)], -1)
    return jnp.einsum('bsf,fd->bsd', o, w_out)

def _swiglu(x, w_gate, w_up, w_down):
    g = jnp.einsum('bsd,df->bsf', x, w_gate)
    u = jnp.einsum('bsd,df->bsf', x, w_up)
    return jnp.einsum('bsf,fd->bsd', jax.nn.silu(g) * u, w_down)

def first_inputs(seed: int = 0) -> dict:
    key = jax.random.key(seed)
    ks = jax.random.split(key, 20)
    ne, no = (DEPTH + 1) // 2, DEPTH // 2
    f32 = jnp.float32

    def normal(k, shape, scale):
        return jax.random.normal(k, shape, f32) * scale

    def gain(k, shape):
        return 1.0 + normal(k, shape, 0.02)

    return {
        'x': normal(ks[0], (BATCH, SEQ, D_MODEL), 1.0),
        'ab_w_in': normal(ks[1], (ne, D_MODEL, sum(AB_SPLITS)), D_MODEL ** -0.5),
        'ab_q_norm': gain(ks[2], (ne, MLA_Q_RANK)),
        'ab_w_uq': normal(ks[3], (ne, MLA_Q_RANK, MLA_HEADS * (MLA_NOPE + MLA_ROPE)), MLA_Q_RANK ** -0.5),
        'ab_kv_norm': gain(ks[4], (ne, MLA_KV_RANK)),
        'ab_w_ukv': normal(ks[5], (ne, MLA_KV_RANK, MLA_HEADS * (MLA_NOPE + MLA_V)), MLA_KV_RANK ** -0.5),
        'ab_sinks': normal(ks[6], (ne, SWA_HEADS), 0.5),
        'ab_w_out': normal(ks[7], (ne, AB_MIX, D_MODEL), DEEPNORM_BETA * AB_MIX ** -0.5),
        'cd_w_in': normal(ks[8], (no, D_MODEL, sum(CD_SPLITS)), D_MODEL ** -0.5),
        'cd_b_forget': jax.random.uniform(ks[9], (no, FOX_HEADS), dtype=f32, minval=1.0, maxval=5.0),
        'cd_rel_bias': normal(ks[10], (no, REL_TABLE, CK_HEADS), 0.2),
        'cd_w_out': normal(ks[11], (no, CD_MIX, D_MODEL), DEEPNORM_BETA * CD_MIX ** -0.5),
        'ln1_g': gain(ks[12], (DEPTH, D_MODEL)),
        'ln1_b': normal(ks[13], (DEPTH, D_MODEL), 0.02),
        'ffn_w_gate': normal(ks[14], (DEPTH, D_MODEL, D_FF), D_MODEL ** -0.5),
        'ffn_w_up': normal(ks[15], (DEPTH, D_MODEL, D_FF), D_MODEL ** -0.5),
        'ffn_w_down': normal(ks[16], (DEPTH, D_FF, D_MODEL), DEEPNORM_BETA * D_FF ** -0.5),
        'ln2_g': gain(ks[17], (DEPTH, D_MODEL)),
        'ln2_b': normal(ks[18], (DEPTH, D_MODEL), 0.02),
    }

def first_block(x, ab_w_in, ab_q_norm, ab_w_uq, ab_kv_norm, ab_w_ukv, ab_sinks, ab_w_out,
              cd_w_in, cd_b_forget, cd_rel_bias, cd_w_out,
              ln1_g, ln1_b, ffn_w_gate, ffn_w_up, ffn_w_down, ln2_g, ln2_b):
    cos, sin = _rope_tables(x.shape[1])
    for layer in range(DEPTH):
        i = layer // 2
        if layer % 2 == 0:
            mix = _mixer_ab(x, ab_w_in[i], ab_q_norm[i], ab_w_uq[i], ab_kv_norm[i], ab_w_ukv[i],
                            ab_sinks[i], ab_w_out[i], cos, sin)
        else:
            mix = _mixer_cd(x, cd_w_in[i], cd_b_forget[i], cd_rel_bias[i], cd_w_out[i])
        x = _layer_norm(DEEPNORM_ALPHA * x + mix, ln1_g[layer], ln1_b[layer])
        ffn = _swiglu(x, ffn_w_gate[layer], ffn_w_up[layer], ffn_w_down[layer])
        x = _layer_norm(DEEPNORM_ALPHA * x + ffn, ln2_g[layer], ln2_b[layer])
    return x


DEPTH_2 = 1

HEAD_DIM_2 = 128
MOBA_HEADS = 6
MOBA_BLOCK = 256
MOBA_TOPK = 3
MOBA_QCHUNK = 32
GMLP_GROUPS = 6
GMLP_GROUP_DIM = 128
GMLP_CHUNK = 128
XATTN_HEADS = 4
MEM_LEN = 256
ROPE_THETA_2 = 500000.0
ROT_DIM = HEAD_DIM_2 // 4
EPS = 1e-6

A_WIDTH = MOBA_HEADS * HEAD_DIM_2
B_WIDTH = GMLP_GROUPS * GMLP_GROUP_DIM
C_WIDTH = XATTN_HEADS * HEAD_DIM_2
IN_SPLITS = (A_WIDTH, A_WIDTH, A_WIDTH, A_WIDTH, B_WIDTH, B_WIDTH, B_WIDTH, C_WIDTH, C_WIDTH, D_MODEL, D_MODEL, D_MODEL)
IN_WIDTH = 4 * A_WIDTH + 3 * B_WIDTH + 2 * C_WIDTH + 3 * D_MODEL


def rms_norm(x, g):
    xf = x.astype(jnp.float32)
    y = xf * lax.rsqrt(jnp.mean(xf * xf, axis=-1, keepdims=True) + EPS)
    return (y * g.astype(jnp.float32)).astype(x.dtype)

def layer_norm(x, g):
    xf = x.astype(jnp.float32)
    mu = jnp.mean(xf, axis=-1, keepdims=True)
    var = jnp.mean(jnp.square(xf - mu), axis=-1, keepdims=True)
    return ((xf - mu) * lax.rsqrt(var + EPS) * g.astype(jnp.float32)).astype(x.dtype)

def split_cols(t, widths):
    offs, acc = [], 0
    for w in widths[:-1]:
        acc += w
        offs.append(acc)
    return jnp.split(t, offs, axis=-1)

def partial_rope(x, pos):
    half = ROT_DIM // 2
    inv_freq = ROPE_THETA_2 ** (-jnp.arange(0, ROT_DIM, 2, dtype=jnp.float32) / ROT_DIM)
    ang = pos.astype(jnp.float32)[:, None] * inv_freq[None, :]
    cos = jnp.cos(ang)[None, :, None, :].astype(x.dtype)
    sin = jnp.sin(ang)[None, :, None, :].astype(x.dtype)
    x1, x2, rest = x[..., :half], x[..., half:ROT_DIM], x[..., ROT_DIM:]
    return jnp.concatenate([x1 * cos - x2 * sin, x2 * cos + x1 * sin, rest], axis=-1)

def moba_attention(q, k, v):
    B, S, H, dh = q.shape
    n_blocks = -(-S // MOBA_BLOCK)
    k_sel_n = min(MOBA_TOPK, n_blocks)
    pad = n_blocks * MOBA_BLOCK - S
    scale = HEAD_DIM_2 ** -0.5
    qh = jnp.transpose(q, (0, 2, 1, 3))
    kh = jnp.pad(jnp.transpose(k, (0, 2, 1, 3)), ((0, 0), (0, 0), (0, pad), (0, 0)))
    vh = jnp.pad(jnp.transpose(v, (0, 2, 1, 3)), ((0, 0), (0, 0), (0, pad), (0, 0)))
    k_blk = kh.reshape(B, H, n_blocks, MOBA_BLOCK, dh)
    v_blk = vh.reshape(B, H, n_blocks, MOBA_BLOCK, dh)
    k_mean = jnp.mean(k_blk.astype(jnp.float32), axis=3)
    b_ix = jnp.arange(B)[:, None, None, None]
    h_ix = jnp.arange(H)[None, :, None, None]
    blk_ids = jnp.arange(n_blocks)

    def chunk_fn(c):
        start = c * MOBA_QCHUNK
        qc = lax.dynamic_slice_in_dim(qh, start, MOBA_QCHUNK, axis=2)
        pos_q = start + jnp.arange(MOBA_QCHUNK)
        own = start // MOBA_BLOCK
        bs = jnp.einsum('bhqd,bhnd->bhqn', qc.astype(jnp.float32), k_mean)
        bs = jnp.where((blk_ids < own)[None, None, None, :], bs, -jnp.inf)
        _, sel_idx = lax.top_k(bs, k_sel_n)
        sel_valid = sel_idx < own
        k_sel = k_blk[b_ix, h_ix, sel_idx]
        v_sel = v_blk[b_ix, h_ix, sel_idx]
        lg_sel = jnp.einsum('bhqd,bhqkpd->bhqkp', qc, k_sel).astype(jnp.float32) * scale
        lg_sel = jnp.where(sel_valid[..., None], lg_sel, -jnp.inf)
        lg_sel = lg_sel.reshape(B, H, MOBA_QCHUNK, k_sel_n * MOBA_BLOCK)
        k_own = lax.dynamic_index_in_dim(k_blk, own, axis=2, keepdims=False)
        v_own = lax.dynamic_index_in_dim(v_blk, own, axis=2, keepdims=False)
        key_pos = own * MOBA_BLOCK + jnp.arange(MOBA_BLOCK)
        causal = key_pos[None, :] <= pos_q[:, None]
        lg_own = jnp.einsum('bhqd,bhpd->bhqp', qc, k_own).astype(jnp.float32) * scale
        lg_own = jnp.where(causal[None, None], lg_own, -jnp.inf)
        p = jax.nn.softmax(jnp.concatenate([lg_sel, lg_own], axis=-1), axis=-1).astype(v.dtype)
        p_sel = p[..., :k_sel_n * MOBA_BLOCK].reshape(B, H, MOBA_QCHUNK, k_sel_n, MOBA_BLOCK)
        p_own = p[..., k_sel_n * MOBA_BLOCK:]
        return (jnp.einsum('bhqkp,bhqkpd->bhqd', p_sel, v_sel)
                + jnp.einsum('bhqp,bhpd->bhqd', p_own, v_own))

    out = lax.map(chunk_fn, jnp.arange(S // MOBA_QCHUNK))
    return jnp.transpose(out, (1, 0, 3, 2, 4)).reshape(B, S, H * dh)

def gmlp_spatial_gate(u, v, ln_g, w_spatial, b_spatial):
    B, S, _ = v.shape
    vn = layer_norm(v, ln_g).reshape(B, S // GMLP_CHUNK, GMLP_CHUNK, GMLP_GROUPS, GMLP_GROUP_DIM)
    w_causal = jnp.tril(w_spatial)
    mixed = jnp.einsum('gts,bnsgd->bntgd', w_causal, vn) + jnp.transpose(b_spatial)[None, None, :, :, None]
    return u * mixed.reshape(B, S, B_WIDTH)

def memory_cross_attention(q, mem_n, w_mem_kv):
    B, S, _ = q.shape
    M = mem_n.shape[1]
    mk, mv = jnp.split(mem_n @ w_mem_kv, 2, axis=-1)
    qh = q.reshape(B, S, XATTN_HEADS, HEAD_DIM_2)
    kh = mk.reshape(B, M, XATTN_HEADS, HEAD_DIM_2)
    vh = mv.reshape(B, M, XATTN_HEADS, HEAD_DIM_2)
    lg = jnp.einsum('bshd,bmhd->bhsm', qh, kh).astype(jnp.float32) * (HEAD_DIM_2 ** -0.5)
    p = jax.nn.softmax(lg, axis=-1).astype(q.dtype)
    return jnp.einsum('bhsm,bmhd->bshd', p, vh).reshape(B, S, C_WIDTH)

def second_inputs(seed: int = 0) -> dict:
    key = jax.random.key(seed)
    ks = jax.random.split(key, 16)
    f32 = jnp.float32

    def nrm(k, shape, fan_in):
        return jax.random.normal(k, shape, f32) * (fan_in ** -0.5)

    def gain(k, shape):
        return 1.0 + 0.1 * jax.random.normal(k, shape, f32)

    return {
        "x": jax.random.normal(ks[0], (BATCH, SEQ, D_MODEL), f32),
        "mem": jax.random.normal(ks[1], (BATCH, MEM_LEN, D_MODEL), f32),
        "norm_g": gain(ks[2], (DEPTH_2, D_MODEL)),
        "mem_norm_g": gain(ks[3], (DEPTH_2, D_MODEL)),
        "final_norm_g": gain(ks[4], (D_MODEL,)),
        "w_in": nrm(ks[5], (DEPTH_2, D_MODEL, IN_WIDTH), D_MODEL),
        "w_mem_kv": nrm(ks[6], (DEPTH_2, D_MODEL, 2 * C_WIDTH), D_MODEL),
        "gmlp_ln_g": gain(ks[7], (DEPTH_2, B_WIDTH)),
        "w_spatial": nrm(ks[8], (DEPTH_2, GMLP_GROUPS, GMLP_CHUNK, GMLP_CHUNK), GMLP_CHUNK),
        "b_spatial": gain(ks[9], (DEPTH_2, GMLP_GROUPS, GMLP_CHUNK)),
        "w_branch_a": nrm(ks[10], (DEPTH_2, A_WIDTH, D_MODEL), A_WIDTH),
        "w_branch_b": nrm(ks[11], (DEPTH_2, B_WIDTH, D_MODEL), B_WIDTH),
        "w_branch_c": nrm(ks[12], (DEPTH_2, C_WIDTH, D_MODEL), C_WIDTH),
        "w_out": nrm(ks[13], (DEPTH_2, D_MODEL, D_MODEL), D_MODEL),
    }

def second_block(x, mem, norm_g, mem_norm_g, final_norm_g, w_in, w_mem_kv, gmlp_ln_g,
              w_spatial, b_spatial, w_branch_a, w_branch_b, w_branch_c, w_out):
    B, S, _ = x.shape
    pos = jnp.arange(S)
    for layer in range(DEPTH_2):
        h = rms_norm(x, norm_g[layer])
        (qa, ka, va, ga, ub, vb, gb, qc, gc, ma, mb, mc) = split_cols(h @ w_in[layer], IN_SPLITS)
        qa = partial_rope(qa.reshape(B, S, MOBA_HEADS, HEAD_DIM_2), pos)
        ka = partial_rope(ka.reshape(B, S, MOBA_HEADS, HEAD_DIM_2), pos)
        va = va.reshape(B, S, MOBA_HEADS, HEAD_DIM_2)
        out_a = moba_attention(qa, ka, va) * jax.nn.silu(ga)
        out_b = gmlp_spatial_gate(ub, vb, gmlp_ln_g[layer], w_spatial[layer], b_spatial[layer]) * jax.nn.silu(gb)
        mem_n = rms_norm(mem, mem_norm_g[layer])
        out_c = memory_cross_attention(qc, mem_n, w_mem_kv[layer]) * jax.nn.silu(gc)
        y = (jax.nn.sigmoid(ma) * (out_a @ w_branch_a[layer])
             + jax.nn.sigmoid(mb) * (out_b @ w_branch_b[layer])
             + jax.nn.sigmoid(mc) * (out_c @ w_branch_c[layer]))
        x = x + y @ w_out[layer]
    return rms_norm(x, final_norm_g)


def setup_inputs(seed=0):
    out = dict(first_inputs(seed))
    for name, value in second_inputs(seed + 1).items():
        if name != "x":
            out[name + "_2"] = value
    return out


def reference(
    x, ab_w_in, ab_q_norm, ab_w_uq, ab_kv_norm, ab_w_ukv, ab_sinks, ab_w_out, cd_w_in,
    cd_b_forget, cd_rel_bias, cd_w_out, ln1_g, ln1_b, ffn_w_gate, ffn_w_up, ffn_w_down, ln2_g,
    ln2_b, mem_2, norm_g_2, mem_norm_g_2, final_norm_g_2, w_in_2, w_mem_kv_2, gmlp_ln_g_2,
    w_spatial_2, b_spatial_2, w_branch_a_2, w_branch_b_2, w_branch_c_2, w_out_2,
):
    x = first_block(
        x, ab_w_in, ab_q_norm, ab_w_uq, ab_kv_norm, ab_w_ukv, ab_sinks, ab_w_out, cd_w_in,
        cd_b_forget, cd_rel_bias, cd_w_out, ln1_g, ln1_b, ffn_w_gate, ffn_w_up, ffn_w_down,
        ln2_g, ln2_b,
    )
    return second_block(
        x, mem_2, norm_g_2, mem_norm_g_2, final_norm_g_2, w_in_2, w_mem_kv_2, gmlp_ln_g_2,
        w_spatial_2, b_spatial_2, w_branch_a_2, w_branch_b_2, w_branch_c_2, w_out_2,
    )


_drawn_inputs = setup_inputs


def setup_inputs(seed=0):
    import zlib

    import numpy as np

    out = dict(_drawn_inputs(seed))
    spreads = {}
    factors = {'ab_q_norm': 8.0,
     'ab_kv_norm': 8.0,
     'ab_sinks': 8.0,
     'cd_rel_bias': 7.386,
     'mem_norm_g_2': 8.0,
     'gmlp_ln_g_2': 5.837,
     'b_spatial_2': 4.113}
    for name, (base, spread) in spreads.items():
        noise = np.random.default_rng([zlib.crc32(name.encode()), seed]).standard_normal(out[name].shape)
        drawn = base * np.exp(spread * noise) if base else spread * noise
        out[name] = jnp.asarray(drawn.astype(out[name].dtype))
    for name, factor in factors.items():
        out[name] = (out[name] * factor).astype(out[name].dtype)
    return out
```

```python
from collections import namedtuple
from contextlib import ExitStack

import numpy as np
import concourse.bass as bass
from concourse import mybir

F32 = mybir.dt.float32
F32R = mybir.dt.float32r
ACT = mybir.ActivationFunctionType
ALU = mybir.AluOpType

P = 128
TT = 2
S = TT * P
D = 1024
CH = 64
MASKED = -1e30
HALF_D = D // 2

MLA_H, MLA_NOPE, MLA_ROPE, MLA_V = 8, 64, 32, 64
MLA_D = MLA_NOPE + MLA_ROPE
Q_RANK, KV_RANK = 384, 256
SWA_H, SWA_KV, HD = 8, 2, 64
FOX_H = CK_H = 8
AB_W = Q_RANK + KV_RANK + MLA_ROPE + SWA_H * HD + 2 * SWA_KV * HD
CD_W = 3 * FOX_H * HD + FOX_H + 3 * CK_H * HD
FF = 2816
ALPHA = 4 ** 0.25
LN_EPS, RMS_EPS = 1e-5, 1e-6
REL, REL_PITCH = 320, 384
MOBA_H, XA_H, HD2 = 6, 4, 128
AW, BW, CW = MOBA_H * HD2, 6 * 128, XA_H * HD2
ROT2 = 16

NS = 4
SLOT = 1024
LEAD = NS - 1

Gemm = namedtuple("Gemm", "name kc kp n steps c0 u0")


def plan_gemms():
    table = [("ab_in", 8, 2, 480, 3), ("mem_k", 8, 2, 512, 1), ("uq", 3, 3, 256, 3), ("ukv", 2, 2, 512, 2),
             ("mem_v", 8, 2, 512, 1), ("ab_out", 8, 2, 512, 2), ("up0", 8, 2, 512, 11), ("down0", 22, 1, 1024, 1),
             ("cd_in", 8, 2, 440, 7), ("cd_out", 8, 2, 512, 2), ("up1", 8, 2, 512, 11), ("down1", 22, 1, 1024, 1),
             ("in_a", 8, 2, 512, 6), ("in_b", 8, 2, 512, 4), ("in_b_end", 8, 4, 256, 1), ("in_c", 8, 2, 512, 2),
             ("gate_a", 8, 2, 512, 2), ("branch_a", 6, 2, 512, 2), ("gate_b", 8, 2, 512, 2),
             ("branch_b", 6, 2, 512, 2), ("gate_c", 8, 2, 512, 2), ("branch_c", 4, 2, 512, 2),
             ("out", 8, 2, 512, 2)]
    plan, c, u = {}, 0, 0
    for name, kc, kp, n, steps in table:
        plan[name] = Gemm(name, kc, kp, n, steps, c, u)
        c += steps * kc // kp
        u += steps * (2 if n > 512 else 1)
    return plan, c


GEMMS, CHUNKS = plan_gemms()
WIDTH = [g.kp * g.n for g in GEMMS.values() for _ in range(g.steps * g.kc // g.kp)]


def plan_turns():
    table = [("x0", 8), ("mem", 8), ("cq", 3), ("ckv", 2), ("o0", 8), ("f0", 8), ("h0", 22), ("x1", 8), ("o1", 8),
             ("f1", 8), ("h1", 22), ("x2", 8), ("a", 6), ("b", 6), ("c", 4), ("y", 8)]
    plan, at = {}, 0
    for name, kc in table:
        plan[name] = (kc, at)
        at += (kc + 1) // 2
    return plan


TURNS = plan_turns()

STREAMS = {"l0": (0, 16), "l1": (16, 32), "moba": (32, 38), "xa": (38, 42)}
STAGES = 4

MEM_K, MEM_V, TAB = 0, 1024, 2048
PROJ0, Q0, K0, V0, O0 = 5120, 8000, 9536, 11072, 12096
PROJ1, O1, CUM = 5120, 11280, 13328
A2, B2 = 2048, 8192
ARENA = 14144


def view(base, offset, dims):
    return bass.AP(tensor=base.tensor, offset=base.offset + offset, ap=[base.ap[0]] + [list(d) for d in dims])


def plus(value, i, per_turn):
    return value if i is None else value + i * per_turn


def build_program(nc, d, out):
    with ExitStack() as ctx:
        def sb(name, shape, dt=F32):
            return ctx.enter_context(nc.sbuf_tensor(name, shape, dt))

        def sem(name):
            return ctx.enter_context(nc.semaphore(name))

        stage = sb("stage", [P, NS, SLOT])
        w_hi = sb("w_hi", [P, NS, SLOT], F32R)
        w_lo = sb("w_lo", [P, NS, SLOT], F32R)
        xt_hi = sb("xt_hi", [P, 8, S], F32R)
        xt_lo = sb("xt_lo", [P, 8, S], F32R)
        ht_hi = sb("ht_hi", [P, 22, S], F32R)
        ht_lo = sb("ht_lo", [P, 22, S], F32R)
        x = sb("x", [P, TT, D])
        arena = sb("arena", [P, ARENA])
        ident = sb("ident", [P, P])
        masks = sb("masks", [P, 2, 384])
        no_mask = sb("no_mask", [P, 256])
        qk_t = sb("qk_t", [P, 2, 512])
        probs = sb("probs", [P, 2, 512])
        probs_t = sb("probs_t", [P, 2, 512])
        ln_par = sb("ln_par", [P, 2, D])
        row_g = sb("row_g", [P, D])
        rope = sb("rope", [P, 4, TT, 16])
        head_par = sb("head_par", [P, 2, 8])
        wsp = sb("wsp", [P, 6, P])
        bsp = sb("bsp", [P, 6])
        cum_k = sb("cum_k", [P, S])
        log_f = sb("log_f", [P, 4, TT, 8])
        eps = sb("eps", [P, 2])
        rms_st = sb("rms_st", [P, 5, 3, 2])
        ln_st = sb("ln_st", [P, 5, 32])
        soft = sb("soft", [P, 4, 5, 2])
        psum = ctx.enter_context(nc.psum_tensor("psum", [P, 8, 512], F32))
        TURN_BANKS = (4, 5)
        QK_BANK, LOGIT_BANK, PT_BANK, O_BANK = 4, 5, 6, 7

        staged = [sem(f"staged{s}") for s in range(NS)]
        hi_done, lo_done = sem("hi_done"), sem("lo_done")
        chunk_used = sem("chunk_used")
        acc_free = [sem("acc_free0"), sem("acc_free1")]
        turned, turn_hi, turn_lo = sem("turned"), sem("turn_hi"), sem("turn_lo")
        qk_turned, qk_copied = sem("qk_turned"), sem("qk_copied")
        logits_ready, max_ready, exp_ready = sem("logits_ready"), sem("max_ready"), sem("exp_ready")
        p_turned, p_copied = sem("p_turned"), sem("p_copied")
        pv_ready, head_done = sem("pv_ready"), sem("head_done")
        silu_ready = sem("silu_ready")
        ln_var, ln_sd, x_ready = sem("ln_var"), sem("ln_sd"), sem("x_ready")
        rms_sd, rms_done = sem("rms_sd"), sem("rms_done")
        act_step, dve_step, pool_step = sem("act_step"), sem("dve_step"), sem("pool_step")
        constants_set = sem("constants_set")
        mla_ready, moba_ready = sem("mla_ready"), sem("moba_ready")
        f_abs, f_ln, log_f_ready, cum_ready, cum_copied = (sem("f_abs"), sem("f_ln"), sem("log_f_ready"),
                                                           sem("cum_ready"), sem("cum_copied"))
        rel_ready, wsp_ready = sem("rel_ready"), sem("wsp_ready")
        vn_ready, mixed, gated_b = sem("vn_ready"), sem("mixed"), sem("gated_b")
        y_ready, stored = sem("y_ready"), sem("stored")
        loads = ["x", "ident", "mem_g", "mem", "gains", "rope", "swa", "masks", "heads", "ln0", "ln1", "ln2", "ln3",
                 "rel", "cum", "sel", "norm_g", "gmlp_g", "final_g", "wsp", "bsp"]
        loaded = {n: sem(f"loaded_{n}") for n in loads}

        def cols(at, width, dims=None):
            return arena[:, at:at + width]

        def region(at, width):
            return arena[:, at:at + TT * width].rearrange("p (t n) -> p t n", t=TT)

        mem_x, o0 = region(O0, D), region(O0, D)
        mem_k, mem_v = region(MEM_K, CW), region(MEM_V, CW)
        proj0, q0, proj1, o1 = region(PROJ0, AB_W), region(Q0, MLA_H * MLA_D), region(PROJ1, CD_W), region(O1, D)
        k0 = arena[:, K0:K0 + TT * MLA_H * MLA_D].rearrange("p (t h n) -> p t h n", t=TT, h=MLA_H)
        v0 = arena[:, V0:V0 + TT * MLA_H * MLA_V].rearrange("p (t h n) -> p t h n", t=TT, h=MLA_H)
        gains = cols(V0, Q_RANK + KV_RANK)
        table = arena[:, TAB:TAB + 8 * 384].rearrange("p (h n) -> p h n", h=8)
        rel_raw = arena[:, PROJ0:PROJ0 + 8 * 384].rearrange("p (h n) -> p h n", h=8)
        cum_tri = region(CUM, S)
        a2 = region(A2, 4 * AW)
        b2 = region(B2, 3 * BW)
        c2 = region(A2 + 6144 - 2 * 2 * CW, 2 * CW)
        a2_out = lambda t: a2[:, t, 0:D]
        y2 = region(A2 + 2 * D, D)
        sig = ln_par
        u_tile = qk_t[:, :, :].rearrange("p b (t n) -> p b t n", t=TT)
        h_tile = probs[:, :, :].rearrange("p b (t n) -> p b t n", t=TT)

        SWA_Q = Q_RANK + KV_RANK + MLA_ROPE
        SWA_K = SWA_Q + SWA_H * HD
        SWA_V = SWA_K + SWA_KV * HD
        CK_Q = 3 * FOX_H * HD + FOX_H

        Head = namedtuple("Head", "dim scale q k v mask full out gate sink fox")

        def head_of(h):
            cut = lambda m, at, w: (lambda t: m[:, t, at:at + w])
            if h < 8:
                return Head(HD, HD ** -0.5, cut(proj0, SWA_Q + h * HD, HD), cut(proj0, SWA_K + h // 4 * HD, HD),
                            cut(proj0, SWA_V + h // 4 * HD, HD), table[:, h, :], False,
                            cut(o0, MLA_H * MLA_V + h * HD, HD), None, h, None)
            if h < 16:
                h -= 8
                return Head(MLA_D, MLA_D ** -0.5, cut(q0, h * MLA_D, MLA_D), lambda t: k0[:, t, h, :],
                            lambda t: v0[:, t, h, :], masks[:, 0, :], False, cut(o0, h * MLA_V, MLA_V),
                            None, None, None)
            if h < 24:
                h -= 16
                return Head(HD, HD ** -0.5, cut(proj1, h * HD, HD), cut(proj1, (FOX_H + h) * HD, HD),
                            cut(proj1, (2 * FOX_H + h) * HD, HD), masks[:, 1, :], False, cut(o1, h * HD, HD),
                            None, None, h)
            if h < 32:
                h -= 24
                return Head(HD, HD ** -0.5, cut(proj1, CK_Q + h * HD, HD), cut(proj1, CK_Q + (CK_H + h) * HD, HD),
                            cut(proj1, CK_Q + (2 * CK_H + h) * HD, HD), table[:, h, :], False,
                            cut(o1, (FOX_H + h) * HD, HD), None, None, None)
            if h < 38:
                h -= 32
                return Head(HD2, HD2 ** -0.5, cut(a2, h * HD2, HD2), cut(a2, AW + h * HD2, HD2),
                            cut(a2, 2 * AW + h * HD2, HD2), masks[:, 1, :], False, cut(a2, h * HD2, HD2),
                            cut(a2, 3 * AW + h * HD2, HD2), None, None)
            h -= 38
            return Head(HD2, HD2 ** -0.5, cut(c2, h * HD2, HD2), cut(mem_k, h * HD2, HD2), cut(mem_v, h * HD2, HD2),
                        None, True, cut(c2, h * HD2, HD2), cut(c2, CW + h * HD2, HD2), None, None)

        def keys0(hd):
            return S if hd.full else P

        def read(name, steps):
            u = GEMMS[name].u0 + steps - 1
            return acc_free[u % 2], TT * (u // 2 + 1)

        block = ctx.enter_context(nc.Block())

        @block.sync
        def _(sp):
            sp.dma_start(ident[:, :], d["ident"]).then_inc(loaded["ident"], 16)
            sp.dma_start(x[:, :, :], d["x"].rearrange("(t p) n -> p t n", t=TT)).then_inc(loaded["x"], 16)

            def load_chunk(g, n, i=None):
                c = g.c0 + n
                s, w = c % NS, WIDTH[c]
                if c >= NS or i is not None:
                    sp.wait_ge(lo_done, plus(c - NS + 1, i, NS))
                src = d["w_" + g.name]
                src = src[n] if i is None else src[bass.ds(i * NS + n, 1), :, :].rearrange("a p n -> (a p) n")
                sp.dma_start(stage[:, s, 0:w], src).then_inc(staged[s], 16)

            for g in GEMMS.values():
                chunks = g.steps * g.kc // g.kp
                n = 0
                while g.c0 + n < NS and n < chunks:
                    load_chunk(g, n)
                    n += 1
                turns = (chunks - n) // NS
                if turns >= 2:
                    with sp.Fori(0, turns) as i:
                        for m in range(NS):
                            load_chunk(g, n + m, i)
                    n += turns * NS
                for m in range(n, chunks):
                    load_chunk(g, m)
            for t in range(TT):
                sp.wait_ge(rms_done, 10)
                sp.dma_start(out[t * P:(t + 1) * P, :], a2_out(t)).then_inc(stored, 16)
            sp.wait_ge(stored, 16 * TT)

        @block.gpsimd
        def _(pool):
            def load(name, dst, src):
                pool.dma_start(dst, src).then_inc(loaded[name], 16)

            def row(src, n):
                return bass.AP(tensor=src.tensor, offset=src.offset, ap=[[0, P], [1, n]])

            load("mem_g", row_g[:, :], row(d["mem_norm_g"], D))
            load("mem", mem_x, d["mem"].rearrange("(t p) n -> p t n", t=TT))
            load("gains", gains, row(d["gains"], Q_RANK + KV_RANK))
            load("rope", rope[:, :, :, :], d["rope"])
            load("swa", table, d["swa"])
            load("masks", masks[:, :, :], d["masks"])
            load("heads", head_par[:, :, :].rearrange("p a h -> p (a h)"), row(d["head_par"], 16))
            load("ln0", ln_par[:, :, :].rearrange("p a n -> p (a n)"),
                 bass.AP(tensor=d["ln"].tensor, offset=0, ap=[[0, P], [1, 2 * D]]))
            load("bsp", bsp[:, :], d["bsp"])
            load("wsp", wsp[:, :, :], d["wsp"])
            pool.wait_ge(loaded["masks"], 16)
            pool.memset(no_mask[:, :], 0.0).then_inc(constants_set, 1)
            pool.wait_ge(loaded["wsp"], 16)
            pool.affine_select(out=wsp[:, :, :], in_=wsp[:, :, :], compare_op=ALU.is_ge, fill=0.0, base=0,
                               pattern=[[0, 6], [1, P]], channel_multiplier=-1).then_inc(wsp_ready, 1)
            pool.wait_ge(rms_done, 2)
            load("sel", row_g[0:8, :], d["sel"])
            pool.wait_ge(head_done, STREAMS["l0"][1])
            rel = d["rel"]
            for at, keys in ((0, P), (P, S)):
                load("rel", rel_raw[:, :, at:at + keys],
                     bass.AP(tensor=rel.tensor, offset=0, ap=[[1, P], [REL_PITCH, CK_H], [1, keys]]))
            pool.wait_ge(loaded["rel"], 32)
            for at, keys in ((0, P), (P, S)):
                last = pool.tensor_scalar(table[:, :, at:at + keys],
                                          view(rel_raw[:, 0, 0:1], at + keys - 1, [[384, CK_H], [-1, keys]]),
                                          HD ** 0.5, None, ALU.mult)
            last.then_inc(pool_step, 1)
            pool.wait_ge(pool_step, 1)
            pool.memset(table[0:CH, :, CH:P], MASKED).then_inc(rel_ready, 1)
            pool.memset(table[0:CH, :, P + S - CH:P + S], MASKED).then_inc(rel_ready, 1)
            for k in range(1, 4):
                pool.wait_ge(x_ready, TT * k)
                if k == 1:
                    load("cum", cum_tri, d["cum"])
                load(f"ln{k}", ln_par[:, :, :].rearrange("p a n -> p (a n)"),
                     bass.AP(tensor=d["ln"].tensor, offset=2 * D * k, ap=[[0, P], [1, 2 * D]]))
                if k == 3:
                    pool.wait_ge(logits_ready, STREAMS["l1"][1])
                    load("norm_g", row_g[:, :], row(d["norm_g"], D))
            pool.wait_ge(rms_done, 8)
            load("gmlp_g", row_g[:, 0:BW], row(d["gmlp_g"], BW))
            pool.wait_ge(vn_ready, 1)
            load("final_g", row_g[:, :], row(d["final_g"], D))

        @block.tensor
        def _(pe):
            def turn(name, src, ready, part=None, i=None, i0=0):
                kc, g0 = TURNS[name]
                groups = range((kc + 1) // 2) if part is None else [part]
                for n in groups:
                    g = g0 + n
                    for s, v in ready(n) if callable(ready) else ready:
                        pe.wait_ge(s, v)
                    if g >= 2 or i is not None:
                        pe.wait_ge(turn_lo, plus(g - 1, i, 2))
                    ks = range(min(2, kc - 2 * n))
                    for k in ks:
                        for t in range(TT):
                            last = pe.transpose(psum[:, TURN_BANKS[g % 2], (k * TT + t) * P:(k * TT + t + 1) * P],
                                                src(2 * n + k, t), ident[:, :])
                    last.then_inc(turned, 1)

            def step(g, j, hi, lo, k0=0, turned_by=None, between=None, i=None, turn_steps=0):
                u, cps = g.u0 + j, g.kc // g.kp
                pair = u % 2
                if u >= 2 or i is not None:
                    pe.wait_ge(acc_free[pair], plus(2 * (u // 2), i, turn_steps))
                for m in range(cps):
                    n = j * cps + m
                    c = g.c0 + n
                    s = c % NS
                    pe.wait_ge(lo_done, plus(c + 1, i, turn_steps * cps))
                    for kk in range(g.kp):
                        k = m * g.kp + kk
                        if turned_by is not None and j == 0 and i is None and k % 2 == 0:
                            pe.wait_ge(turn_lo, TURNS[turned_by][1] + k // 2 + 1)
                        wh, wl = w_hi[:, s, kk * g.n:(kk + 1) * g.n], w_lo[:, s, kk * g.n:(kk + 1) * g.n]
                        for t in range(TT):
                            acc = psum[:, 2 * pair + t, 0:g.n]
                            ah, al = hi[:, k0 + k, t * P:(t + 1) * P], lo[:, k0 + k, t * P:(t + 1) * P]
                            pe.matmul(acc, ah, wh, start=(k == 0), stop=False)
                            pe.matmul(acc, ah, wl, start=False, stop=False)
                            last = pe.matmul(acc, al, wh, start=False, stop=(k == g.kc - 1))
                    last.then_inc(chunk_used, 1)
                    if between and n in between:
                        between[n]()

            def gemm(name, hi, lo, k0=0, turned_by=None, between=None):
                g = GEMMS[name]
                for j in range(g.steps):
                    step(g, j, hi, lo, k0, turned_by, between)

            def up(layer):
                g, name = GEMMS[f"up{layer}"], f"h{layer}"

                def turn_step(j, i=None):
                    u = g.u0 + j
                    ready = [(acc_free[u % 2], plus(2 * (u // 2 + 1), i, 2))]
                    turn(name, lambda k, t: h_tile[:, j % 2, t, (k % 2) * P:(k % 2 + 1) * P], ready, part=j, i=i)

                cps = g.kc // g.kp

                def one(j, i=None):
                    between = {j * cps + 1: lambda: turn_step(j - 1, i)} if j else None
                    step(g, j, xt_hi, xt_lo, 0, f"f{layer}", between, i, 2)

                one(0)
                with pe.Fori(0, 4) as i:
                    for s in range(2):
                        one(1 + s, i)
                one(9)
                one(10)
                return lambda: turn_step(10)

            def down(layer, turn_last):
                g = GEMMS[f"down{layer}"]
                for pair in range(2):
                    u = g.u0 + (pair - g.u0) % 2
                    pe.wait_ge(acc_free[pair], 2 * (u // 2))
                for k in range(g.kc):
                    c = g.c0 + k
                    s = c % NS
                    pe.wait_ge(lo_done, c + 1)
                    pe.wait_ge(turn_lo, TURNS[f"h{layer}"][1] + k // 2 + 1)
                    for t in range(TT):
                        ah, al = ht_hi[:, k, t * P:(t + 1) * P], ht_lo[:, k, t * P:(t + 1) * P]
                        for a, w in ((ah, w_hi), (ah, w_lo), (al, w_hi)):
                            for half in range(2):
                                last = pe.matmul(psum[:, 2 * ((g.u0 + half) % 2) + t, :], a,
                                                 w[:, s, half * 512:(half + 1) * 512],
                                                 start=(k == 0 and w is w_hi and a is ah),
                                                 stop=(k == g.kc - 1 and a is al))
                    last.then_inc(chunk_used, 1)
                    if k == 1:
                        turn_last()

            def slot(stream, s):
                lo_h, hi_h = STREAMS[stream]
                h = lo_h + s - 3
                if lo_h <= h < hi_h:
                    hd = head_of(h)
                    pe.wait_ge(p_copied, h + 1)
                    if h >= 1:
                        pe.wait_ge(head_done, h)
                    dv = hd.v(0).shape[-1]
                    for t in range(TT):
                        kts = range(TT) if hd.full or t else range(1)
                        for kt in kts:
                            n = (kt * TT + t) if hd.full else (t + kt)
                            last = pe.matmul(psum[:, O_BANK, t * dv:(t + 1) * dv],
                                             probs_t[:, h % 2, n * P:(n + 1) * P], hd.v(kt),
                                             start=(kt == 0), stop=(kt == kts[-1]))
                    last.then_inc(pv_ready, 1)
                h = lo_h + s - 2
                if lo_h <= h < hi_h:
                    hd = head_of(h)
                    pe.wait_ge(exp_ready, h + 1)
                    if h >= 1:
                        pe.wait_ge(p_copied, h)
                    n0 = keys0(hd)
                    pairs = ([(0, 0), (0, 1), (1, 0), (1, 1)] if hd.full else [(0, 0), (0, 1), (1, 1)])
                    for n, (kt, t) in enumerate(pairs):
                        at = t * n0 + kt * P
                        last = pe.transpose(psum[:, PT_BANK, n * P:(n + 1) * P], probs[:, h % 2, at:at + P],
                                            ident[:, :])
                    last.then_inc(p_turned, 1)
                h = lo_h + s - 1
                if lo_h <= h < hi_h:
                    hd = head_of(h)
                    pe.wait_ge(qk_copied, h + 1)
                    if h >= 1:
                        pe.wait_ge(max_ready, h)
                    n0 = keys0(hd)
                    for t in range(TT):
                        nk = S if t else n0
                        acc = psum[:, LOGIT_BANK, t * n0:t * n0 + nk]
                        last = pe.matmul(acc, qk_t[0:hd.dim, h % 2, t * P:(t + 1) * P],
                                         qk_t[0:hd.dim, h % 2, S:S + nk], start=True, stop=hd.fox is None)
                        if hd.fox is not None:
                            if h == STREAMS["l1"][0] and t == 0:
                                pe.wait_ge(cum_copied, 1)
                                pe.wait_ge(loaded["sel"], 16)
                            last = pe.matmul(acc, row_g[0:8, hd.fox * P:(hd.fox + 1) * P], cum_k[0:8, 0:nk],
                                             start=False, stop=True)
                    last.then_inc(logits_ready, 1)
                h = lo_h + s
                if lo_h <= h < hi_h:
                    hd = head_of(h)
                    if h == 8:
                        pe.wait_ge(mla_ready, 1)
                        pe.wait_ge(*read("ukv", 2))
                    if h == 24:
                        pe.wait_ge(*read("cd_in", 7))
                        pe.wait_ge(rel_ready, 2)
                    if h >= 1:
                        pe.wait_ge(qk_copied, h)
                    for n, src in enumerate((hd.q(0), hd.q(1), hd.k(0), hd.k(1))):
                        last = pe.transpose(psum[0:hd.dim, QK_BANK, n * P:(n + 1) * P], src, ident[:, :])
                    last.then_inc(qk_turned, 1)

            def slots(stream, *numbers):
                return lambda: [slot(stream, s) for s in numbers]

            tile_of = lambda m, at=0: (lambda k, t: m[:, t, at + k * P:at + (k + 1) * P])

            pe.wait_ge(loaded["ident"], 16)
            turn("x0", tile_of(x), [(loaded["x"], 16)])
            gemm("ab_in", xt_hi, xt_lo, turned_by="x0")
            turn("mem", tile_of(mem_x), [(rms_done, 2)])
            gemm("mem_k", ht_hi, ht_lo, turned_by="mem")
            turn("cq", tile_of(proj0), [(rms_done, 4)])
            turn("ckv", tile_of(proj0, Q_RANK), [(rms_done, 6)])
            pe.wait_ge(turn_lo, TURNS["o0"][1])
            slot("l0", 0)
            gemm("uq", ht_hi, ht_lo, 8, "cq", {0: slots("l0", 1), 1: slots("l0", 2), 2: slots("l0", 3)})
            gemm("ukv", ht_hi, ht_lo, 11, "ckv", {0: slots("l0", 4), 1: slots("l0", 5)})
            slots("l0", 6, 7)()
            gemm("mem_v", ht_hi, ht_lo, 0, None, {0: slots("l0", 8), 1: slots("l0", 9, 10),
                                                  2: slots("l0", 11, 12), 3: slots("l0", 13, 14)})
            slots("l0", 15, 16, 17, 18)()
            turn("o0", tile_of(o0), [(head_done, 16)])
            gemm("ab_out", xt_hi, xt_lo, turned_by="o0")
            turn("f0", tile_of(x), [(x_ready, 2)])
            down(0, up(0))
            turn("x1", tile_of(x), [(x_ready, 4)])
            pe.wait_ge(turn_lo, TURNS["o1"][1])

            def cumulate():
                pe.wait_ge(log_f_ready, 1)
                pe.wait_ge(loaded["cum"], 16)
                for t in range(TT):
                    last = pe.matmul(psum[0:FOX_H, O_BANK, 0:S], log_f[:, 3, t, :], cum_tri[:, t, :],
                                     start=(t == 0), stop=(t == TT - 1))
                last.then_inc(cum_ready, 1)

            def first_slot():
                pe.wait_ge(*read("cd_in", 4))
                slot("l1", 0)

            gemm("cd_in", xt_hi, xt_lo, 0, "x1",
                 {18: cumulate, 19: first_slot, **{19 + s: slots("l1", s) for s in range(1, 8)}})
            slots("l1", *range(8, 19))()
            turn("o1", tile_of(o1), [(head_done, 32)])
            gemm("cd_out", xt_hi, xt_lo, turned_by="o1")
            turn("f1", tile_of(x), [(x_ready, 6)])
            down(1, up(1))
            turn("x2", tile_of(arena[:, B2:B2 + TT * D].rearrange("p (t n) -> p t n", t=TT)), [(rms_done, 8)])
            gemm("in_a", xt_hi, xt_lo, turned_by="x2")

            def moba_first():
                pe.wait_ge(turn_lo, TURNS["a"][1])
                pe.wait_ge(moba_ready, 1)
                pe.wait_ge(*read("in_a", 6))
                slot("moba", 0)

            gemm("in_b", xt_hi, xt_lo, 0, None, {2: moba_first, **{2 + s: slots("moba", s) for s in range(1, 9)}})
            gemm("in_b_end", xt_hi, xt_lo)

            def mix(groups):
                for g in groups:
                    if g == 0:
                        pe.wait_ge(vn_ready, 1)
                        pe.wait_ge(wsp_ready, 1)
                    if g >= 2:
                        pe.wait_ge(gated_b, g - 1)
                    pe.matmul(psum[:, PT_BANK + g % 2, 0:S].rearrange("p (t n) -> p t n", t=TT), wsp[:, g, :],
                              b2[:, :, BW + g * P:BW + (g + 1) * P], start=True, stop=True).then_inc(mixed, 1)

            gemm("in_c", xt_hi, xt_lo, 0, None,
                 {1: lambda: turn("a", tile_of(a2), [(head_done, 38)]), 2: lambda: mix(range(3)),
                  3: lambda: mix(range(3, 6))})

            def xa_first():
                pe.wait_ge(*read("in_c", 2))
                pe.wait_ge(turn_lo, TURNS["b"][1])
                pe.wait_ge(gated_b, 6)
                slot("xa", 0)

            gemm("gate_a", xt_hi, xt_lo, 0, None, {0: xa_first, **{s: slots("xa", s) for s in range(1, 7)}})
            turn("b", tile_of(b2), [(gated_b, 6), (head_done, 42)])
            turn("c", tile_of(c2), [(head_done, 42)])
            gemm("branch_a", ht_hi, ht_lo, 0, "a")
            gemm("gate_b", xt_hi, xt_lo)
            gemm("branch_b", ht_hi, ht_lo, 6, "b")
            gemm("gate_c", xt_hi, xt_lo)
            gemm("branch_c", ht_hi, ht_lo, 12, "c")
            turn("y", tile_of(y2), lambda n: [(y_ready, 6 if n < 2 else 8)])
            gemm("out", xt_hi, xt_lo, turned_by="y")

        @block.scalar
        def _(act):
            done = {"chunks": 0, "steps": 0}

            def settle(ins):
                done["steps"] += 1
                ins.then_inc(act_step, 1)
                act.wait_ge(act_step, done["steps"])

            def split_hi(c, i=None, per_turn=0):
                s, w = c % NS, WIDTH[c]
                act.wait_ge(staged[s], plus(16 * (c // NS + 1), i, 16 * per_turn // NS))
                if c >= NS or i is not None:
                    act.wait_ge(chunk_used, plus(c - NS + 1, i, per_turn))
                act.copy(w_hi[:, s, 0:w], stage[:, s, 0:w]).then_inc(hi_done, 1)

            def split_to(c):
                while done["chunks"] < min(c, CHUNKS):
                    split_hi(done["chunks"])
                    done["chunks"] += 1

            def gemm(name, evacuate=None, between=None, after=()):
                g = GEMMS[name]
                cps = g.kc // g.kp
                for j in range(g.steps):
                    for n in range(j * cps, (j + 1) * cps):
                        split_to(g.c0 + n + 1 + LEAD)
                        if between and n in between:
                            between[n]()
                    if evacuate is not None:
                        for s, v in after if j == 0 else ():
                            act.wait_ge(s, v)
                        pair = (g.u0 + j) % 2
                        act.wait_ge(chunk_used, g.c0 + (j + 1) * cps)
                        for t in range(TT):
                            evacuate(j, t, psum[:, 2 * pair + t, :]).then_inc(acc_free[pair], 1)

            def turn(name, dst, part=None, i=None):
                kc, g0 = TURNS[name]
                for n in (range((kc + 1) // 2) if part is None else [part]):
                    g = g0 + n
                    act.wait_ge(turned, plus(g + 1, i, 2))
                    w = min(2, kc - 2 * n)
                    act.copy(dst(2 * n, w), psum[:, TURN_BANKS[g % 2], 0:w * S].rearrange("p (k n) -> p k n", k=w)
                             ).then_inc(turn_hi, 1)

            into = lambda m, k0=0: (lambda k, w: m[:, k0 + k:k0 + k + w, :])

            def slot(stream, s):
                lo_h, hi_h = STREAMS[stream]
                h = lo_h + s - 2
                if lo_h <= h < hi_h:
                    hd = head_of(h)
                    w = 4 * P if hd.full else 3 * P
                    act.wait_ge(p_turned, h + 1)
                    if h >= 2:
                        act.wait_ge(pv_ready, h - 1)
                    act.copy(probs_t[:, h % 2, 0:w], psum[:, PT_BANK, 0:w]).then_inc(p_copied, 1)
                h = lo_h + s - 1
                if lo_h <= h < hi_h:
                    hd = head_of(h)
                    n0, b = keys0(hd), h % 4
                    act.wait_ge(max_ready, h + 1)
                    if hd.sink is not None:
                        act.activation(soft[:, b, 3, :], soft[:, b, 1, :], ACT.Exp,
                                       bias=head_par[:, 0, hd.sink:hd.sink + 1])
                    for t in range(TT):
                        p = probs[:, h % 2, t * n0:t * n0 + (S if t else n0)]
                        last = act.activation(p, p, ACT.Exp, bias=soft[:, b, 1, t:t + 1],
                                              accum_out=soft[:, b, 2, t:t + 1])
                    last.then_inc(exp_ready, 1)

            def slots(stream, *numbers):
                return lambda: [slot(stream, s) for s in numbers]

            def rms(k, src, junk, n, ready):
                for s, v in ready:
                    act.wait_ge(s, v)
                for t in range(TT):
                    settle(act.activation(junk, src(t), ACT.Square, accum_out=rms_st[:, k, 0, t:t + 1]))
                act.activation(rms_st[:, k, 1, :], rms_st[:, k, 0, :], ACT.Sqrt, scale=1.0 / n,
                               bias=eps[:, 1:2]).then_inc(rms_sd, 1)

            def ln_root(k, which_eps=0):
                act.wait_ge(ln_var, TT * (k + 1))
                act.activation(ln_st[:, k, 28:30], view(ln_st[:, k, 24:25], 1, [[2, 2]]), ACT.Sqrt,
                               bias=eps[:, which_eps:which_eps + 1]).then_inc(ln_sd, 1)

            def copy_to(dst):
                return lambda j, t, acc: act.copy(*dst(j, t, acc))

            def copy_through(func, dst):
                return lambda j, t, acc: act.activation(dst(j, t), acc, func)

            def up(layer):
                g, name = GEMMS[f"up{layer}"], f"h{layer}"
                cps = g.kc // g.kp
                act.preload_act_table(ACT.Silu)

                def one(j, i=None):
                    for m in range(cps):
                        if i is None:
                            split_to(g.c0 + j * cps + m + 1 + LEAD)
                        else:
                            split_hi(g.c0 + j * cps + m + LEAD, i, 2 * cps)
                        if m == 1 and j:
                            k = 2 * (j - 1)
                            dst = ht_hi[:, k:k + 2, :] if i is None else ht_hi[:, bass.ds(i * 4 + k, 2), :]
                            turn(name, lambda a, b: dst, part=j - 1, i=i)
                    pair = (g.u0 + j) % 2
                    act.wait_ge(chunk_used, plus(g.c0 + (j + 1) * cps, i, 2 * cps))
                    for t in range(TT):
                        act.activation(u_tile[:, j % 2, t, :], psum[:, 2 * pair + t, 0:256], ACT.Silu
                                       ).then_inc(silu_ready, 1)

                one(0)
                assert done["chunks"] == g.c0 + cps + LEAD
                with act.Fori(0, 4) as i:
                    for s in range(2):
                        one(1 + s, i)
                done["chunks"] += 8 * cps
                one(9)
                one(10)

            def down(layer):
                g = GEMMS[f"down{layer}"]
                for k in range(g.kc):
                    split_to(g.c0 + k + 1 + LEAD)
                    if k == 1:
                        turn(f"h{layer}", into(ht_hi), part=10)

            split_to(LEAD)
            turn("x0", into(xt_hi))

            def memory_norm():
                act.wait_ge(constants_set, 3)
                rms(0, lambda t: mem_x[:, t, :], arena[:, Q0:Q0 + D], D, [(loaded["mem"], 16)])

            gemm("ab_in", copy_to(lambda j, t, acc: (proj0[:, t, j * 480:(j + 1) * 480], acc[:, 0:480])),
                 {4: memory_norm})
            turn("mem", into(ht_hi))
            rms(1, lambda t: proj0[:, t, 0:Q_RANK], arena[:, K0:K0 + Q_RANK], Q_RANK, [read("ab_in", 3)])
            rms(2, lambda t: proj0[:, t, Q_RANK:Q_RANK + KV_RANK], arena[:, K0:K0 + KV_RANK], KV_RANK, [])
            gemm("mem_k", copy_to(lambda j, t, acc: (mem_k[:, t, :], acc)))
            turn("cq", into(ht_hi, 8))
            turn("ckv", into(ht_hi, 11))
            act.wait_ge(loaded["heads"], 16)
            slot("l0", 0)
            gemm("uq", copy_to(lambda j, t, acc: (q0[:, t, j * 256:(j + 1) * 256], acc[:, 0:256])),
                 {0: slots("l0", 1), 1: slots("l0", 2), 2: slots("l0", 3)})

            def split_kv(j, t, acc):
                kv = acc.rearrange("p (h n) -> p h n", h=4)
                settle(act.copy(k0[:, t, 4 * j:4 * j + 4, 0:MLA_NOPE], kv[:, :, 0:MLA_NOPE]))
                return act.copy(v0[:, t, 4 * j:4 * j + 4, :], kv[:, :, MLA_NOPE:])

            gemm("ukv", split_kv, {0: slots("l0", 4), 1: slots("l0", 5)})
            slots("l0", 6, 7)()
            gemm("mem_v", copy_to(lambda j, t, acc: (mem_v[:, t, :], acc)),
                 {0: slots("l0", 8), 1: slots("l0", 9, 10), 2: slots("l0", 11, 12), 3: slots("l0", 13, 14)})
            slots("l0", 15, 16, 17, 18)()
            turn("o0", into(xt_hi))
            gemm("ab_out")
            ln_root(0)
            turn("f0", into(xt_hi))
            up(0)
            down(0)
            ln_root(1)
            turn("x1", into(xt_hi))

            def log_sigmoid():
                act.wait_ge(f_abs, 1)
                settle(act.activation(log_f[:, 2, :, :], log_f[:, 1, :, :], ACT.Exp, scale=-1.0))
                act.activation(log_f[:, 1, :, :], log_f[:, 2, :, :], ACT.Ln, bias=1.0).then_inc(f_ln, 1)

            gemm("cd_in", copy_to(lambda j, t, acc: (proj1[:, t, j * 440:(j + 1) * 440], acc[:, 0:440])),
                 {17: log_sigmoid, **{19 + s: slots("l1", s) for s in range(8)}})
            slots("l1", *range(8, 19))()
            turn("o1", into(xt_hi))
            gemm("cd_out")
            ln_root(2)
            turn("f1", into(xt_hi))
            up(1)
            down(1)
            ln_root(3)
            rms(3, lambda t: x[:, t, :], arena[:, B2 + TT * D:B2 + TT * D + D], D, [(x_ready, 8)])
            turn("x2", into(xt_hi))

            def pieces(dst, gate_from):
                def evacuate(j, t, acc, n=512):
                    at = j * 512
                    cut = min(max(gate_from - at, 0), n)
                    if 0 < cut < n:
                        settle(act.copy(dst[:, t, at:at + cut], acc[:, 0:cut]))
                    if cut < n:
                        return act.activation(dst[:, t, at + cut:at + n], acc[:, cut:n], ACT.Silu)
                    return act.copy(dst[:, t, at:at + n], acc[:, 0:n])
                return evacuate

            gemm("in_a", pieces(a2, 3 * AW))
            gemm("in_b", pieces(b2, 2 * BW), {**{2 + s: slots("moba", s) for s in range(9)},
                                              14: lambda: ln_root(4, 1)})
            gemm("in_b_end", lambda j, t, acc: pieces(b2, 2 * BW)(4, t, acc, 256))
            gemm("in_c", pieces(c2, CW), {1: lambda: turn("a", into(ht_hi))})

            gate = copy_through(ACT.Sigmoid, lambda j, t: sig[:, t, j * 512:(j + 1) * 512])
            gemm("gate_a", gate, {s: slots("xa", s) for s in range(7)})
            turn("b", into(ht_hi, 6))
            turn("c", into(ht_hi, 12))
            gemm("branch_a")
            gemm("gate_b", gate, after=[read("branch_a", 2)])
            gemm("branch_b")
            gemm("gate_c", gate, after=[(y_ready, 4)])
            gemm("branch_c")
            turn("y", into(xt_hi))
            gemm("out")
            rms(4, lambda t: x[:, t, :], arena[:, B2:B2 + D], D, [read("out", 2)])

        @block.vector
        def _(dve):
            done = {"chunks": 0, "steps": 0}

            def settle(ins):
                done["steps"] += 1
                ins.then_inc(dve_step, 1)
                dve.wait_ge(dve_step, done["steps"])

            def split_lo(c, i=None, per_turn=0):
                s, w = c % NS, WIDTH[c]
                dve.wait_ge(hi_done, plus(c + 1, i, per_turn))
                dve.tensor_tensor(w_lo[:, s, 0:w], stage[:, s, 0:w], w_hi[:, s, 0:w].bitcast(F32), ALU.subtract
                                  ).then_inc(lo_done, 1)

            def split_to(c):
                while done["chunks"] < min(c, CHUNKS):
                    split_lo(done["chunks"])
                    done["chunks"] += 1

            def gemm(name, evacuate=None, between=None):
                g = GEMMS[name]
                cps = g.kc // g.kp
                for j in range(g.steps):
                    for n in range(j * cps, (j + 1) * cps):
                        split_to(g.c0 + n + 1 + LEAD)
                        if between and n in between:
                            between[n]()
                    if evacuate is not None:
                        u = g.u0 + j
                        dve.wait_ge(chunk_used, g.c0 + (j + 1) * cps)
                        for t in range(TT):
                            evacuate(j, t, psum[:, 2 * (u % 2) + t, 0:g.n], acc_free[u % 2], 2 * (u // 2) + t + 1)

            def turn(name, hi, lo, part=None, i=None):
                kc, g0 = TURNS[name]
                for n in (range((kc + 1) // 2) if part is None else [part]):
                    g = g0 + n
                    w = min(2, kc - 2 * n)
                    dve.wait_ge(turn_hi, plus(g + 1, i, 2))
                    dve.tensor_tensor(lo(2 * n, w), psum[:, TURN_BANKS[g % 2], 0:w * S].rearrange(
                        "p (k n) -> p k n", k=w), hi(2 * n, w).bitcast(F32), ALU.subtract).then_inc(turn_lo, 1)

            into = lambda m, k0=0: (lambda k, w: m[:, k0 + k:k0 + k + w, :])
            into_x = (into(xt_hi), into(xt_lo))
            into_h = lambda k0=0: (into(ht_hi, k0), into(ht_lo, k0))

            def slot(stream, s):
                lo_h, hi_h = STREAMS[stream]
                h = lo_h + s - 3
                if lo_h <= h < hi_h:
                    hd = head_of(h)
                    dve.wait_ge(pv_ready, h + 1)
                    dv = hd.v(0).shape[-1]
                    for t in range(TT):
                        o, r = psum[:, O_BANK, t * dv:(t + 1) * dv], soft[:, h % 4, 4, t:t + 1]
                        if hd.gate is None:
                            last = dve.tensor_scalar(hd.out(t), o, r, None, ALU.mult)
                        else:
                            last = dve.scalar_tensor_tensor(hd.out(t), o, r, hd.gate(t), ALU.mult, ALU.mult)
                    last.then_inc(head_done, 1)
                h = lo_h + s - 2
                if lo_h <= h < hi_h:
                    hd = head_of(h)
                    b = h % 4
                    dve.wait_ge(exp_ready, h + 1)
                    if hd.sink is not None:
                        settle(dve.tensor_tensor(soft[:, b, 2, :], soft[:, b, 2, :], soft[:, b, 3, :], ALU.add))
                    settle(dve.reciprocal(soft[:, b, 4, :], soft[:, b, 2, :]))
                h = lo_h + s - 1
                if lo_h <= h < hi_h:
                    hd = head_of(h)
                    n0, b = keys0(hd), h % 4
                    dve.wait_ge(logits_ready, h + 1)
                    if h >= 2:
                        dve.wait_ge(p_turned, h - 1)
                    for t in range(TT):
                        at, nk = t * n0, S if t else n0
                        added = no_mask[:, 0:nk] if hd.mask is None else hd.mask[:, at:at + nk]
                        last = dve.tensor_tensor_reduce(probs[:, h % 2, at:at + nk], psum[:, LOGIT_BANK, at:at + nk],
                                                        added, hd.scale, -3e38, ALU.add, ALU.max,
                                                        soft[:, b, 0, t:t + 1])
                    settle(last)
                    if hd.sink is None:
                        last = dve.tensor_scalar(soft[:, b, 1, :], soft[:, b, 0, :], -1.0, None, ALU.mult)
                    else:
                        last = dve.tensor_scalar(soft[:, b, 1, :], soft[:, b, 0, :],
                                                 head_par[:, 0, hd.sink:hd.sink + 1], -1.0, ALU.max, ALU.mult)
                    last.then_inc(max_ready, 1)
                h = lo_h + s
                if lo_h <= h < hi_h:
                    hd = head_of(h)
                    dve.wait_ge(qk_turned, h + 1)
                    if h >= 2:
                        dve.wait_ge(logits_ready, h - 1)
                    dve.tensor_copy(qk_t[0:hd.dim, h % 2, :], psum[0:hd.dim, QK_BANK, :]).then_inc(qk_copied, 1)

            def slots(stream, *numbers):
                return lambda: [slot(stream, s) for s in numbers]

            def rms(k, src, dst, gain):
                dve.wait_ge(rms_sd, k + 1)
                settle(dve.reciprocal(rms_st[:, k, 2, :], rms_st[:, k, 1, :]))
                for t in range(TT):
                    dve.scalar_tensor_tensor(dst(t), src(t), rms_st[:, k, 2, t:t + 1], gain, ALU.mult, ALU.mult
                                             ).then_inc(rms_done, 1)

            def statistics(k, t, n, part):
                return dve.bn_stats(ln_st[:, k, 12 * t + 6 * n:12 * t + 6 * n + 6], part)

            def variances(k):
                for t in range(TT):
                    dve.bn_aggr(ln_st[:, k, 24 + 2 * t:26 + 2 * t], ln_st[:, k, 12 * t:12 * t + 12]
                                ).then_inc(ln_var, 1)

            def layer_norm(k, m, gain, bias=None):
                dve.wait_ge(ln_sd, k + 1)
                settle(dve.reciprocal(ln_st[:, k, 30:32], ln_st[:, k, 28:30]))
                for t in range(TT):
                    last = dve.scalar_tensor_tensor(m(t), m(t), ln_st[:, k, 24 + 2 * t:25 + 2 * t], gain,
                                                    ALU.subtract, ALU.mult)
                settle(last)
                for t in range(TT):
                    r = ln_st[:, k, 30 + t:31 + t]
                    if bias is None:
                        last = dve.tensor_scalar(m(t), m(t), r, None, ALU.mult)
                    else:
                        dve.scalar_tensor_tensor(m(t), m(t), r, bias, ALU.mult, ALU.add).then_inc(x_ready, 1)
                return last

            def residual(k):
                def evacuate(j, t, acc, freed, count):
                    part = x[:, t, j * 512:(j + 1) * 512]
                    dve.scalar_tensor_tensor(part, part, ALPHA, acc, ALU.mult, ALU.add).then_inc(freed, 1)
                    dve.wait_ge(freed, count)
                    done["stats"] = statistics(k, t, j, part)
                return evacuate

            def norm_x(k):
                settle(done["stats"])
                variances(k)
                dve.wait_ge(loaded[f"ln{k}"], 16)
                layer_norm(k, lambda t: x[:, t, :], ln_par[:, 0, :], ln_par[:, 1, :])

            def rotate(a, b, cos, sin, tmp):
                settle(dve.tensor_tensor(tmp(0), a, cos, ALU.mult))
                settle(dve.tensor_tensor(tmp(1), b, sin, ALU.mult))
                settle(dve.tensor_tensor(tmp(2), a, sin, ALU.mult))
                settle(dve.tensor_tensor(tmp(3), b, cos, ALU.mult))
                settle(dve.tensor_tensor(a, tmp(0), tmp(1), ALU.subtract))
                settle(dve.tensor_tensor(b, tmp(2), tmp(3), ALU.add))

            def angles(n, heads):
                return view(rope[:, n, :, :], 0, [[16, TT], [0, heads], [1, 16]])

            def up(layer):
                g, name = GEMMS[f"up{layer}"], f"h{layer}"
                cps = g.kc // g.kp
                silus = layer * 2 * g.steps

                def one(j, i=None):
                    for m in range(cps):
                        if i is None:
                            split_to(g.c0 + j * cps + m + 1 + LEAD)
                        else:
                            split_lo(g.c0 + j * cps + m + LEAD, i, 2 * cps)
                        if m == 1 and j:
                            k = 2 * (j - 1)
                            at = slice(k, k + 2) if i is None else bass.ds(i * 4 + k, 2)
                            turn(name, lambda a, b: ht_hi[:, at, :], lambda a, b: ht_lo[:, at, :], part=j - 1, i=i)
                    pair = (g.u0 + j) % 2
                    for t in range(TT):
                        dve.wait_ge(silu_ready, plus(silus + 2 * j + t + 1, i, 4))
                        dve.tensor_tensor(h_tile[:, j % 2, t, :], u_tile[:, j % 2, t, :],
                                          psum[:, 2 * pair + t, 256:512], ALU.mult).then_inc(acc_free[pair], 1)

                one(0)
                assert done["chunks"] == g.c0 + cps + LEAD
                with dve.Fori(0, 4) as i:
                    for s in range(2):
                        one(1 + s, i)
                done["chunks"] += 8 * cps
                one(9)
                one(10)

            def down(layer, k_norm):
                g = GEMMS[f"down{layer}"]
                for k in range(g.kc):
                    split_to(g.c0 + k + 1 + LEAD)
                    if k == 1:
                        turn(f"h{layer}", *into_h(), part=10)
                dve.wait_ge(chunk_used, g.c0 + g.kc)
                for j in range(2):
                    u = g.u0 + j
                    for t in range(TT):
                        residual(k_norm)(j, t, psum[:, 2 * (u % 2) + t, :], acc_free[u % 2], 2 * (u // 2) + t + 1)

            dve.memset(eps[:, 0:1], LN_EPS).then_inc(constants_set, 1)
            dve.memset(eps[:, 1:2], RMS_EPS).then_inc(constants_set, 1)
            split_to(LEAD)
            turn("x0", *into_x)

            def memory_norm():
                dve.wait_ge(loaded["mem_g"], 16)
                rms(0, lambda t: mem_x[:, t, :], lambda t: mem_x[:, t, :], row_g[:, :])

            gemm("ab_in", None, {4: memory_norm})
            turn("mem", *into_h())
            dve.wait_ge(loaded["gains"], 16)
            rms(1, lambda t: proj0[:, t, 0:Q_RANK], lambda t: proj0[:, t, 0:Q_RANK], gains[:, 0:Q_RANK])
            rms(2, lambda t: proj0[:, t, Q_RANK:Q_RANK + KV_RANK], lambda t: proj0[:, t, Q_RANK:Q_RANK + KV_RANK],
                gains[:, Q_RANK:])
            gemm("mem_k")
            turn("cq", *into_h(8))
            turn("ckv", *into_h(11))
            dve.wait_ge(loaded["swa"], 16)
            dve.wait_ge(loaded["heads"], 16)
            slot("l0", 0)
            gemm("uq", None, {0: slots("l0", 1), 1: slots("l0", 2), 2: slots("l0", 3)})
            gemm("ukv", None, {0: slots("l0", 4), 1: slots("l0", 5)})

            def mla_positions():
                dve.wait_ge(*read("uq", 3))
                dve.wait_ge(loaded["rope"], 16)
                q = q0.rearrange("p t (h n) -> p t h n", h=MLA_H)
                tmp = lambda heads: (lambda n: proj0[:, :, n * P:n * P + heads * 16].rearrange(
                    "p t (h n) -> p t h n", h=heads))
                rotate(q[:, :, :, 64:80], q[:, :, :, 80:96], angles(0, 8), angles(1, 8), tmp(8))
                kr = proj0[:, :, Q_RANK + KV_RANK:SWA_Q].rearrange("p t (h n) -> p t h n", h=1)
                rotate(kr[:, :, :, 0:16], kr[:, :, :, 16:32], angles(0, 1), angles(1, 1), tmp(1))
                dve.tensor_copy(k0[:, :, :, MLA_NOPE:],
                                view(proj0[:, 0, Q_RANK + KV_RANK:SWA_Q], 0, [[AB_W, TT], [0, MLA_H], [1, MLA_ROPE]])
                                ).then_inc(mla_ready, 1)

            mla_positions()
            slots("l0", 6, 7)()
            dve.wait_ge(loaded["masks"], 16)
            gemm("mem_v", None, {0: slots("l0", 8), 1: slots("l0", 9, 10), 2: slots("l0", 11, 12),
                                 3: slots("l0", 13, 14)})
            slots("l0", 15, 16, 17, 18)()
            turn("o0", *into_x)
            gemm("ab_out", residual(0))
            norm_x(0)
            turn("f0", *into_x)
            up(0)
            down(0, 1)
            norm_x(1)
            turn("x1", *into_x)

            def forget_abs():
                dve.wait_ge(*read("cd_in", 4))
                f = proj1[:, :, 3 * FOX_H * HD:CK_Q]
                bias = view(head_par[:, 1, :], 0, [[0, TT], [1, 8]])
                settle(dve.tensor_tensor(log_f[:, 0, :, :], f, bias, ALU.add))
                dve.scalar_tensor_tensor(log_f[:, 1, :, :], log_f[:, 0, :, :], -1.0, log_f[:, 0, :, :],
                                         ALU.mult, ALU.max).then_inc(f_abs, 1)

            def forget_log():
                dve.wait_ge(f_ln, 1)
                dve.scalar_tensor_tensor(log_f[:, 3, :, :], log_f[:, 0, :, :], 0.0, log_f[:, 1, :, :],
                                         ALU.min, ALU.subtract).then_inc(log_f_ready, 1)

            def copy_cumulated():
                dve.wait_ge(cum_ready, 1)
                dve.tensor_copy(cum_k[0:FOX_H, :], psum[0:FOX_H, O_BANK, 0:S]).then_inc(cum_copied, 1)

            gemm("cd_in", None, {16: forget_abs, 17: forget_log, 18: copy_cumulated,
                                 **{19 + s: slots("l1", s) for s in range(8)}})
            dve.wait_ge(rel_ready, 2)
            slots("l1", *range(8, 19))()
            turn("o1", *into_x)
            gemm("cd_out", residual(2))
            norm_x(2)
            turn("f1", *into_x)
            up(1)
            down(1, 3)
            norm_x(3)
            dve.wait_ge(loaded["norm_g"], 16)
            rms(3, lambda t: x[:, t, :], lambda t: region(B2, D)[:, t, :], row_g[:, :])
            turn("x2", *into_x)

            def moba_positions():
                dve.wait_ge(*read("in_a", 3))
                tmp = lambda n: region(12800, 4 * 96)[:, :, n * 96:(n + 1) * 96].rearrange(
                    "p t (h n) -> p t h n", h=MOBA_H)
                for at in (0, AW):
                    m = a2[:, :, at:at + AW].rearrange("p t (h n) -> p t h n", h=MOBA_H)
                    rotate(m[:, :, :, 0:ROT2], m[:, :, :, ROT2:2 * ROT2], angles(2, MOBA_H), angles(3, MOBA_H), tmp)
                dve.nop().then_inc(moba_ready, 1)

            gemm("in_a", None, {13: moba_positions})

            def gmlp_stats():
                dve.wait_ge(*read("in_b", 3))
                for t in range(TT):
                    for n in range(2):
                        last = statistics(4, t, n, b2[:, t, BW + n * 384:BW + (n + 1) * 384])
                settle(last)
                variances(4)

            def gmlp_norm():
                dve.wait_ge(loaded["gmlp_g"], 16)
                layer_norm(4, lambda t: b2[:, t, BW:2 * BW], row_g[:, 0:BW]).then_inc(vn_ready, 1)

            gemm("in_b", None, {**{2 + s: slots("moba", s) for s in range(9)}, 13: gmlp_stats, 15: gmlp_norm})
            gemm("in_b_end")

            def gate_b(groups):
                dve.wait_ge(*read("in_b_end", 1))
                for g in groups:
                    dve.wait_ge(mixed, g + 1)
                    u = b2[:, :, g * P:(g + 1) * P]
                    acc = psum[:, PT_BANK + g % 2, 0:S].rearrange("p (t n) -> p t n", t=TT)
                    settle(dve.scalar_tensor_tensor(u, acc, bsp[:, g:g + 1], u, ALU.add, ALU.mult))
                    dve.tensor_tensor(u, u, b2[:, :, 2 * BW + g * P:2 * BW + (g + 1) * P], ALU.mult
                                      ).then_inc(gated_b, 1)

            gemm("in_c", None, {1: lambda: turn("a", *into_h()), 2: lambda: gate_b(range(3)),
                                3: lambda: gate_b(range(3, 6))})
            gemm("gate_a", None, {s: slots("xa", s) for s in range(7)})
            turn("b", *into_h(6))
            turn("c", *into_h(12))

            def branch(n):
                def evacuate(j, t, acc, freed, count):
                    y, s = y2[:, t, j * 512:(j + 1) * 512], sig[:, t, j * 512:(j + 1) * 512]
                    dve.tensor_tensor(s if n else y, acc, s, ALU.mult).then_inc(freed, 1)
                    if n:
                        dve.wait_ge(freed, count)
                        dve.tensor_tensor(y, y, s, ALU.add).then_inc(y_ready, 1)
                return evacuate

            dve.wait_ge(*read("gate_a", 2))
            gemm("branch_a", branch(0))
            gemm("gate_b")
            dve.wait_ge(*read("gate_b", 2))
            gemm("branch_b", branch(1))
            gemm("gate_c")
            dve.wait_ge(*read("gate_c", 2))
            gemm("branch_c", branch(2))
            turn("y", *into_x)

            def last_residual(j, t, acc, freed, count):
                part = x[:, t, j * 512:(j + 1) * 512]
                dve.tensor_tensor(part, part, acc, ALU.add).then_inc(freed, 1)

            gemm("out", last_residual)
            dve.wait_ge(loaded["final_g"], 16)
            rms(4, lambda t: x[:, t, :], a2_out, row_g[:, :])


def chunks_of(w, name):
    g = GEMMS[name]
    w = w.reshape(g.kc // g.kp, g.kp, P, g.steps, g.n).transpose(3, 0, 2, 1, 4)
    return np.ascontiguousarray(w.reshape(-1, P, g.kp * g.n))


def shape_constants():
    q, k = np.arange(S)[:, None], np.arange(S)[None, :]
    by_chunk = np.where(k // CH <= q // CH, 0.0, MASKED)
    causal = np.where(k <= q, 0.0, MASKED)
    window = np.where((k // CH <= q // CH) & (k // CH >= q // CH - 2), 0.0, MASKED)

    def tiles(m):
        return np.concatenate([m[0:P, 0:P], m[P:S, :]], 1)

    slopes = np.exp2(-8.0 * np.arange(1, SWA_H + 1) / SWA_H)
    swa = np.stack([tiles(np.where(window < 0, MASKED, -s * np.abs(q - k) * HD ** 0.5)) for s in slopes], 1)

    def angles(theta, width):
        inv = np.float32(theta) ** (-np.arange(0, width, 2, dtype=np.float32) / np.float32(width))
        a = (np.arange(S, dtype=np.float32)[:, None] * inv[None, :].astype(np.float32)).astype(np.float64)
        return [f(a).reshape(TT, P, width // 2).transpose(1, 0, 2) for f in (np.cos, np.sin)]

    c = {"ident": np.eye(P), "masks": np.stack([tiles(by_chunk), tiles(causal)], 1), "swa": swa,
         "rope": np.stack(angles(10000.0, MLA_ROPE) + angles(500000.0, 2 * ROT2), 1),
         "cum": np.where(q <= k, -HD ** 0.5, 0.0).reshape(TT, P, S).transpose(1, 0, 2),
         "sel": np.repeat(np.eye(FOX_H), P, 1)}
    return {n: np.ascontiguousarray(a, dtype=np.float32) for n, a in c.items()}


def kernel(**inputs):
    import concourse.bacc as bacc
    from concourse.bass_utils import run_bass_kernel_spmd

    a = {k: np.asarray(v) for k, v in inputs.items()}
    w2 = a["w_in_2"][0]
    cut = np.cumsum([0, 4 * AW, 3 * BW, 2 * CW, D, D, D])
    in_a, in_b, in_c, gate_a, gate_b, gate_c = (w2[:, cut[n]:cut[n + 1]] for n in range(6))

    def up_of(layer):
        g, u = (a[n][layer].reshape(D, FF // 256, 256) for n in ("ffn_w_gate", "ffn_w_up"))
        return np.stack([g, u], 2).reshape(D, 2 * FF)

    weights = {"ab_in": a["ab_w_in"][0], "mem_k": a["w_mem_kv_2"][0][:, :CW], "uq": a["ab_w_uq"][0],
               "ukv": a["ab_w_ukv"][0], "mem_v": a["w_mem_kv_2"][0][:, CW:], "ab_out": a["ab_w_out"][0],
               "up0": up_of(0), "down0": a["ffn_w_down"][0], "cd_in": a["cd_w_in"][0], "cd_out": a["cd_w_out"][0],
               "up1": up_of(1), "down1": a["ffn_w_down"][1], "in_a": in_a, "in_b": in_b[:, :2048],
               "in_b_end": in_b[:, 2048:], "in_c": in_c, "gate_a": gate_a, "branch_a": a["w_branch_a_2"][0],
               "gate_b": gate_b, "branch_b": a["w_branch_b_2"][0], "gate_c": gate_c,
               "branch_c": a["w_branch_c_2"][0], "out": a["w_out_2"][0]}
    arrays = {"w_" + n: chunks_of(w, n) for n, w in weights.items()}
    rel = np.zeros((CK_H, REL_PITCH), np.float32)
    rel[:, CH:] = a["cd_rel_bias"][0].T
    arrays.update(
        x=a["x"][0], mem=a["mem_2"][0], mem_norm_g=a["mem_norm_g_2"][0], norm_g=a["norm_g_2"][0],
        final_g=a["final_norm_g_2"], gmlp_g=a["gmlp_ln_g_2"][0],
        gains=np.concatenate([a["ab_q_norm"][0], a["ab_kv_norm"][0]]),
        head_par=np.concatenate([a["ab_sinks"][0], a["cd_b_forget"][0]]),
        ln=np.stack([np.stack([a[f"{n}_g"][k], a[f"{n}_b"][k]]) for k in range(2) for n in ("ln1", "ln2")]),
        wsp=a["w_spatial_2"][0].transpose(2, 0, 1), bsp=a["b_spatial_2"][0].T, rel=rel, **shape_constants())
    arrays = {n: np.ascontiguousarray(m) for n, m in arrays.items()}

    nc = bacc.Bacc("TRN2", target_bir_lowering=False, num_devices=1)
    d = {n: nc.dram_tensor(f"in_{n}", m.shape, mybir.dt.from_np(m.dtype), kind="ExternalInput").ap()
         for n, m in arrays.items()}
    out = nc.dram_tensor("out_x", (S, D), F32, kind="ExternalOutput").ap()
    build_program(nc, d, out)
    r = run_bass_kernel_spmd(nc, [{f"in_{n}": m for n, m in arrays.items()}], core_ids=[0])
    return r.results[0]["out_x"].reshape(1, S, D)
```

```python
from collections import namedtuple
from contextlib import ExitStack

import numpy as np
import concourse.bass as bass
from concourse import mybir

F32 = mybir.dt.float32
F32R = mybir.dt.float32r
ACT = mybir.ActivationFunctionType
ALU = mybir.AluOpType

P = 128
TT = 2
S = TT * P
D = 1024
CH = 64
MASKED = -1e30
HALF_D = D // 2

MLA_H, MLA_NOPE, MLA_ROPE, MLA_V = 8, 64, 32, 64
MLA_D = MLA_NOPE + MLA_ROPE
Q_RANK, KV_RANK = 384, 256
SWA_H, SWA_KV, HD = 8, 2, 64
FOX_H = CK_H = 8
AB_W = Q_RANK + KV_RANK + MLA_ROPE + SWA_H * HD + 2 * SWA_KV * HD
CD_W = 3 * FOX_H * HD + FOX_H + 3 * CK_H * HD
FF = 2816
ALPHA = 4 ** 0.25
LN_EPS, RMS_EPS = 1e-5, 1e-6
REL, REL_PITCH = 320, 384
MOBA_H, XA_H, HD2 = 6, 4, 128
AW, BW, CW = MOBA_H * HD2, 6 * 128, XA_H * HD2
ROT2 = 16

NS = 4
SLOT = 1024
LEAD = NS - 1

Gemm = namedtuple("Gemm", "name kc kp n steps c0 u0")


def plan_gemms():
    table = [("ab_in", 8, 2, 480, 3), ("uq", 3, 3, 256, 3), ("ukv", 2, 2, 512, 2), ("mem_k", 8, 2, 512, 1),
             ("mem_v", 8, 2, 512, 1), ("ab_out", 8, 1, 1024, 1), ("up0", 8, 2, 512, 11), ("down0", 22, 1, 1024, 1),
             ("cd_in", 8, 2, 440, 7), ("cd_out", 8, 1, 1024, 1), ("up1", 8, 2, 512, 11), ("down1", 22, 1, 1024, 1),
             ("in_a", 8, 2, 512, 6), ("in_b", 8, 2, 512, 4), ("in_b_end", 8, 4, 256, 1), ("in_c", 8, 2, 512, 2),
             ("gate_a", 8, 2, 512, 2), ("branch_a", 6, 2, 512, 2), ("gate_b", 8, 2, 512, 2),
             ("branch_b", 6, 2, 512, 2), ("gate_c", 8, 2, 512, 2), ("branch_c", 4, 1, 1024, 1),
             ("out", 8, 1, 1024, 1)]
    plan, c, u = {}, 0, 0
    for name, kc, kp, n, steps in table:
        plan[name] = Gemm(name, kc, kp, n, steps, c, u)
        c += steps * kc // kp
        u += steps * (2 if n > 512 else 1)
    return plan, c


GEMMS, CHUNKS = plan_gemms()
WIDTH = [g.kp * g.n for g in GEMMS.values() for _ in range(g.steps * g.kc // g.kp)]


def plan_turns():
    table = [("x0", 8), ("mem", 8), ("cq", 3), ("ckv", 2), ("o0a", 4), ("o0b", 4), ("f0", 8), ("h0", 22), ("x1", 8), ("o1a", 4), ("o1b", 4),
             ("f1", 8), ("h1", 22), ("x2", 8), ("a", 6), ("b", 6), ("c", 4), ("y", 8)]
    plan, at = {}, 0
    for name, kc in table:
        plan[name] = (kc, at)
        at += kc // 2 if name[0] == "h" else TT * -(-kc // 4)
    return plan


TURNS = plan_turns()

def turned_at(names, t, k):
    if isinstance(names, tuple):
        return turned_at(names[k // 4], t, k % 4)
    name = names
    kc, g0 = TURNS[name]
    return g0 + 1 + (k // 2 if name[0] == "h" else t * -(-kc // 4) + k // 4)


STREAMS = {"l0": (0, 16), "l1": (16, 32), "moba": (32, 38), "xa": (38, 42)}

L1_SLOTS = {8: 0, 9: 1, 10: 2, 11: 3, 13: 4, 14: 5, 17: 6, 18: 7, 19: 8, 21: 9, 22: 10, 25: 11, 26: 12}

MEM_K, MEM_V, TAB = 0, 1024, 2048
PROJ0, Q0, K0, V0, O0 = 5120, 8000, 9536, 11072, 12096
PROJ1, O1, CUM = 5120, 11280, 13328
A2, B2 = 2048, 8192
ARENA = 14144


def view(base, offset, dims):
    return bass.AP(tensor=base.tensor, offset=base.offset + offset, ap=[base.ap[0]] + [list(d) for d in dims])


def plus(value, i, per_turn):
    return value if i is None else value + i * per_turn


def build_program(nc, d, out):
    with ExitStack() as ctx:
        def sb(name, shape, dt=F32):
            return ctx.enter_context(nc.sbuf_tensor(name, shape, dt))

        def sem(name):
            return ctx.enter_context(nc.semaphore(name))

        stage = sb("stage", [P, NS, SLOT])
        w_hi = sb("w_hi", [P, NS, SLOT], F32R)
        w_lo = sb("w_lo", [P, NS, SLOT], F32R)
        xt_hi = sb("xt_hi", [P, 8, S], F32R)
        xt_lo = sb("xt_lo", [P, 8, S], F32R)
        ht_hi = sb("ht_hi", [P, 22, S], F32R)
        ht_lo = sb("ht_lo", [P, 22, S], F32R)
        x = sb("x", [P, TT, D])
        arena = sb("arena", [P, ARENA])
        ident = sb("ident", [P, P])
        masks = sb("masks", [P, 2, 384])
        no_mask = sb("no_mask", [P, 256])
        qk_t = sb("qk_t", [P, 2, 512])
        probs = sb("probs", [P, 2, 512])
        probs_t = sb("probs_t", [P, 2, 512])
        ln_par = sb("ln_par", [P, 2, D])
        row_g = sb("row_g", [P, D])
        rope = sb("rope", [P, 4, TT, 16])
        head_par = sb("head_par", [P, 2, 8])
        wsp = sb("wsp", [P, 6, P])
        bsp = sb("bsp", [P, 6])
        cum_k = sb("cum_k", [P, S])
        log_f = sb("log_f", [P, 4, TT, 8])
        eps = sb("eps", [P, 2])
        rms_st = sb("rms_st", [P, 5, 3, 2])
        ln_st = sb("ln_st", [P, 5, 32])
        soft = sb("soft", [P, 4, 5, 2])
        psum = ctx.enter_context(nc.psum_tensor("psum", [P, 8, 512], F32))
        TURN_BANKS = {"cq": (2, 3), "ckv": (2, 3), "o0a": (0, 1), "o1a": (0, 1)}
        QK_BANK, LOGIT_BANK, PT_BANK, O_BANK = 4, 5, 6, 7


        def turn_bank(name, g):
            return psum[:, TURN_BANKS.get(name, (4, 5))[g % 2], :]

        def turn_parts(name, tiles):
            kc, g0 = TURNS[name]
            per = -(-kc // 4)
            return [(g0 + t * per + q, t, 4 * q, min(4, kc - 4 * q)) for t in tiles for q in range(per)]

        staged = [sem(f"staged{s}") for s in range(NS)]
        hi_done, lo_done = sem("hi_done"), sem("lo_done")
        chunk_used = sem("chunk_used")
        tile0_done = sem("tile0_done")
        acc_free = [sem("acc_free0"), sem("acc_free1")]
        turned, turn_hi, turn_lo = sem("turned"), sem("turn_hi"), sem("turn_lo")
        qk_turned, qk_copied = sem("qk_turned"), sem("qk_copied")
        logits_ready, max_ready, exp_ready = sem("logits_ready"), sem("max_ready"), sem("exp_ready")
        p_turned, p_copied = sem("p_turned"), sem("p_copied")
        pv_ready, head_done = sem("pv_ready"), sem("head_done")
        silu_ready = sem("silu_ready")
        ln_var, ln_sd, x_ready = sem("ln_var"), sem("ln_sd"), sem("x_ready")
        rms_sd, rms_done = sem("rms_sd"), sem("rms_done")
        act_step, dve_step, pool_step = sem("act_step"), sem("dve_step"), sem("pool_step")
        constants_set = sem("constants_set")
        mla_ready, moba_ready = sem("mla_ready"), sem("moba_ready")
        f_abs, f_ln, log_f_ready, cum_ready, cum_copied = (sem("f_abs"), sem("f_ln"), sem("log_f_ready"),
                                                           sem("cum_ready"), sem("cum_copied"))
        rel_ready, wsp_ready = sem("rel_ready"), sem("wsp_ready")
        vn_ready, mixed, gated_b = sem("vn_ready"), sem("mixed"), sem("gated_b")
        y_ready, stored = sem("y_ready"), sem("stored")
        h2_ready = sem("h2_ready")
        loads = ["x0", "x1", "ident", "mem_g", "mem", "gains", "rope", "swa", "masks", "heads", "ln0", "ln1", "ln2", "ln3",
                 "rel", "cum", "sel", "norm_g", "gmlp_g", "final_g", "wsp", "bsp"]
        loaded = {n: sem(f"loaded_{n}") for n in loads}

        def cols(at, width, dims=None):
            return arena[:, at:at + width]

        def region(at, width):
            return arena[:, at:at + TT * width].rearrange("p (t n) -> p t n", t=TT)

        mem_x, o0 = region(O0, D), region(O0, D)
        mem_k, mem_v = region(MEM_K, CW), region(MEM_V, CW)
        proj0, q0, proj1, o1 = region(PROJ0, AB_W), region(Q0, MLA_H * MLA_D), region(PROJ1, CD_W), region(O1, D)
        k0 = arena[:, K0:K0 + TT * MLA_H * MLA_D].rearrange("p (t h n) -> p t h n", t=TT, h=MLA_H)
        v0 = arena[:, V0:V0 + TT * MLA_H * MLA_V].rearrange("p (t h n) -> p t h n", t=TT, h=MLA_H)
        gains = cols(V0, Q_RANK + KV_RANK)
        table = arena[:, TAB:TAB + 8 * 384].rearrange("p (h n) -> p h n", h=8)
        rel_raw = arena[:, PROJ0:PROJ0 + 8 * 384].rearrange("p (h n) -> p h n", h=8)
        cum_tri = region(CUM, S)
        h2 = region(B2, D)
        a2 = region(A2, 4 * AW)
        b2 = region(B2, 3 * BW)
        c2 = region(A2 + 6144 - 2 * 2 * CW, 2 * CW)
        a2_out = lambda t: a2[:, t, 0:D]
        y2 = region(A2 + 2 * D, D)
        sig = ln_par
        u_tile = qk_t[:, :, :].rearrange("p b (t n) -> p b t n", t=TT)
        h_tile = probs[:, :, :].rearrange("p b (t n) -> p b t n", t=TT)

        SWA_AT = Q_RANK + KV_RANK + MLA_ROPE
        SWA_GROUP = (2 + SWA_H // SWA_KV) * HD
        FOX_AT = FOX_H
        CK_AT = FOX_AT + 3 * FOX_H * HD

        Head = namedtuple("Head", "dim scale q k v mask full out gate sink fox")

        def head_of(h):
            cut = lambda m, at, w: (lambda t: m[:, t, at:at + w])
            if h < 8:
                at = SWA_AT + h // 4 * SWA_GROUP
                return Head(HD, HD ** -0.5, cut(proj0, at + (2 + h % 4) * HD, HD), cut(proj0, at, HD),
                            cut(proj0, at + HD, HD), table[:, h, :], False,
                            cut(o0, h * HD, HD), None, h, None)
            if h < 16:
                h -= 8
                return Head(MLA_D, MLA_D ** -0.5, cut(q0, h * MLA_D, MLA_D), lambda t: k0[:, t, h, :],
                            lambda t: v0[:, t, h, :], masks[:, 0, :], False, cut(o0, SWA_H * HD + h * MLA_V, MLA_V),
                            None, None, None)
            if h < 24:
                h -= 16
                at = FOX_AT + 3 * h * HD
                return Head(HD, HD ** -0.5, cut(proj1, at, HD), cut(proj1, at + HD, HD),
                            cut(proj1, at + 2 * HD, HD), masks[:, 1, :], False, cut(o1, h * HD, HD),
                            None, None, h)
            if h < 32:
                h -= 24
                at = CK_AT + 3 * h * HD
                return Head(HD, HD ** -0.5, cut(proj1, at, HD), cut(proj1, at + HD, HD),
                            cut(proj1, at + 2 * HD, HD), table[:, h, :], False,
                            cut(o1, (FOX_H + h) * HD, HD), None, None, None)
            if h < 38:
                h -= 32
                return Head(HD2, HD2 ** -0.5, cut(a2, h * HD2, HD2), cut(a2, AW + h * HD2, HD2),
                            cut(a2, 2 * AW + h * HD2, HD2), masks[:, 1, :], False, cut(a2, h * HD2, HD2),
                            cut(a2, 3 * AW + h * HD2, HD2), None, None)
            h -= 38
            return Head(HD2, HD2 ** -0.5, cut(c2, h * HD2, HD2), cut(mem_k, h * HD2, HD2), cut(mem_v, h * HD2, HD2),
                        None, True, cut(c2, h * HD2, HD2), cut(c2, CW + h * HD2, HD2), None, None)

        def keys0(hd):
            return S if hd.full else P

        def read(name, steps):
            u = GEMMS[name].u0 + steps - 1
            return acc_free[u % 2], TT * (u // 2 + 1)

        block = ctx.enter_context(nc.Block())

        @block.sync
        def _(sp):
            sp.dma_start(ident[:, :], d["ident"]).then_inc(loaded["ident"], 16)

            def load_x(t):
                sp.dma_start(x[:, t, :], d["x"][t * P:(t + 1) * P, :]).then_inc(loaded[f"x{t}"], 16)

            load_x(0)

            def load_chunk(g, n, i=None):
                c = g.c0 + n
                s, w = c % NS, WIDTH[c]
                if c >= NS or i is not None:
                    sp.wait_ge(lo_done, plus(c - NS + 1, i, NS))
                src = d["w_" + g.name]
                src = src[n] if i is None else src[bass.ds(i * NS + n, 1), :, :].rearrange("a p n -> (a p) n")
                sp.dma_start(stage[:, s, 0:w], src).then_inc(staged[s], 16)

            for g in GEMMS.values():
                chunks = g.steps * g.kc // g.kp
                n = 0
                while g.c0 + n < NS and n < chunks:
                    load_chunk(g, n)
                    n += 1
                    if g.c0 + n == 2:
                        load_x(1)
                turns = (chunks - n) // NS
                if turns >= 2:
                    with sp.Fori(0, turns) as i:
                        for m in range(NS):
                            load_chunk(g, n + m, i)
                    n += turns * NS
                for m in range(n, chunks):
                    load_chunk(g, m)
            for t in range(TT):
                sp.wait_ge(rms_done, 9 + t)
                sp.dma_start(out[t * P:(t + 1) * P, :], a2_out(t)).then_inc(stored, 16)
            sp.wait_ge(stored, 16 * TT)

        @block.gpsimd
        def _(pool):
            def load(name, dst, src):
                pool.dma_start(dst, src).then_inc(loaded[name], 16)

            def row(src, n):
                return bass.AP(tensor=src.tensor, offset=src.offset, ap=[[0, P], [1, n]])

            pool.memset(no_mask[:, :], 0.0).then_inc(constants_set, 1)
            pool.wait_ge(hi_done, 2)
            load("mem_g", row_g[:, :], row(d["mem_norm_g"], D))
            load("mem", mem_x, d["mem"].rearrange("(t p) n -> p t n", t=TT))
            load("gains", gains, row(d["gains"], Q_RANK + KV_RANK))
            load("heads", head_par[:, :, :].rearrange("p a h -> p (a h)"), row(d["head_par"], 16))
            pool.wait_ge(hi_done, 2 * NS)
            load("swa", table, d["swa"])
            load("rope", rope[:, :, :, :], d["rope"])
            pool.wait_ge(hi_done, 3 * NS)
            load("masks", masks[:, :, :], d["masks"])
            load("ln0", ln_par[:, :, :].rearrange("p a n -> p (a n)"),
                 bass.AP(tensor=d["ln"].tensor, offset=0, ap=[[0, P], [1, 2 * D]]))
            load("bsp", bsp[:, :], d["bsp"])
            load("wsp", wsp[:, :, :], d["wsp"])
            pool.wait_ge(loaded["wsp"], 16)
            pool.affine_select(out=wsp[:, :, :], in_=wsp[:, :, :], compare_op=ALU.is_ge, fill=0.0, base=0,
                               pattern=[[0, 6], [1, P]], channel_multiplier=-1).then_inc(wsp_ready, 1)
            pool.wait_ge(rms_done, 2)
            load("sel", row_g[0:8, :], d["sel"])

            def split_fourth(name):
                c = GEMMS[name].c0 + NS - 1
                s, w = c % NS, WIDTH[c]
                pool.wait_ge(hi_done, c + 1)
                pool.wait_ge(lo_done, c)
                pool.tensor_tensor(w_lo[:, s, 0:w], stage[:, s, 0:w], w_hi[:, s, 0:w].bitcast(F32), ALU.subtract
                                   ).then_inc(lo_done, 1)

            split_fourth("up0")
            pool.wait_ge(head_done, STREAMS["l0"][1])
            rel = d["rel"]
            for at, keys in ((0, P), (P, S)):
                load("rel", rel_raw[:, :, at:at + keys],
                     bass.AP(tensor=rel.tensor, offset=0, ap=[[1, P], [REL_PITCH, CK_H], [1, keys]]))
            pool.wait_ge(loaded["rel"], 32)
            for at, keys in ((0, P), (P, S)):
                last = pool.tensor_scalar(table[:, :, at:at + keys],
                                          view(rel_raw[:, 0, 0:1], at + keys - 1, [[384, CK_H], [-1, keys]]),
                                          HD ** 0.5, None, ALU.mult)
            last.then_inc(pool_step, 1)
            pool.wait_ge(pool_step, 1)
            pool.memset(table[0:CH, :, CH:P], MASKED).then_inc(rel_ready, 1)
            pool.memset(table[0:CH, :, P + S - CH:P + S], MASKED).then_inc(rel_ready, 1)
            load("cum", cum_tri, d["cum"])
            for k in range(1, 4):
                pool.wait_ge(x_ready, 2 * TT * k)
                load(f"ln{k}", ln_par[:, :, :].rearrange("p a n -> p (a n)"),
                     bass.AP(tensor=d["ln"].tensor, offset=2 * D * k, ap=[[0, P], [1, 2 * D]]))
                if k == 3:
                    pool.wait_ge(logits_ready, STREAMS["l1"][1])
                    load("norm_g", row_g[:, :], row(d["norm_g"], D))
                split_fourth(["cd_in", "up1", "in_a"][k - 1])
            pool.wait_ge(h2_ready, 4)
            load("gmlp_g", row_g[:, 0:BW], row(d["gmlp_g"], BW))
            pool.wait_ge(vn_ready, 1)
            load("final_g", row_g[:, :], row(d["final_g"], D))

        @block.tensor
        def _(pe):
            def turn(name, src, ready, tiles=range(TT)):
                for g, t, k0, w in turn_parts(name, tiles):
                    for s, v in ready(t, k0) if callable(ready) else ready:
                        pe.wait_ge(s, v)
                    if g >= 2:
                        pe.wait_ge(turn_lo, g - 1)
                    for k in range(w):
                        last = pe.transpose(turn_bank(name, g)[:, k * P:(k + 1) * P], src(k0 + k, t), ident[:, :])
                    last.then_inc(turned, 1)

            def step(g, j, hi, lo, k0=0, turned_by=None, between=None, i=None, per_turn=0, second=None):
                u, cps = g.u0 + j, g.kc // g.kp
                pair = u % 2
                passes = [(t,) for t in range(TT)] if second else [tuple(range(TT))]
                for tiles in passes:
                    if second and tiles == (1,):
                        second()
                    if u >= 2 or i is not None:
                        pe.wait_ge(acc_free[pair], plus(2 * (u // 2) - (tiles == (0,)), i, per_turn))
                    for m in range(cps):
                        n = j * cps + m
                        c = g.c0 + n
                        s = c % NS
                        if i is not None:
                            pe.wait_ge(lo_done, plus(c + 1, i, per_turn * cps))
                        for kk in range(g.kp):
                            k = m * g.kp + kk
                            wh, wl = w_hi[:, s, kk * g.n:(kk + 1) * g.n], w_lo[:, s, kk * g.n:(kk + 1) * g.n]
                            for t in tiles:
                                turn_of = turned_by is not None and j == 0 and turned_at(turned_by, t, k)
                                acc = psum[:, 2 * pair + t, 0:g.n]
                                ah, al = hi[:, k0 + k, t * P:(t + 1) * P], lo[:, k0 + k, t * P:(t + 1) * P]
                                if i is None:
                                    pe.wait_ge(hi_done, c + 1)
                                if turn_of:
                                    pe.wait_ge(turn_hi, turn_of)
                                pe.matmul(acc, ah, wh, start=(k == 0), stop=False)
                                if i is None:
                                    pe.wait_ge(lo_done, c + 1)
                                pe.matmul(acc, ah, wl, start=False, stop=False)
                                if turn_of:
                                    pe.wait_ge(turn_lo, turn_of)
                                last = pe.matmul(acc, al, wh, start=False, stop=(k == g.kc - 1))
                        if tiles[-1] == 1:
                            last.then_inc(chunk_used, 1)
                            if between and n in between:
                                between[n]()

            def gemm(name, hi, lo, k0=0, turned_by=None, between=None, second=None):
                g = GEMMS[name]
                for j in range(g.steps):
                    step(g, j, hi, lo, k0, turned_by, between, second=second if j == 0 else None)

            def wide(name, hi, lo, turned_by, k0=0, between=None, head=0, second=None):
                g = GEMMS[name]
                apart = not head and g.kc > NS
                for half in range(1 if apart else 2):
                    u = g.u0 + half
                    pe.wait_ge(acc_free[u % 2], 2 * (u // 2) - (second is not None))
                if isinstance(turned_by, tuple):
                    pe.wait_ge(turn_lo, turned_at(turned_by, 1, 0))
                spans = [(0, head)] if head else []
                spans += [(k, k + 1) for k in range(head, g.kc - NS)]
                if g.kc - NS >= head:
                    spans.append((g.kc - NS, g.kc))

                def products(k, t, halves):
                    c = g.c0 + k
                    s = c % NS
                    turn_of = turned_at(turned_by, t, k)
                    ah, al = hi[:, k0 + k, t * P:(t + 1) * P], lo[:, k0 + k, t * P:(t + 1) * P]
                    for a, w in ((ah, w_hi), (ah, w_lo), (al, w_hi)):
                        if w is w_lo:
                            pe.wait_ge(lo_done, c + 1)
                        elif a is ah:
                            pe.wait_ge(hi_done, c + 1)
                            pe.wait_ge(turn_hi, turn_of)
                        else:
                            pe.wait_ge(turn_lo, turn_of)
                        for half in halves:
                            last = pe.matmul(psum[:, 2 * ((g.u0 + half) % 2) + t, :], a,
                                             w[:, s, half * 512:(half + 1) * 512],
                                             start=(k == 0 and w is w_hi and a is ah),
                                             stop=(k == g.kc - 1 and a is al))
                    return last

                for first, end in spans:
                    if first == 0 and apart:
                        products(0, 0, [0])
                        products(0, 1, [0])
                        u = g.u0 + 1
                        pe.wait_ge(acc_free[u % 2], 2 * (u // 2))
                        products(0, 0, [1])
                        products(0, 1, [1]).then_inc(chunk_used, 1)
                        if between and 0 in between:
                            between[0]()
                        continue
                    for t in range(TT):
                        if t and first == 0 and second is not None:
                            second()
                            for pair in range(2):
                                u = g.u0 + (pair - g.u0) % 2
                                pe.wait_ge(acc_free[pair], 2 * (u // 2))
                        for k in range(first, end):
                            last = products(k, t, range(2))
                            if t == 1:
                                last.then_inc(chunk_used, 1)
                                if between and k in between:
                                    between[k]()
                            elif k == g.kc - 1:
                                last.then_inc(tile0_done, 1)

            def up(layer, second):
                g, name = GEMMS[f"up{layer}"], f"h{layer}"
                g0 = TURNS[name][1]

                def turn_step(j, i=None):
                    u = g.u0 + j
                    pe.wait_ge(acc_free[u % 2], plus(2 * (u // 2 + 1), i, 2))
                    pe.wait_ge(turn_lo, plus(g0 + j - 1, i, 2))
                    for k in range(2):
                        for t in range(TT):
                            last = pe.transpose(turn_bank(name, g0 + j)[:, (k * TT + t) * P:(k * TT + t + 1) * P],
                                                h_tile[:, j % 2, t, k * P:(k + 1) * P], ident[:, :])
                    last.then_inc(turned, 1)

                cps = g.kc // g.kp

                def one(j, i=None):
                    between = {j * cps + 1: lambda: turn_step(j - 1, i)} if j else None
                    step(g, j, xt_hi, xt_lo, 0, f"f{layer}", between, i, 2, None if j else second)

                one(0)
                with pe.Fori(0, 4) as i:
                    for s in range(2):
                        one(1 + s, i)
                one(9)
                one(10)
                return lambda: turn_step(10)

            def slot(stream, s):
                lo_h, hi_h = STREAMS[stream]
                h = lo_h + s
                if lo_h <= h < hi_h:
                    hd = head_of(h)
                    if h == 8:
                        pe.wait_ge(mla_ready, 1)
                        pe.wait_ge(*read("ukv", 2))
                    if 16 <= h < 32:
                        pe.wait_ge(*read("cd_in", -(-(FOX_AT + 3 * (h - 15) * HD) // GEMMS["cd_in"].n)))
                    if h == 0 or h == 2:
                        pe.wait_ge(*read("ab_in", 2 if h == 0 else 3))
                    if h >= 1:
                        pe.wait_ge(qk_copied, h)
                    for n, src in enumerate((hd.q(0), hd.q(1), hd.k(0), hd.k(1))):
                        last = pe.transpose(psum[0:hd.dim, QK_BANK, n * P:(n + 1) * P], src, ident[:, :])
                    last.then_inc(qk_turned, 1)
                h = lo_h + s - 3
                if lo_h <= h < hi_h:
                    hd = head_of(h)
                    pe.wait_ge(p_copied, h + 1)
                    if h >= 1:
                        pe.wait_ge(head_done, h)
                    dv = hd.v(0).shape[-1]
                    for t in range(TT):
                        kts = range(TT) if hd.full or t else range(1)
                        for kt in kts:
                            n = (kt * TT + t) if hd.full else (t + kt)
                            last = pe.matmul(psum[:, O_BANK, t * dv:(t + 1) * dv],
                                             probs_t[:, h % 2, n * P:(n + 1) * P], hd.v(kt),
                                             start=(kt == 0), stop=(kt == kts[-1]))
                    last.then_inc(pv_ready, 1)
                h = lo_h + s - 2
                if lo_h <= h < hi_h:
                    hd = head_of(h)
                    pe.wait_ge(exp_ready, h + 1)
                    if h >= 1:
                        pe.wait_ge(p_copied, h)
                    n0 = keys0(hd)
                    pairs = ([(0, 0), (0, 1), (1, 0), (1, 1)] if hd.full else [(0, 0), (0, 1), (1, 1)])
                    for n, (kt, t) in enumerate(pairs):
                        at = t * n0 + kt * P
                        last = pe.transpose(psum[:, PT_BANK, n * P:(n + 1) * P], probs[:, h % 2, at:at + P],
                                            ident[:, :])
                    last.then_inc(p_turned, 1)
                h = lo_h + s - 1
                if lo_h <= h < hi_h:
                    hd = head_of(h)
                    pe.wait_ge(qk_copied, h + 1)
                    if h >= 1:
                        pe.wait_ge(max_ready, h)
                    n0 = keys0(hd)
                    for t in range(TT):
                        nk = S if t else n0
                        acc = psum[:, LOGIT_BANK, t * n0:t * n0 + nk]
                        last = pe.matmul(acc, qk_t[0:hd.dim, h % 2, t * P:(t + 1) * P],
                                         qk_t[0:hd.dim, h % 2, S:S + nk], start=True, stop=hd.fox is None)
                        if hd.fox is not None:
                            if h == STREAMS["l1"][0] and t == 0:
                                pe.wait_ge(cum_copied, 1)
                                pe.wait_ge(loaded["sel"], 16)
                            last = pe.matmul(acc, row_g[0:8, hd.fox * P:(hd.fox + 1) * P], cum_k[0:8, 0:nk],
                                             start=False, stop=True)
                    last.then_inc(logits_ready, 1)

            def slots(stream, *numbers):
                return lambda: [slot(stream, s) for s in numbers]

            tile_of = lambda m, at=0: (lambda k, t: m[:, t, at + k * P:at + (k + 1) * P])

            pe.wait_ge(loaded["ident"], 16)
            turn("x0", tile_of(x), [(loaded["x0"], 16)], [0])

            def heads_banks(name):
                pe.wait_ge(turn_lo, TURNS[name][1])

            def turn_low_rank():
                pe.wait_ge(*read("ab_in", 2))
                turn("cq", tile_of(proj0), [(rms_done, 4)])
                turn("ckv", tile_of(proj0, Q_RANK), [(rms_done, 6)])

            gemm("ab_in", xt_hi, xt_lo, 0, "x0",
                 {7: lambda: turn("mem", tile_of(mem_x), [(rms_done, 1)], [0]),
                  8: lambda: turn("mem", tile_of(mem_x), [(rms_done, 2)], [1]), 9: turn_low_rank,
                  10: lambda: [heads_banks("cq"), slot("l0", 0)], 11: slots("l0", 1)},
                 second=lambda: turn("x0", tile_of(x), [(loaded["x1"], 16)], [1]))
            pe.wait_ge(turn_lo, turned_at("ckv", 1, 1))
            gemm("uq", ht_hi, ht_lo, 8, "cq", {n: slots("l0", 2 + n) for n in range(3)})
            gemm("ukv", ht_hi, ht_lo, 11, "ckv", {n: slots("l0", 5 + n) for n in range(2)})
            gemm("mem_k", ht_hi, ht_lo, 0, None, {n: slots("l0", 7 + n) for n in range(4)})

            def first_results(name, src, heads, free):
                pe.wait_ge(*free)
                turn(name, tile_of(src), [(head_done, heads)])

            gemm("mem_v", ht_hi, ht_lo, 0, None,
                 {0: slots("l0", 11), 1: lambda: [slot("l0", 12), first_results("o0a", o0, 8, read("mem_k", 1))],
                  2: slots("l0", 13), 3: slots("l0", 14)})

            def after_norm(name, k):
                half = lambda t, k0: [(x_ready, 4 * k + 2 * t + k0 // 4 + 1)]
                turn(name, tile_of(x), half, [0])
                return lambda: turn(name, tile_of(x), half, [1])

            def last_results(name, src, stream, s):
                slots(stream, *s)()
                turn(name, tile_of(src, 4 * P), [(head_done, STREAMS[stream][1])])

            wide("ab_out", xt_hi, xt_lo, ("o0a", "o0b"),
                 between={0: slots("l0", 15), 1: slots("l0", 16), 2: slots("l0", 17),
                          3: lambda: last_results("o0b", o0, "l0", [18])})
            second = after_norm("f0", 0)
            wide("down0", ht_hi, ht_lo, "h0", between={1: up(0, second)})
            second = after_norm("x1", 1)

            def cumulate():
                pe.wait_ge(log_f_ready, 1)
                pe.wait_ge(loaded["cum"], 16)
                for t in range(TT):
                    last = pe.matmul(psum[0:FOX_H, O_BANK, 0:S], log_f[:, 3, t, :], cum_tri[:, t, :],
                                     start=(t == 0), stop=(t == TT - 1))
                last.then_inc(cum_ready, 1)

            gemm("cd_in", xt_hi, xt_lo, 0, "x1",
                 {7: lambda: [heads_banks("o1a"), cumulate()], **{n: slots("l1", s) for n, s in L1_SLOTS.items()},
                  24: lambda: first_results("o1a", o1, 24, read("cd_in", 6))},
                 second=second)
            wide("cd_out", ht_hi, ht_lo, ("o1a", "o1b"),
                 between={0: slots("l1", 13), 1: slots("l1", 14), 2: slots("l1", 15),
                          3: lambda: last_results("o1b", o1, "l1", [16, 17, 18])})
            second = after_norm("f1", 2)
            wide("down1", ht_hi, ht_lo, "h1", between={1: up(1, second)})
            h2_of = lambda t, k0: [(h2_ready, 2 * t + k0 // 4 + 1)]
            turn("x2", tile_of(h2), h2_of, [0])
            gemm("in_a", xt_hi, xt_lo, 0, "x2", second=lambda: turn("x2", tile_of(h2), h2_of, [1]))

            def moba_first():
                heads_banks("a")
                pe.wait_ge(moba_ready, 1)
                pe.wait_ge(*read("in_a", 6))
                slot("moba", 0)

            gemm("in_b", xt_hi, xt_lo, 0, None, {2: moba_first, **{2 + s: slots("moba", s) for s in range(1, 9)}})
            gemm("in_b_end", xt_hi, xt_lo)

            def mix(groups):
                for g in groups:
                    if g == 0:
                        pe.wait_ge(vn_ready, 1)
                        pe.wait_ge(wsp_ready, 1)
                    if g >= 2:
                        pe.wait_ge(gated_b, g - 1)
                    pe.matmul(psum[:, PT_BANK + g % 2, 0:S].rearrange("p (t n) -> p t n", t=TT), wsp[:, g, :],
                              b2[:, :, BW + g * P:BW + (g + 1) * P], start=True, stop=True).then_inc(mixed, 1)

            gemm("in_c", xt_hi, xt_lo, 0, None,
                 {0: lambda: turn("a", tile_of(a2), [(head_done, 38)], [0]),
                  1: lambda: turn("a", tile_of(a2), [(head_done, 38)], [1]),
                  **{2 + g: lambda g=g: mix([g]) for g in range(6)}})

            def xa_first():
                pe.wait_ge(*read("in_c", 2))
                heads_banks("b")
                pe.wait_ge(gated_b, 6)
                slot("xa", 0)

            gemm("gate_a", xt_hi, xt_lo, 0, None, {0: xa_first, **{s: slots("xa", s) for s in range(1, 7)}})
            gemm("branch_a", ht_hi, ht_lo, 0, "a",
                 {0: lambda: turn("b", tile_of(b2), [(gated_b, 6), (head_done, 42)], [0]),
                  1: lambda: turn("b", tile_of(b2), [], [1]),
                  2: lambda: turn("c", tile_of(c2), [(head_done, 42)])})
            gemm("gate_b", xt_hi, xt_lo)
            gemm("branch_b", ht_hi, ht_lo, 6, "b")
            gemm("gate_c", xt_hi, xt_lo)
            wide("branch_c", ht_hi, ht_lo, "c", 12)
            y_of = lambda t, k0: [(y_ready, 4 + 2 * t + k0 // 4 + 1)]
            turn("y", tile_of(y2), y_of, [0])
            wide("out", xt_hi, xt_lo, "y", head=NS, second=lambda: turn("y", tile_of(y2), y_of, [1]))

        @block.scalar
        def _(act):
            done = {"chunks": 0, "steps": 0, "due": 0}

            def settle(ins):
                done["steps"] += 1
                ins.then_inc(act_step, 1)
                act.wait_ge(act_step, done["steps"])

            def split_hi(c, i=None, per_turn=0):
                s, w = c % NS, WIDTH[c]
                act.wait_ge(staged[s], plus(16 * (c // NS + 1), i, 16 * per_turn // NS))
                if c >= NS or i is not None:
                    act.wait_ge(chunk_used, plus(c - NS + 1, i, per_turn))
                act.copy(w_hi[:, s, 0:w], stage[:, s, 0:w]).then_inc(hi_done, 1)

            def split_to(c):
                while done["chunks"] < min(c, CHUNKS):
                    split_hi(done["chunks"])
                    done["chunks"] += 1

            def gemm(name, evacuate=None, between=None, after=()):
                g = GEMMS[name]
                cps = g.kc // g.kp
                for j in range(g.steps):
                    for n in range(j * cps, (j + 1) * cps):
                        done["due"] = g.c0 + n + 1 + LEAD
                        if evacuate is not None and n == (j + 1) * cps - 1:
                            for s, v in after if j == 0 else ():
                                act.wait_ge(s, v)
                            pair = (g.u0 + j) % 2
                            act.wait_ge(chunk_used, g.c0 + n + 1)
                            for t in range(TT):
                                evacuate(j, t, psum[:, 2 * pair + t, :]).then_inc(acc_free[pair], 1)
                        if between and n in between:
                            between[n]()
                        split_to(done["due"])

            def turn(name, hi, k0=0, tiles=range(TT)):
                for g, t, k, w in turn_parts(name, tiles):
                    act.wait_ge(turned, g + 1)
                    act.copy(hi[:, k0 + k:k0 + k + w, t * P:(t + 1) * P],
                             turn_bank(name, g)[:, 0:w * P].rearrange("p (k n) -> p k n", k=w)).then_inc(turn_hi, 1)

            def turn_hidden(layer, j, dst, i=None):
                name = f"h{layer}"
                g = TURNS[name][1] + j
                act.wait_ge(turned, plus(g + 1, i, 2))
                act.copy(dst, turn_bank(name, g).rearrange("p (k n) -> p k n", k=2)).then_inc(turn_hi, 1)

            def wide(name, between=None):
                g = GEMMS[name]
                for k in range(g.kc):
                    done["due"] = min(g.c0 + k + 1 + LEAD, g.c0 + g.kc)
                    if between and k in between:
                        between[k]()
                    split_to(done["due"])

            def slot(stream, s):
                lo_h, hi_h = STREAMS[stream]
                h = lo_h + s - 2
                if lo_h <= h < hi_h:
                    hd = head_of(h)
                    w = 4 * P if hd.full else 3 * P
                    act.wait_ge(p_turned, h + 1)
                    if h >= 2:
                        act.wait_ge(pv_ready, h - 1)
                    act.copy(probs_t[:, h % 2, 0:w], psum[:, PT_BANK, 0:w]).then_inc(p_copied, 1)
                split_to(done["due"])
                h = lo_h + s - 1
                if lo_h <= h < hi_h:
                    hd = head_of(h)
                    n0, b = keys0(hd), h % 4
                    act.wait_ge(max_ready, h + 1)
                    if hd.sink is not None:
                        act.activation(soft[:, b, 3, :], soft[:, b, 1, :], ACT.Exp,
                                       bias=head_par[:, 0, hd.sink:hd.sink + 1])
                    for t in range(TT):
                        p = probs[:, h % 2, t * n0:t * n0 + (S if t else n0)]
                        last = act.activation(p, p, ACT.Exp, bias=soft[:, b, 1, t:t + 1],
                                              accum_out=soft[:, b, 2, t:t + 1])
                    last.then_inc(exp_ready, 1)

            def slots(stream, *numbers):
                return lambda: [slot(stream, s) for s in numbers]

            def rms(k, src, junk, n, ready, tiles=range(TT)):
                for t in tiles:
                    for s, v in ready(t) if callable(ready) else ready:
                        act.wait_ge(s, v)
                    settle(act.activation(junk, src(t), ACT.Square, accum_out=rms_st[:, k, 0, t:t + 1]))
                    act.activation(rms_st[:, k, 1, t:t + 1], rms_st[:, k, 0, t:t + 1], ACT.Sqrt, scale=1.0 / n,
                                   bias=eps[:, 1:2]).then_inc(rms_sd, 1)

            def deviation(k, t, which_eps=0):
                act.wait_ge(ln_var, TT * k + t + 1)
                act.activation(ln_st[:, k, 28 + t:29 + t], ln_st[:, k, 25 + 2 * t:26 + 2 * t], ACT.Sqrt,
                               bias=eps[:, which_eps:which_eps + 1]).then_inc(ln_sd, 1)

            def norm_and_turn(k, name):
                end = done["chunks"]
                act.preload_act_table(ACT.Sqrt)
                deviation(k, 0)
                split_to(end + LEAD)
                turn(name, xt_hi, 0, [0])
                split_to(end + NS)
                deviation(k, 1)
                turn(name, xt_hi, 0, [1])

            def copy_to(dst):
                return lambda j, t, acc: act.copy(*dst(j, t, acc))

            def up(layer):
                g, name = GEMMS[f"up{layer}"], f"h{layer}"
                cps = g.kc // g.kp
                act.preload_act_table(ACT.Silu)

                def one(j, i=None):
                    for m in range(cps):
                        if i is None:
                            split_to(g.c0 + j * cps + m + 1 + LEAD)
                        else:
                            split_hi(g.c0 + j * cps + m + LEAD, i, 2 * cps)
                        if m == 1 and j:
                            k = 2 * (j - 1)
                            turn_hidden(layer, j - 1,
                                        ht_hi[:, k:k + 2, :] if i is None else ht_hi[:, bass.ds(i * 4 + k, 2), :], i)
                    pair = (g.u0 + j) % 2
                    act.wait_ge(chunk_used, plus(g.c0 + (j + 1) * cps, i, 2 * cps))
                    for t in range(TT):
                        act.activation(u_tile[:, j % 2, t, :], psum[:, 2 * pair + t, 0:256], ACT.Silu
                                       ).then_inc(silu_ready, 1)

                one(0)
                assert done["chunks"] == g.c0 + cps + LEAD
                with act.Fori(0, 4) as i:
                    for s in range(2):
                        one(1 + s, i)
                done["chunks"] += 8 * cps
                one(9)
                one(10)

            def down(layer):
                wide(f"down{layer}", {1: lambda: turn_hidden(layer, 10, ht_hi[:, 20:22, :])})

            act.preload_act_table(ACT.Sqrt)
            turn("x0", xt_hi, 0, [0])
            split_to(NS)
            turn("x0", xt_hi, 0, [1])

            def memory_norm():
                act.wait_ge(constants_set, 3)
                rms(0, lambda t: mem_x[:, t, :], arena[:, Q0:Q0 + D], D, [(loaded["mem"], 16)])

            def low_rank_norms():
                rms(1, lambda t: proj0[:, t, 0:Q_RANK], arena[:, K0:K0 + Q_RANK], Q_RANK, [read("ab_in", 2)])
                rms(2, lambda t: proj0[:, t, Q_RANK:Q_RANK + KV_RANK], arena[:, K0:K0 + KV_RANK], KV_RANK, [])

            def first_slot():
                act.wait_ge(loaded["heads"], 16)
                slot("l0", 0)

            gemm("ab_in", copy_to(lambda j, t, acc: (proj0[:, t, j * 480:(j + 1) * 480], acc[:, 0:480])),
                 {4: memory_norm, 7: lambda: [turn("mem", ht_hi, 0, [0]), low_rank_norms()],
                  8: lambda: turn("mem", ht_hi, 0, [1]),
                  9: lambda: [turn("cq", ht_hi, 8), turn("ckv", ht_hi, 11), act.preload_act_table(ACT.Exp)], 10: first_slot, 11: slots("l0", 1)})
            gemm("uq", copy_to(lambda j, t, acc: (q0[:, t, j * 256:(j + 1) * 256], acc[:, 0:256])),
                 {n: slots("l0", 2 + n) for n in range(3)})

            def split_kv(j, t, acc):
                kv = acc.rearrange("p (h n) -> p h n", h=4)
                settle(act.copy(k0[:, t, 4 * j:4 * j + 4, 0:MLA_NOPE], kv[:, :, 0:MLA_NOPE]))
                return act.copy(v0[:, t, 4 * j:4 * j + 4, :], kv[:, :, MLA_NOPE:])

            gemm("ukv", split_kv, {n: slots("l0", 5 + n) for n in range(2)})
            gemm("mem_k", copy_to(lambda j, t, acc: (mem_k[:, t, :], acc)),
                 {n: slots("l0", 7 + n) for n in range(4)})
            gemm("mem_v", copy_to(lambda j, t, acc: (mem_v[:, t, :], acc)),
                 {0: slots("l0", 11), 1: lambda: [slot("l0", 12), turn("o0a", xt_hi)],
                  2: slots("l0", 13), 3: slots("l0", 14)})
            wide("ab_out", {0: slots("l0", 15), 1: slots("l0", 16), 2: slots("l0", 17),
                            3: lambda: [slot("l0", 18), turn("o0b", xt_hi, 4)]})
            norm_and_turn(0, "f0")
            up(0)
            down(0)
            norm_and_turn(1, "x1")

            def log_sigmoid():
                act.wait_ge(f_abs, 1)
                settle(act.activation(log_f[:, 2, :, :], log_f[:, 1, :, :], ACT.Exp, scale=-1.0))
                act.activation(log_f[:, 1, :, :], log_f[:, 2, :, :], ACT.Ln, bias=1.0).then_inc(f_ln, 1)

            gemm("cd_in", copy_to(lambda j, t, acc: (proj1[:, t, j * 440:(j + 1) * 440], acc[:, 0:440])),
                 {4: log_sigmoid, **{n: slots("l1", s) for n, s in L1_SLOTS.items()},
            24: lambda: turn("o1a", ht_hi)})
            wide("cd_out", {0: slots("l1", 13), 1: slots("l1", 14), 2: slots("l1", 15),
                            3: lambda: [slots("l1", 16, 17, 18)(), turn("o1b", ht_hi, 4)]})
            norm_and_turn(2, "f1")
            up(1)
            down(1)
            act.preload_act_table(ACT.Sqrt)
            end = done["chunks"]
            deviation(3, 0)
            split_to(end + LEAD)
            turn("x2", xt_hi, 0, [0])
            h_junk = arena[:, B2 + TT * D:B2 + TT * D + D]
            rms(3, lambda t: x[:, t, :], h_junk, D, lambda t: [(x_ready, 14 + 2 * t)], [0])
            split_to(end + NS)
            deviation(3, 1)
            turn("x2", xt_hi, 0, [1])
            rms(3, lambda t: x[:, t, :], h_junk, D, lambda t: [(x_ready, 14 + 2 * t)], [1])
            root = lambda t: rms_st[:, 3, 2, t:t + 1]
            act.wait_ge(rms_done, 8)

            def pieces(dst, gate_from):
                def evacuate(j, t, acc, n=512):
                    at = j * 512
                    cut = min(max(gate_from - at, 0), n)
                    if 0 < cut < n:
                        settle(act.activation(dst[:, t, at:at + cut], acc[:, 0:cut], ACT.Copy, scale=root(t)))
                    if cut < n:
                        return act.activation(dst[:, t, at + cut:at + n], acc[:, cut:n], ACT.Silu,
                                              scale=root(t))
                    return act.activation(dst[:, t, at:at + n], acc[:, 0:n], ACT.Copy, scale=root(t))
                return evacuate

            gemm("in_a", pieces(a2, 3 * AW))
            gemm("in_b", pieces(b2, 2 * BW), {**{2 + s: slots("moba", s) for s in range(9)},
                                              14: lambda: [deviation(4, 0, 1), deviation(4, 1, 1)]})
            gemm("in_b_end", lambda j, t, acc: pieces(b2, 2 * BW)(4, t, acc, 256))
            gemm("in_c", pieces(c2, CW), {0: lambda: turn("a", ht_hi, 0, [0]), 1: lambda: turn("a", ht_hi, 0, [1])})

            def gate(j, t, acc):
                return act.activation(sig[:, t, j * 512:(j + 1) * 512], acc, ACT.Sigmoid, scale=root(t))

            act.wait_ge(x_ready, 16)
            gemm("gate_a", gate, {s: slots("xa", s) for s in range(7)})
            gemm("branch_a", None, {0: lambda: turn("b", ht_hi, 6, [0]), 1: lambda: turn("b", ht_hi, 6, [1]),
                                    2: lambda: turn("c", ht_hi, 12)})
            gemm("gate_b", gate, after=[read("branch_a", 2)])
            gemm("branch_b")
            gemm("gate_c", gate, after=[(y_ready, 4)])
            wide("branch_c")
            end = done["chunks"]
            split_to(end + LEAD)
            turn("y", xt_hi, 0, [0])
            split_to(end + NS)
            turn("y", xt_hi, 0, [1])
            wide("out")
            act.preload_act_table(ACT.Sqrt)
            rms(4, lambda t: x[:, t, :], arena[:, B2:B2 + D], D, lambda t: [(x_ready, 16 + 2 * (t + 1))])

        @block.vector
        def _(dve):
            done = {"chunks": 0, "steps": 0}

            def settle(ins):
                done["steps"] += 1
                ins.then_inc(dve_step, 1)
                dve.wait_ge(dve_step, done["steps"])

            def split_lo(c, i=None, per_turn=0):
                s, w = c % NS, WIDTH[c]
                dve.wait_ge(hi_done, plus(c + 1, i, per_turn))
                dve.tensor_tensor(w_lo[:, s, 0:w], stage[:, s, 0:w], w_hi[:, s, 0:w].bitcast(F32), ALU.subtract
                                  ).then_inc(lo_done, 1)

            def split_to(c):
                while done["chunks"] < min(c, CHUNKS):
                    split_lo(done["chunks"])
                    done["chunks"] += 1

            def gemm(name, evacuate=None, between=None):
                g = GEMMS[name]
                cps = g.kc // g.kp
                for j in range(g.steps):
                    for n in range(j * cps, (j + 1) * cps):
                        if evacuate is not None and n == (j + 1) * cps - 1:
                            u = g.u0 + j
                            dve.wait_ge(chunk_used, g.c0 + n + 1)
                            for t in range(TT):
                                evacuate(j, t, psum[:, 2 * (u % 2) + t, 0:g.n], acc_free[u % 2],
                                         2 * (u // 2) + t + 1)
                        if between and n in between:
                            between[n]()
                        split_to(g.c0 + n + 1 + LEAD)

            def turn(name, hi, lo, k0=0, tiles=range(TT)):
                for part in turn_parts(name, tiles):
                    turn_part(part, hi, lo, k0, name)

            def turn_part(part, hi, lo, k0, name=None):
                g, t, k, w = part
                dst = (slice(None), slice(k0 + k, k0 + k + w), slice(t * P, (t + 1) * P))
                dve.wait_ge(turn_hi, g + 1)
                dve.tensor_tensor(lo[dst], turn_bank(name, g)[:, 0:w * P].rearrange("p (k n) -> p k n", k=w),
                                  hi[dst].bitcast(F32), ALU.subtract).then_inc(turn_lo, 1)

            def turn_hidden(layer, j, at, i=None):
                name = f"h{layer}"
                g = TURNS[name][1] + j
                dve.wait_ge(turn_hi, plus(g + 1, i, 2))
                dve.tensor_tensor(ht_lo[:, at, :], turn_bank(name, g).rearrange("p (k n) -> p k n", k=2),
                                  ht_hi[:, at, :].bitcast(F32), ALU.subtract).then_inc(turn_lo, 1)

            def wide(name, between=None):
                g = GEMMS[name]
                for k in range(g.kc):
                    if between and k in between:
                        between[k]()
                    split_to(min(g.c0 + k + 1 + LEAD, g.c0 + g.kc))

            def summed(name, t, tile0):
                g = GEMMS[name]
                if t == 0:
                    dve.wait_ge(tile0_done, tile0)
                else:
                    dve.wait_ge(chunk_used, g.c0 + g.kc)

            def halves(name, t, evacuate):
                g = GEMMS[name]
                for j in range(2):
                    u = g.u0 + j
                    evacuate(j, t, psum[:, 2 * (u % 2) + t, :], acc_free[u % 2], 2 * (u // 2) + t + 1)

            def slot(stream, s):
                lo_h, hi_h = STREAMS[stream]
                h = lo_h + s
                if lo_h <= h < hi_h:
                    hd = head_of(h)
                    dve.wait_ge(qk_turned, h + 1)
                    if h >= 2:
                        dve.wait_ge(logits_ready, h - 1)
                    dve.tensor_copy(qk_t[0:hd.dim, h % 2, :], psum[0:hd.dim, QK_BANK, :]).then_inc(qk_copied, 1)
                h = lo_h + s - 3
                if lo_h <= h < hi_h:
                    hd = head_of(h)
                    dve.wait_ge(pv_ready, h + 1)
                    dv = hd.v(0).shape[-1]
                    for t in range(TT):
                        o, r = psum[:, O_BANK, t * dv:(t + 1) * dv], soft[:, h % 4, 4, t:t + 1]
                        if hd.gate is None:
                            last = dve.tensor_scalar(hd.out(t), o, r, None, ALU.mult)
                        else:
                            last = dve.scalar_tensor_tensor(hd.out(t), o, r, hd.gate(t), ALU.mult, ALU.mult)
                    last.then_inc(head_done, 1)
                h = lo_h + s - 2
                if lo_h <= h < hi_h:
                    hd = head_of(h)
                    b = h % 4
                    dve.wait_ge(exp_ready, h + 1)
                    if hd.sink is not None:
                        settle(dve.tensor_tensor(soft[:, b, 2, :], soft[:, b, 2, :], soft[:, b, 3, :], ALU.add))
                    settle(dve.reciprocal(soft[:, b, 4, :], soft[:, b, 2, :]))
                h = lo_h + s - 1
                if lo_h <= h < hi_h:
                    hd = head_of(h)
                    n0, b = keys0(hd), h % 4
                    if h == 24:
                        dve.wait_ge(rel_ready, 2)
                    dve.wait_ge(logits_ready, h + 1)
                    if h >= 2:
                        dve.wait_ge(p_turned, h - 1)
                    for t in range(TT):
                        at, nk = t * n0, S if t else n0
                        added = no_mask[:, 0:nk] if hd.mask is None else hd.mask[:, at:at + nk]
                        last = dve.tensor_tensor_reduce(probs[:, h % 2, at:at + nk], psum[:, LOGIT_BANK, at:at + nk],
                                                        added, hd.scale, -3e38, ALU.add, ALU.max,
                                                        soft[:, b, 0, t:t + 1])
                    settle(last)
                    if hd.sink is None:
                        last = dve.tensor_scalar(soft[:, b, 1, :], soft[:, b, 0, :], -1.0, None, ALU.mult)
                    else:
                        last = dve.tensor_scalar(soft[:, b, 1, :], soft[:, b, 0, :],
                                                 head_par[:, 0, hd.sink:hd.sink + 1], -1.0, ALU.max, ALU.mult)
                    last.then_inc(max_ready, 1)

            def slots(stream, *numbers):
                return lambda: [slot(stream, s) for s in numbers]

            def rms(k, src, dst, gain, tiles=range(TT)):
                for t in tiles:
                    dve.wait_ge(rms_sd, TT * k + t + 1)
                    settle(dve.reciprocal(rms_st[:, k, 2, t:t + 1], rms_st[:, k, 1, t:t + 1]))
                    dve.scalar_tensor_tensor(dst(t), src(t), rms_st[:, k, 2, t:t + 1], gain, ALU.mult, ALU.mult
                                             ).then_inc(rms_done, 1)

            def statistics(k, t, n, part):
                return dve.bn_stats(ln_st[:, k, 12 * t + 6 * n:12 * t + 6 * n + 6], part)

            def variance(k, t):
                dve.bn_aggr(ln_st[:, k, 24 + 2 * t:26 + 2 * t], ln_st[:, k, 12 * t:12 * t + 12]).then_inc(ln_var, 1)

            def deviate(k, t, m, gain, first=True):
                r = ln_st[:, k, 30 + t:31 + t]
                if first:
                    dve.wait_ge(ln_sd, TT * k + t + 1)
                    dve.reciprocal(r, ln_st[:, k, 28 + t:29 + t])
                settle(dve.scalar_tensor_tensor(m, m, ln_st[:, k, 24 + 2 * t:25 + 2 * t], gain,
                                                ALU.subtract, ALU.mult))
                return r

            def sum_tile(k, name, t):
                summed(name, t, k + 1)

                def evacuate(j, t, acc, freed, count):
                    part = x[:, t, j * 512:(j + 1) * 512]
                    dve.scalar_tensor_tensor(part, part, ALPHA, acc, ALU.mult, ALU.add).then_inc(freed, 1)

                halves(name, t, evacuate)
                for j in range(2):
                    u = GEMMS[name].u0 + j
                    dve.wait_ge(acc_free[u % 2], 2 * (u // 2) + t + 1)
                    last = statistics(k, t, j, x[:, t, j * 512:(j + 1) * 512])
                settle(last)
                variance(k, t)

            def norm_tile(k, t):
                dve.wait_ge(loaded[f"ln{k}"], 16)
                for j in range(2):
                    part = x[:, t, j * 512:(j + 1) * 512]
                    r = deviate(k, t, part, ln_par[:, 0, j * 512:(j + 1) * 512], j == 0)
                    dve.scalar_tensor_tensor(part, part, r, ln_par[:, 1, j * 512:(j + 1) * 512],
                                             ALU.mult, ALU.add).then_inc(x_ready, 1)

            def turn_and_split(name):
                for part in turn_parts(name, [0]):
                    split_to(done["chunks"] + 1)
                    turn_part(part, xt_hi, xt_lo, 0)
                split_to(done["chunks"] + 1)
                done["chunks"] += 1

            def norm_and_turn(k, projection, name):
                sum_tile(k, projection, 0)
                norm_tile(k, 0)
                turn_and_split(name)
                sum_tile(k, projection, 1)
                norm_tile(k, 1)
                turn(name, xt_hi, xt_lo, 0, [1])

            def rotate(a, b, cos, sin, tmp):
                settle(dve.tensor_tensor(tmp(0), a, cos, ALU.mult))
                settle(dve.tensor_tensor(tmp(1), b, sin, ALU.mult))
                settle(dve.tensor_tensor(tmp(2), a, sin, ALU.mult))
                settle(dve.tensor_tensor(tmp(3), b, cos, ALU.mult))
                settle(dve.tensor_tensor(a, tmp(0), tmp(1), ALU.subtract))
                settle(dve.tensor_tensor(b, tmp(2), tmp(3), ALU.add))

            def angles(n, heads):
                return view(rope[:, n, :, :], 0, [[16, TT], [0, heads], [1, 16]])

            def up(layer):
                g, name = GEMMS[f"up{layer}"], f"h{layer}"
                cps = g.kc // g.kp
                silus = layer * 2 * g.steps

                def one(j, i=None):
                    for m in range(cps):
                        if i is None:
                            split_to(g.c0 + j * cps + m + 1 + LEAD)
                        else:
                            split_lo(g.c0 + j * cps + m + LEAD, i, 2 * cps)
                        if m == 1 and j:
                            k = 2 * (j - 1)
                            turn_hidden(layer, j - 1, slice(k, k + 2) if i is None else bass.ds(i * 4 + k, 2), i)
                    pair = (g.u0 + j) % 2
                    for t in range(TT):
                        dve.wait_ge(silu_ready, plus(silus + 2 * j + t + 1, i, 4))
                        dve.tensor_tensor(h_tile[:, j % 2, t, :], u_tile[:, j % 2, t, :],
                                          psum[:, 2 * pair + t, 256:512], ALU.mult).then_inc(acc_free[pair], 1)

                one(0)
                assert done["chunks"] == g.c0 + cps + LEAD
                with dve.Fori(0, 4) as i:
                    for s in range(2):
                        one(1 + s, i)
                done["chunks"] += 8 * cps
                one(9)
                one(10)

            def down(layer):
                wide(f"down{layer}", {1: lambda: turn_hidden(layer, 10, slice(20, 22))})

            dve.memset(eps[:, 0:1], LN_EPS).then_inc(constants_set, 1)
            dve.memset(eps[:, 1:2], RMS_EPS).then_inc(constants_set, 1)
            turn("x0", xt_hi, xt_lo, 0, [0])
            split_to(NS)
            turn("x0", xt_hi, xt_lo, 0, [1])

            def memory_norm():
                dve.wait_ge(loaded["mem_g"], 16)
                rms(0, lambda t: mem_x[:, t, :], lambda t: mem_x[:, t, :], row_g[:, :])

            def first_slot():
                dve.wait_ge(loaded["swa"], 16)
                dve.wait_ge(loaded["heads"], 16)
                slot("l0", 0)

            def low_rank_norms():
                dve.wait_ge(loaded["gains"], 16)
                rms(1, lambda t: proj0[:, t, 0:Q_RANK], lambda t: proj0[:, t, 0:Q_RANK], gains[:, 0:Q_RANK])
                rms(2, lambda t: proj0[:, t, Q_RANK:Q_RANK + KV_RANK], lambda t: proj0[:, t, Q_RANK:Q_RANK + KV_RANK],
                    gains[:, Q_RANK:])

            gemm("ab_in", None, {4: memory_norm, 7: lambda: [turn("mem", ht_hi, ht_lo, 0, [0]), low_rank_norms()],
                                 8: lambda: turn("mem", ht_hi, ht_lo, 0, [1]),
                                 9: lambda: [turn("cq", ht_hi, ht_lo, 8), turn("ckv", ht_hi, ht_lo, 11)],
                                 10: first_slot, 11: slots("l0", 1)})
            gemm("uq", None, {n: slots("l0", 2 + n) for n in range(3)})
            gemm("ukv", None, {n: slots("l0", 5 + n) for n in range(2)})

            def mla_positions():
                dve.wait_ge(*read("uq", 3))
                dve.wait_ge(loaded["rope"], 16)
                q = q0.rearrange("p t (h n) -> p t h n", h=MLA_H)
                tmp = lambda heads: (lambda n: proj0[:, :, n * P:n * P + heads * 16].rearrange(
                    "p t (h n) -> p t h n", h=heads))
                rotate(q[:, :, :, 64:80], q[:, :, :, 80:96], angles(0, 8), angles(1, 8), tmp(8))
                kr = proj0[:, :, Q_RANK + KV_RANK:SWA_AT].rearrange("p t (h n) -> p t h n", h=1)
                rotate(kr[:, :, :, 0:16], kr[:, :, :, 16:32], angles(0, 1), angles(1, 1), tmp(1))
                dve.tensor_copy(k0[:, :, :, MLA_NOPE:],
                                view(proj0[:, 0, Q_RANK + KV_RANK:SWA_AT], 0, [[AB_W, TT], [0, MLA_H], [1, MLA_ROPE]])
                                ).then_inc(mla_ready, 1)

            mla_positions()
            dve.wait_ge(loaded["masks"], 16)
            gemm("mem_k", None, {n: slots("l0", 7 + n) for n in range(4)})
            gemm("mem_v", None, {0: slots("l0", 11), 1: lambda: [slot("l0", 12), turn("o0a", xt_hi, xt_lo)],
                                 2: slots("l0", 13), 3: slots("l0", 14)})
            wide("ab_out", {0: slots("l0", 15), 1: slots("l0", 16), 2: slots("l0", 17),
                            3: lambda: [slot("l0", 18), turn("o0b", xt_hi, xt_lo, 4)]})
            norm_and_turn(0, "ab_out", "f0")
            up(0)
            down(0)
            norm_and_turn(1, "down0", "x1")

            def forget_abs():
                dve.wait_ge(*read("cd_in", 1))
                f = proj1[:, :, 0:FOX_H]
                bias = view(head_par[:, 1, :], 0, [[0, TT], [1, 8]])
                settle(dve.tensor_tensor(log_f[:, 0, :, :], f, bias, ALU.add))
                dve.scalar_tensor_tensor(log_f[:, 1, :, :], log_f[:, 0, :, :], -1.0, log_f[:, 0, :, :],
                                         ALU.mult, ALU.max).then_inc(f_abs, 1)

            def forget_log():
                dve.wait_ge(f_ln, 1)
                dve.scalar_tensor_tensor(log_f[:, 3, :, :], log_f[:, 0, :, :], 0.0, log_f[:, 1, :, :],
                                         ALU.min, ALU.subtract).then_inc(log_f_ready, 1)

            def copy_cumulated():
                dve.wait_ge(cum_ready, 1)
                dve.tensor_copy(cum_k[0:FOX_H, :], psum[0:FOX_H, O_BANK, 0:S]).then_inc(cum_copied, 1)

            gemm("cd_in", None, {4: forget_abs, 5: forget_log, 7: copy_cumulated,
                                 **{n: slots("l1", s) for n, s in L1_SLOTS.items()},
            24: lambda: turn("o1a", ht_hi, ht_lo)})
            wide("cd_out", {0: slots("l1", 13), 1: slots("l1", 14), 2: slots("l1", 15),
                            3: lambda: [slots("l1", 16, 17, 18)(), turn("o1b", ht_hi, ht_lo, 4)]})
            norm_and_turn(2, "cd_out", "f1")
            up(1)
            down(1)
            def second_gain(t):
                dve.wait_ge(loaded["norm_g"], 16)
                for j in range(2):
                    cut = slice(j * 512, (j + 1) * 512)
                    dve.wait_ge(x_ready, 4 * 3 + 2 * t + j + 1)
                    dve.tensor_tensor(h2[:, t, cut], x[:, t, cut], row_g[:, cut], ALU.mult).then_inc(h2_ready, 1)

            def second_root(t):
                dve.wait_ge(rms_sd, TT * 3 + t + 1)
                dve.reciprocal(rms_st[:, 3, 2, t:t + 1], rms_st[:, 3, 1, t:t + 1]).then_inc(rms_done, 1)

            sum_tile(3, "down1", 0)
            norm_tile(3, 0)
            second_gain(0)
            turn_and_split("x2")
            second_root(0)
            sum_tile(3, "down1", 1)
            norm_tile(3, 1)
            second_gain(1)
            turn("x2", xt_hi, xt_lo, 0, [1])
            second_root(1)

            def moba_positions():
                dve.wait_ge(*read("in_a", 3))
                tmp = lambda n: region(12800, 4 * 96)[:, :, n * 96:(n + 1) * 96].rearrange(
                    "p t (h n) -> p t h n", h=MOBA_H)
                for at in (0, AW):
                    m = a2[:, :, at:at + AW].rearrange("p t (h n) -> p t h n", h=MOBA_H)
                    rotate(m[:, :, :, 0:ROT2], m[:, :, :, ROT2:2 * ROT2], angles(2, MOBA_H), angles(3, MOBA_H), tmp)
                dve.nop().then_inc(moba_ready, 1)

            gemm("in_a", None, {13: moba_positions})

            def gmlp_stats():
                dve.wait_ge(*read("in_b", 3))
                for t in range(TT):
                    for n in range(2):
                        last = statistics(4, t, n, b2[:, t, BW + n * 384:BW + (n + 1) * 384])
                settle(last)
                for t in range(TT):
                    variance(4, t)

            def gmlp_norm():
                dve.wait_ge(loaded["gmlp_g"], 16)
                for t in range(TT):
                    v = b2[:, t, BW:2 * BW]
                    last = dve.tensor_scalar(v, v, deviate(4, t, v, row_g[:, 0:BW]), None, ALU.mult)
                last.then_inc(vn_ready, 1)

            gemm("in_b", None, {**{2 + s: slots("moba", s) for s in range(9)}, 13: gmlp_stats, 15: gmlp_norm})
            gemm("in_b_end")

            def gate_b(groups):
                dve.wait_ge(*read("in_b_end", 1))
                for g in groups:
                    dve.wait_ge(mixed, g + 1)
                    u = b2[:, :, g * P:(g + 1) * P]
                    acc = psum[:, PT_BANK + g % 2, 0:S].rearrange("p (t n) -> p t n", t=TT)
                    settle(dve.scalar_tensor_tensor(u, acc, bsp[:, g:g + 1], u, ALU.add, ALU.mult))
                    dve.tensor_tensor(u, u, b2[:, :, 2 * BW + g * P:2 * BW + (g + 1) * P], ALU.mult
                                      ).then_inc(gated_b, 1)

            gemm("in_c", None, {0: lambda: turn("a", ht_hi, ht_lo, 0, [0]), 1: lambda: turn("a", ht_hi, ht_lo, 0, [1]),
                                **{2 + g: lambda g=g: gate_b([g]) for g in range(6)}})
            gemm("gate_a", None, {s: slots("xa", s) for s in range(7)})

            def branch(n):
                def evacuate(j, t, acc, freed, count):
                    y, s = y2[:, t, j * 512:(j + 1) * 512], sig[:, t, j * 512:(j + 1) * 512]
                    dve.tensor_tensor(s if n else y, acc, s, ALU.mult).then_inc(freed, 1)
                    if n:
                        dve.wait_ge(freed, count)
                        dve.tensor_tensor(y, y, s, ALU.add).then_inc(y_ready, 1)
                return evacuate

            dve.wait_ge(*read("gate_a", 2))
            gemm("branch_a", branch(0), {0: lambda: turn("b", ht_hi, ht_lo, 6, [0]),
                                         1: lambda: turn("b", ht_hi, ht_lo, 6, [1]),
                                         2: lambda: turn("c", ht_hi, ht_lo, 12)})
            gemm("gate_b")
            dve.wait_ge(*read("gate_b", 2))
            gemm("branch_b", branch(1))
            gemm("gate_c")
            dve.wait_ge(*read("gate_c", 2))
            wide("branch_c")
            end = done["chunks"]
            summed("branch_c", 0, 5)
            halves("branch_c", 0, branch(2))
            split_to(end + LEAD)
            turn("y", xt_hi, xt_lo, 0, [0])
            summed("branch_c", 1, 5)
            halves("branch_c", 1, branch(2))
            split_to(end + NS)
            turn("y", xt_hi, xt_lo, 0, [1])
            wide("out")

            def last_residual(j, t, acc, freed, count):
                part = x[:, t, j * 512:(j + 1) * 512]
                dve.tensor_tensor(part, part, acc, ALU.add).then_inc(x_ready, 1)

            dve.wait_ge(loaded["final_g"], 16)
            for t in range(TT):
                summed("out", t, 6)
                halves("out", t, last_residual)
                rms(4, lambda t: x[:, t, :], a2_out, row_g[:, :], [t])


def chunks_of(w, name):
    g = GEMMS[name]
    w = w.reshape(g.kc // g.kp, g.kp, P, g.steps, g.n).transpose(3, 0, 2, 1, 4)
    return np.ascontiguousarray(w.reshape(-1, P, g.kp * g.n))


def shape_constants():
    q, k = np.arange(S)[:, None], np.arange(S)[None, :]
    by_chunk = np.where(k // CH <= q // CH, 0.0, MASKED)
    causal = np.where(k <= q, 0.0, MASKED)
    window = np.where((k // CH <= q // CH) & (k // CH >= q // CH - 2), 0.0, MASKED)

    def tiles(m):
        return np.concatenate([m[0:P, 0:P], m[P:S, :]], 1)

    slopes = np.exp2(-8.0 * np.arange(1, SWA_H + 1) / SWA_H)
    swa = np.stack([tiles(np.where(window < 0, MASKED, -s * np.abs(q - k) * HD ** 0.5)) for s in slopes], 1)

    def angles(theta, width):
        inv = np.float32(theta) ** (-np.arange(0, width, 2, dtype=np.float32) / np.float32(width))
        a = (np.arange(S, dtype=np.float32)[:, None] * inv[None, :].astype(np.float32)).astype(np.float64)
        return [f(a).reshape(TT, P, width // 2).transpose(1, 0, 2) for f in (np.cos, np.sin)]

    c = {"ident": np.eye(P), "masks": np.stack([tiles(by_chunk), tiles(causal)], 1), "swa": swa,
         "rope": np.stack(angles(10000.0, MLA_ROPE) + angles(500000.0, 2 * ROT2), 1),
         "cum": np.where(q <= k, -HD ** 0.5, 0.0).reshape(TT, P, S).transpose(1, 0, 2),
         "sel": np.repeat(np.eye(FOX_H), P, 1)}
    return {n: np.ascontiguousarray(a, dtype=np.float32) for n, a in c.items()}


def kernel(**inputs):
    import concourse.bacc as bacc
    from concourse.bass_utils import run_bass_kernel_spmd

    a = {k: np.asarray(v) for k, v in inputs.items()}
    w2 = a["w_in_2"][0]
    cut = np.cumsum([0, 4 * AW, 3 * BW, 2 * CW, D, D, D])
    in_a, in_b, in_c, gate_a, gate_b, gate_c = (w2[:, cut[n]:cut[n + 1]] for n in range(6))

    ab = a["ab_w_in"][0]
    low = Q_RANK + KV_RANK + MLA_ROPE
    q, k, v = (ab[:, low + m:low + n].reshape(D, SWA_KV, -1) for m, n in ((0, 512), (512, 640), (640, 768)))
    ab = np.concatenate([ab[:, :low], np.concatenate([k, v, q], 2).reshape(D, -1)], 1)
    cd = a["cd_w_in"][0]
    n = FOX_H * HD

    def by_head(w):
        return w.reshape(D, 3, 8, HD).transpose(0, 2, 1, 3).reshape(D, 3 * 8 * HD)

    cd = np.concatenate([cd[:, 3 * n:3 * n + FOX_H], by_head(cd[:, :3 * n]), by_head(cd[:, 3 * n + FOX_H:])], 1)

    def up_of(layer):
        g, u = (a[n][layer].reshape(D, FF // 256, 256) for n in ("ffn_w_gate", "ffn_w_up"))
        return np.stack([g, u], 2).reshape(D, 2 * FF)

    weights = {"ab_in": ab, "mem_k": a["w_mem_kv_2"][0][:, :CW], "uq": a["ab_w_uq"][0],
               "ukv": a["ab_w_ukv"][0], "mem_v": a["w_mem_kv_2"][0][:, CW:], "ab_out": np.roll(a["ab_w_out"][0], SWA_H * HD, 0),
               "up0": up_of(0), "down0": a["ffn_w_down"][0], "cd_in": cd, "cd_out": a["cd_w_out"][0],
               "up1": up_of(1), "down1": a["ffn_w_down"][1], "in_a": in_a, "in_b": in_b[:, :2048],
               "in_b_end": in_b[:, 2048:], "in_c": in_c, "gate_a": gate_a, "branch_a": a["w_branch_a_2"][0],
               "gate_b": gate_b, "branch_b": a["w_branch_b_2"][0], "gate_c": gate_c,
               "branch_c": a["w_branch_c_2"][0], "out": a["w_out_2"][0]}
    arrays = {"w_" + n: chunks_of(w, n) for n, w in weights.items()}
    rel = np.zeros((CK_H, REL_PITCH), np.float32)
    rel[:, CH:] = a["cd_rel_bias"][0].T
    arrays.update(
        x=a["x"][0], mem=a["mem_2"][0], mem_norm_g=a["mem_norm_g_2"][0], norm_g=a["norm_g_2"][0],
        final_g=a["final_norm_g_2"], gmlp_g=a["gmlp_ln_g_2"][0],
        gains=np.concatenate([a["ab_q_norm"][0], a["ab_kv_norm"][0]]),
        head_par=np.concatenate([a["ab_sinks"][0], a["cd_b_forget"][0]]),
        ln=np.stack([np.stack([a[f"{n}_g"][k], a[f"{n}_b"][k]]) for k in range(2) for n in ("ln1", "ln2")]),
        wsp=a["w_spatial_2"][0].transpose(2, 0, 1), bsp=a["b_spatial_2"][0].T, rel=rel, **shape_constants())
    arrays = {n: np.ascontiguousarray(m) for n, m in arrays.items()}

    nc = bacc.Bacc("TRN2", target_bir_lowering=False, num_devices=1)
    d = {n: nc.dram_tensor(f"in_{n}", m.shape, mybir.dt.from_np(m.dtype), kind="ExternalInput").ap()
         for n, m in arrays.items()}
    out = nc.dram_tensor("out_x", (S, D), F32, kind="ExternalOutput").ap()
    build_program(nc, d, out)
    r = run_bass_kernel_spmd(nc, [{f"in_{n}": m for n, m in arrays.items()}], core_ids=[0])
    return r.results[0]["out_x"].reshape(1, S, D)
```

```python
from collections import namedtuple
from contextlib import ExitStack

import numpy as np
import concourse.bass as bass
from concourse import mybir

F32 = mybir.dt.float32
F32R = mybir.dt.float32r
ACT = mybir.ActivationFunctionType
ALU = mybir.AluOpType

P = 128
TT = 2
S = TT * P
D = 1024
CH = 64
MASKED = -1e30
HALF_D = D // 2

MLA_H, MLA_NOPE, MLA_ROPE, MLA_V = 8, 64, 32, 64
MLA_D = MLA_NOPE + MLA_ROPE
Q_RANK, KV_RANK = 384, 256
SWA_H, SWA_KV, HD = 8, 2, 64
FOX_H = CK_H = 8
AB_W = Q_RANK + KV_RANK + MLA_ROPE + SWA_H * HD + 2 * SWA_KV * HD
CD_W = 3 * FOX_H * HD + FOX_H + 3 * CK_H * HD
FF = 2816
ALPHA = 4 ** 0.25
LN_EPS, RMS_EPS = 1e-5, 1e-6
REL, REL_PITCH = 320, 384
MOBA_H, XA_H, HD2 = 6, 4, 128
AW, BW, CW = MOBA_H * HD2, 6 * 128, XA_H * HD2
ROT2 = 16

NS = 4
SLOT = 1024
LEAD = NS - 1

Gemm = namedtuple("Gemm", "name kc kp n steps c0 u0")


def plan_gemms():
    table = [("ab_in", 8, 2, 480, 3), ("uq", 3, 3, 256, 3), ("ukv", 2, 2, 512, 2), ("mem_k", 8, 2, 512, 1),
             ("mem_v", 8, 2, 512, 1), ("ab_out", 8, 1, 1024, 1), ("up0", 8, 2, 512, 11), ("down0", 22, 1, 1024, 1),
             ("cd_in", 8, 2, 440, 7), ("cd_out", 8, 1, 1024, 1), ("up1", 8, 2, 512, 11), ("down1", 22, 1, 1024, 1),
             ("in_a", 8, 2, 512, 6), ("in_b", 8, 2, 512, 4), ("in_b_end", 8, 4, 256, 1), ("in_c", 8, 2, 512, 2),
             ("gate_a", 8, 2, 512, 2), ("branch_a", 6, 2, 512, 2), ("gate_b", 8, 2, 512, 2),
             ("branch_b", 6, 2, 512, 2), ("gate_c", 8, 2, 512, 2), ("branch_c", 4, 1, 1024, 1),
             ("out", 8, 1, 1024, 1)]
    plan, c, u = {}, 0, 0
    for name, kc, kp, n, steps in table:
        plan[name] = Gemm(name, kc, kp, n, steps, c, u)
        c += steps * kc // kp
        u += steps * (2 if n > 512 else 1)
    return plan, c


GEMMS, CHUNKS = plan_gemms()
WIDE = [g.name for g in GEMMS.values() if g.n == D]
WIDTH = [g.kp * g.n for g in GEMMS.values() for _ in range(g.steps * g.kc // g.kp)]


def plan_turns():
    table = [("x0", 8), ("mem", 8), ("cq", 3), ("ckv", 2), ("o0a", 4), ("o0b", 4), ("f0", 8), ("h0", 22), ("x1", 8),
             ("o1a", 4), ("o1b", 4), ("f1", 8), ("h1", 22), ("x2", 8), ("a", 6), ("b", 6), ("c", 4), ("y", 8)]
    plan, at = {}, 0
    for name, kc in table:
        plan[name] = (kc, at)
        at += kc // 2 if name[0] == "h" else TT * -(-kc // 4)
    return plan


TURNS = plan_turns()


def turned_at(names, t, k):
    if isinstance(names, tuple):
        return turned_at(names[k // 4], t, k % 4)
    name = names
    kc, g0 = TURNS[name]
    return g0 + 1 + (k // 2 if name[0] == "h" else t * -(-kc // 4) + k // 4)


AFTER_NORM = ("up0", "cd_in", "up1", "in_a")
POOL_CHUNKS = {GEMMS[name].c0 + 2 + m: 2 * n + m + 1 for n, name in enumerate(AFTER_NORM) for m in range(2)}

STREAMS = {"l0": (0, 16), "l1": (16, 32), "moba": (32, 38), "xa": (38, 42)}

L1_SLOTS = {8: 0, 9: 1, 10: 2, 11: 3, 13: 4, 14: 5, 17: 6, 18: 7, 20: 8, 21: 9, 22: 10, 25: 11, 26: 12, 27: 13}


def paired(h):
    return h < 8 or 16 <= h < 32


def turns_of(h):
    return sum(1 for m in range(h + 1) if not (paired(m) and m % 2))


def qk_buffer(h):
    return (h // 2 if paired(h) else h) % 2


def last_user(h):
    first = h - h % 2 if paired(h) else h
    return max([m for m in range(first) if qk_buffer(m) == qk_buffer(h)], default=-1)


MEM_K, MEM_V, TAB = 0, 1024, 2048
PROJ0, Q0, K0, V0, O0 = 5120, 8000, 9536, 11072, 12096
PROJ1, O1, CUM = 5120, 11280, 13328
A2, B2 = 2048, 8192
ARENA = 14144


def view(base, offset, dims):
    return bass.AP(tensor=base.tensor, offset=base.offset + offset, ap=[base.ap[0]] + [list(d) for d in dims])


def plus(value, i, per_turn):
    return value if i is None else value + i * per_turn


def build_program(nc, d, out):
    with ExitStack() as ctx:
        def sb(name, shape, dt=F32):
            return ctx.enter_context(nc.sbuf_tensor(name, shape, dt))

        def sem(name):
            return ctx.enter_context(nc.semaphore(name))

        stage = sb("stage", [P, NS, SLOT])
        w_hi = sb("w_hi", [P, NS, SLOT], F32R)
        w_lo = sb("w_lo", [P, NS, SLOT], F32R)
        xt_hi = sb("xt_hi", [P, 8, S], F32R)
        xt_lo = sb("xt_lo", [P, 8, S], F32R)
        ht_hi = sb("ht_hi", [P, 22, S], F32R)
        ht_lo = sb("ht_lo", [P, 22, S], F32R)
        x = sb("x", [P, TT, D])
        arena = sb("arena", [P, ARENA])
        ident = sb("ident", [P, P])
        masks = sb("masks", [P, 2, 384])
        no_mask = sb("no_mask", [P, 256])
        qk_t = sb("qk_t", [P, 2, 512])
        probs = sb("probs", [P, 2, 512])
        probs_t = sb("probs_t", [P, 2, 512])
        ln_par = sb("ln_par", [P, 2, D])
        row_g = sb("row_g", [P, D])
        rope = sb("rope", [P, 4, TT, 16])
        head_par = sb("head_par", [P, 2, 8])
        wsp = sb("wsp", [P, 6, P])
        bsp = sb("bsp", [P, 6])
        norm_g = sb("norm_g", [P, 8])
        cum_k = sb("cum_k", [P, S])
        log_f = sb("log_f", [P, 4, TT, 8])
        eps = sb("eps", [P, 2])
        rms_st = sb("rms_st", [P, 5, 3, 2])
        ln_st = sb("ln_st", [P, 5, 32])
        soft = sb("soft", [P, 4, 5, 2])
        psum = ctx.enter_context(nc.psum_tensor("psum", [P, 8, 512], F32))
        TURN_BANKS = {"cq": (2, 3), "ckv": (2, 3), "o0a": (0, 1), "o1a": (0, 1)}
        QK_BANK, LOGIT_BANK, PT_BANK, O_BANK = 4, 5, 6, 7

        def turn_bank(name, g):
            return psum[:, TURN_BANKS.get(name, (4, 5))[g % 2], :]

        def turn_parts(name, tiles):
            kc, g0 = TURNS[name]
            per = -(-kc // 4)
            return [(g0 + t * per + q, t, 4 * q, min(4, kc - 4 * q)) for t in tiles for q in range(per)]

        staged = [sem(f"staged{s}") for s in range(NS)]
        hi_done, lo_done = sem("hi_done"), sem("lo_done")
        pool_lo = sem("pool_lo")
        chunk_used = sem("chunk_used")
        half_done = sem("half_done")
        acc_free = [sem("acc_free0"), sem("acc_free1")]
        turned, turn_hi, turn_lo = sem("turned"), sem("turn_hi"), sem("turn_lo")
        qk_turned, qk_copied = sem("qk_turned"), sem("qk_copied")
        logits_ready, max_ready, exp_ready = sem("logits_ready"), sem("max_ready"), sem("exp_ready")
        p_turned, p_copied = sem("p_turned"), sem("p_copied")
        pv_ready, head_done = sem("pv_ready"), sem("head_done")
        silu_ready = sem("silu_ready")
        ln_var, ln_sd, x_ready = sem("ln_var"), sem("ln_sd"), sem("x_ready")
        rms_sd, rms_done = sem("rms_sd"), sem("rms_done")
        act_step, dve_step, pool_step = sem("act_step"), sem("dve_step"), sem("pool_step")
        constants_set = sem("constants_set")
        mla_ready, moba_ready = sem("mla_ready"), sem("moba_ready")
        f_abs, f_ln, log_f_ready, cum_ready, cum_copied = (sem("f_abs"), sem("f_ln"), sem("log_f_ready"),
                                                           sem("cum_ready"), sem("cum_copied"))
        rel_ready, wsp_ready = sem("rel_ready"), sem("wsp_ready")
        key_twice = sem("key_twice")
        vn_ready, mixed, gated_b = sem("vn_ready"), sem("mixed"), sem("gated_b")
        y_ready, stored, final_sum = sem("y_ready"), sem("stored"), sem("final_sum")
        loads = ["x0", "x1", "ident", "mem_g", "mem", "gains", "rope", "swa", "masks", "heads", "ln0", "ln1", "ln2",
                 "ln3",
                 "rel", "cum", "sel", "norm_g", "gmlp_g", "final_g", "wsp", "bsp"]
        loaded = {n: sem(f"loaded_{n}") for n in loads}

        def cols(at, width):
            return arena[:, at:at + width]

        def region(at, width):
            return arena[:, at:at + TT * width].rearrange("p (t n) -> p t n", t=TT)

        mem_x, o0 = region(O0, D), region(O0, D)
        mem_k, mem_v = region(MEM_K, CW), region(MEM_V, CW)
        proj0, q0, proj1, o1 = region(PROJ0, AB_W), region(Q0, MLA_H * MLA_D), region(PROJ1, CD_W), region(O1, D)
        k0 = arena[:, K0:K0 + TT * MLA_H * MLA_D].rearrange("p (t h n) -> p t h n", t=TT, h=MLA_H)
        v0 = arena[:, V0:V0 + TT * MLA_H * MLA_V].rearrange("p (t h n) -> p t h n", t=TT, h=MLA_H)
        gains = cols(V0, Q_RANK + KV_RANK)
        table = arena[:, TAB:TAB + 8 * 384].rearrange("p (h n) -> p h n", h=8)
        rel_raw = arena[:, PROJ0:PROJ0 + 8 * 384].rearrange("p (h n) -> p h n", h=8)
        cum_tri = region(CUM, S)
        twice_k = row_g[:, 0:TT * SWA_KV * 2 * HD].rearrange("p (t g n) -> p t g n", t=TT, g=SWA_KV)
        a2 = region(A2, 4 * AW)
        b2 = region(B2, 3 * BW)
        c2 = region(A2 + 6144 - 2 * 2 * CW, 2 * CW)
        a2_out = lambda t: a2[:, t, 0:D]
        y2 = region(A2 + 2 * D, D)
        sig = ln_par
        u_tile = qk_t[:, :, :].rearrange("p b (t n) -> p b t n", t=TT)
        h_tile = probs[:, :, :].rearrange("p b (t n) -> p b t n", t=TT)

        SWA_AT = Q_RANK + KV_RANK + MLA_ROPE
        SWA_GROUP = (2 + SWA_H // SWA_KV) * HD
        FOX_AT = FOX_H
        CK_AT = FOX_AT + 3 * FOX_H * HD

        def pair_columns(h):
            return [h // 2 * 6 * HD + (2 * n + h % 2) * HD for n in range(3)]

        Head = namedtuple("Head", "dim scale q k v mask full out gate sink fox")

        def head_of(h):
            cut = lambda m, at, w: (lambda t: m[:, t, at:at + w])
            if h < 8:
                at = SWA_AT + h // 4 * SWA_GROUP
                return Head(HD, HD ** -0.5, cut(proj0, at + (2 + h % 4) * HD, HD), cut(proj0, at, HD),
                            cut(proj0, at + HD, HD), table[:, h, :], False,
                            cut(o0, h * HD, HD), None, h, None)
            if h < 16:
                h -= 8
                return Head(MLA_D, MLA_D ** -0.5, cut(q0, h * MLA_D, MLA_D), lambda t: k0[:, t, h, :],
                            lambda t: v0[:, t, h, :], masks[:, 0, :], False, cut(o0, SWA_H * HD + h * MLA_V, MLA_V),
                            None, None, None)
            if h < 24:
                h -= 16
                q, k, v = (cut(proj1, FOX_AT + at, HD) for at in pair_columns(h))
                return Head(HD, HD ** -0.5, q, k, v, masks[:, 1, :], False, cut(o1, h * HD, HD), None, None, h)
            if h < 32:
                h -= 24
                q, k, v = (cut(proj1, CK_AT + at, HD) for at in pair_columns(h))
                return Head(HD, HD ** -0.5, q, k, v, table[:, h, :], False,
                            cut(o1, (FOX_H + h) * HD, HD), None, None, None)
            if h < 38:
                h -= 32
                return Head(HD2, HD2 ** -0.5, cut(a2, h * HD2, HD2), cut(a2, AW + h * HD2, HD2),
                            cut(a2, 2 * AW + h * HD2, HD2), masks[:, 1, :], False, cut(a2, h * HD2, HD2),
                            cut(a2, 3 * AW + h * HD2, HD2), None, None)
            h -= 38
            return Head(HD2, HD2 ** -0.5, cut(c2, h * HD2, HD2), cut(mem_k, h * HD2, HD2), cut(mem_v, h * HD2, HD2),
                        None, True, cut(c2, h * HD2, HD2), cut(c2, CW + h * HD2, HD2), None, None)

        def to_turn(h):
            hd = head_of(h)
            if not paired(h):
                return [hd.q(0), hd.q(1), hd.k(0), hd.k(1)]
            both = lambda m: view(m, 0, [[1, 2 * HD]])
            keys = [twice_k[:, t, h // 4, :] if h < 8 else both(hd.k(t)) for t in range(TT)]
            return [both(hd.q(t)) for t in range(TT)] + keys

        def keys0(hd):
            return S if hd.full else P

        def read(name, steps):
            u = GEMMS[name].u0 + steps - 1
            return acc_free[u % 2], TT * (u // 2 + 1)

        def chunk_lo(c):
            return (pool_lo, POOL_CHUNKS[c]) if c in POOL_CHUNKS else (lo_done, c + 1)

        block = ctx.enter_context(nc.Block())

        @block.sync
        def _(sp):

            def load_x(t):
                sp.dma_start(x[:, t, :], d["x"][t * P:(t + 1) * P, :]).then_inc(loaded[f"x{t}"], 16)

            load_x(0)
            sp.dma_start(ident[:, :], d["ident"]).then_inc(loaded["ident"], 16)

            def load_chunk(g, n, i=None):
                c = g.c0 + n
                s, w = c % NS, WIDTH[c]
                if c >= NS or i is not None:
                    sp.wait_ge(lo_done, plus(c - NS + 1, i, NS))
                src = d["w_" + g.name]
                src = src[n] if i is None else src[bass.ds(i * NS + n, 1), :, :].rearrange("a p n -> (a p) n")
                sp.dma_start(stage[:, s, 0:w], src).then_inc(staged[s], 16)

            for g in GEMMS.values():
                chunks = g.steps * g.kc // g.kp
                n = 0
                while g.c0 + n < NS and n < chunks:
                    load_chunk(g, n)
                    n += 1
                    if g.c0 + n == 2:
                        load_x(1)
                turns = (chunks - n) // NS
                if turns >= 2:
                    with sp.Fori(0, turns) as i:
                        for m in range(NS):
                            load_chunk(g, n + m, i)
                    n += turns * NS
                for m in range(n, chunks):
                    load_chunk(g, m)
            for t in range(TT):
                for j in range(2):
                    cut = slice(j * 512, (j + 1) * 512)
                    sp.wait_ge(rms_done, 9 + 2 * t + j)
                    sp.dma_start(out[t * P:(t + 1) * P, cut], a2_out(t)[:, cut]).then_inc(stored, 16)
            sp.wait_ge(stored, 16 * 2 * TT)

        @block.gpsimd
        def _(pool):
            def load(name, dst, src):
                pool.dma_start(dst, src).then_inc(loaded[name], 16)

            def row(src, n):
                return bass.AP(tensor=src.tensor, offset=src.offset, ap=[[0, P], [1, n]])

            pool.memset(no_mask[:, :], 0.0).then_inc(constants_set, 1)
            pool.wait_ge(hi_done, 2)
            load("mem_g", row_g[:, :], row(d["mem_norm_g"], D))
            load("mem", mem_x, d["mem"].rearrange("(t p) n -> p t n", t=TT))
            load("gains", gains, row(d["gains"], Q_RANK + KV_RANK))
            load("heads", head_par[:, :, :].rearrange("p a h -> p (a h)"), row(d["head_par"], 16))
            pool.wait_ge(hi_done, 2 * NS)
            load("swa", table, d["swa"])
            load("rope", rope[:, :, :, :], d["rope"])
            pool.wait_ge(hi_done, 3 * NS)
            load("masks", masks[:, :, :], d["masks"])
            load("ln0", ln_par[:, :, :].rearrange("p a n -> p (a n)"),
                 bass.AP(tensor=d["ln"].tensor, offset=0, ap=[[0, P], [1, 2 * D]]))
            load("bsp", bsp[:, :], d["bsp"])
            load("norm_g", norm_g[:, :], d["norm_g"])
            load("wsp", wsp[:, :, :], d["wsp"])
            pool.wait_ge(loaded["wsp"], 16)
            pool.affine_select(out=wsp[:, :, :], in_=wsp[:, :, :], compare_op=ALU.is_ge, fill=0.0, base=0,
                               pattern=[[0, 6], [1, P]], channel_multiplier=-1).then_inc(wsp_ready, 1)
            pool.wait_ge(qk_turned, SWA_H // 2)
            load("sel", row_g[0:8, :], d["sel"])

            def split_two(name):
                for c in (GEMMS[name].c0 + 2, GEMMS[name].c0 + 3):
                    s, w = c % NS, WIDTH[c]
                    pool.wait_ge(hi_done, c + 1)
                    pool.tensor_tensor(w_lo[:, s, 0:w], stage[:, s, 0:w], w_hi[:, s, 0:w].bitcast(F32), ALU.subtract
                                       ).then_inc(pool_lo, 1)

            split_two(AFTER_NORM[0])
            pool.wait_ge(head_done, STREAMS["l0"][1])
            rel = d["rel"]
            for at, keys in ((0, P), (P, S)):
                load("rel", rel_raw[:, :, at:at + keys],
                     bass.AP(tensor=rel.tensor, offset=0, ap=[[1, P], [REL_PITCH, CK_H], [1, keys]]))
            pool.wait_ge(loaded["rel"], 32)
            for at, keys in ((0, P), (P, S)):
                last = pool.tensor_scalar(table[:, :, at:at + keys],
                                          view(rel_raw[:, 0, 0:1], at + keys - 1, [[384, CK_H], [-1, keys]]),
                                          HD ** 0.5, None, ALU.mult)
            last.then_inc(pool_step, 1)
            pool.wait_ge(pool_step, 1)
            pool.memset(table[0:CH, :, CH:P], MASKED).then_inc(rel_ready, 1)
            pool.memset(table[0:CH, :, P + S - CH:P + S], MASKED).then_inc(rel_ready, 1)
            load("cum", cum_tri, d["cum"])
            for k in range(1, 4):
                pool.wait_ge(x_ready, 2 * TT * k)
                load(f"ln{k}", ln_par[:, :, :].rearrange("p a n -> p (a n)"),
                     bass.AP(tensor=d["ln"].tensor, offset=2 * D * k, ap=[[0, P], [1, 2 * D]]))
                split_two(AFTER_NORM[k])
            pool.wait_ge(logits_ready, STREAMS["l1"][1])
            load("gmlp_g", row_g[:, 0:BW], row(d["gmlp_g"], BW))
            pool.wait_ge(vn_ready, 1)
            load("final_g", row_g[:, :], row(d["final_g"], D))

        @block.tensor
        def _(pe):
            def turn(name, src, ready, tiles=range(TT)):
                for part in turn_parts(name, tiles):
                    turn_part(part, name, src, ready)

            def turn_tile(name, src, t, ready, count):
                for q, part in enumerate(turn_parts(name, [t])):
                    turn_part(part, name, tile_of(src), [(ready, count + q)])

            def turn_part(part, name, src, ready):
                g, t, k0, w = part
                for s, v in ready:
                    pe.wait_ge(s, v)
                if g >= 2:
                    pe.wait_ge(turn_lo, g - 1)
                for k in range(w):
                    last = pe.transpose(turn_bank(name, g)[:, k * P:(k + 1) * P], src(k0 + k, t), ident[:, :])
                last.then_inc(turned, 1)

            def step(g, j, hi, lo, k0=0, turned_by=None, between=None, i=None, per_turn=0, second=None):
                u, cps = g.u0 + j, g.kc // g.kp
                pair = u % 2
                passes = [(t,) for t in range(TT)] if second else [tuple(range(TT))]
                for tiles in passes:
                    if second:
                        second(tiles[0])
                    if u >= 2 or i is not None:
                        pe.wait_ge(acc_free[pair], plus(2 * (u // 2) - (tiles == (0,)), i, per_turn))
                    for m in range(cps):
                        n = j * cps + m
                        c = g.c0 + n
                        s = c % NS
                        if i is not None:
                            pe.wait_ge(lo_done, plus(c + 1, i, per_turn * cps))
                        for kk in range(g.kp):
                            k = m * g.kp + kk
                            wh, wl = w_hi[:, s, kk * g.n:(kk + 1) * g.n], w_lo[:, s, kk * g.n:(kk + 1) * g.n]
                            for t in tiles:
                                turn_of = turned_by is not None and j == 0 and turned_at(turned_by, t, k)
                                acc = psum[:, 2 * pair + t, 0:g.n]
                                ah, al = hi[:, k0 + k, t * P:(t + 1) * P], lo[:, k0 + k, t * P:(t + 1) * P]
                                if i is None:
                                    pe.wait_ge(hi_done, c + 1)
                                if turn_of:
                                    pe.wait_ge(turn_hi, turn_of)
                                pe.matmul(acc, ah, wh, start=(k == 0), stop=False)
                                if i is None:
                                    pe.wait_ge(*chunk_lo(c))
                                pe.matmul(acc, ah, wl, start=False, stop=False)
                                if turn_of:
                                    pe.wait_ge(turn_lo, turn_of)
                                last = pe.matmul(acc, al, wh, start=False, stop=(k == g.kc - 1))
                        if tiles[-1] == 1:
                            last.then_inc(chunk_used, 1)
                            if between and n in between:
                                between[n]()

            def gemm(name, hi, lo, k0=0, turned_by=None, between=None, second=None):
                g = GEMMS[name]
                for j in range(g.steps):
                    step(g, j, hi, lo, k0, turned_by, between, second=second if j == 0 else None)

            def wide(name, hi, lo, turned_by, k0=0, between=None, head=0, second=None):
                g = GEMMS[name]
                apart = not head and g.kc > NS
                if second is None:
                    pe.wait_ge(acc_free[g.u0 % 2], 2 * (g.u0 // 2))
                if isinstance(turned_by, tuple):
                    pe.wait_ge(turn_lo, turned_at(turned_by, 1, 0))
                spans = [(0, head)] if head else []
                spans += [(k, k + 1) for k in range(head, g.kc - NS)]
                if g.kc - NS >= head:
                    spans.append((g.kc - NS, g.kc))

                def products(k, t, halves):
                    c = g.c0 + k
                    s = c % NS
                    turn_of = turned_at(turned_by, t, k)
                    ah, al = hi[:, k0 + k, t * P:(t + 1) * P], lo[:, k0 + k, t * P:(t + 1) * P]
                    for a, w in ((ah, w_hi), (ah, w_lo), (al, w_hi)):
                        if w is w_lo:
                            pe.wait_ge(lo_done, c + 1)
                        elif a is ah:
                            pe.wait_ge(hi_done, c + 1)
                            pe.wait_ge(turn_hi, turn_of)
                        else:
                            pe.wait_ge(turn_lo, turn_of)
                        for half in halves:
                            summed = k == g.kc - 1 and a is al
                            last = pe.matmul(psum[:, 2 * ((g.u0 + half) % 2) + t, :], a,
                                             w[:, s, half * 512:(half + 1) * 512],
                                             start=(k == 0 and w is w_hi and a is ah), stop=summed)
                            if summed and (t, half) != (1, 1):
                                last.then_inc(half_done, 1)
                    return last

                for first, end in spans:
                    if first == 0 and apart:
                        products(0, 0, [0])
                        products(0, 1, [0])
                        u = g.u0 + 1
                        pe.wait_ge(acc_free[u % 2], 2 * (u // 2))
                        products(0, 0, [1])
                        products(0, 1, [1]).then_inc(chunk_used, 1)
                        if between and 0 in between:
                            between[0]()
                        continue
                    for t in range(TT):
                        if t == 0 and first == 0 and not head:
                            products(0, 0, [0])
                            u = g.u0 + 1
                            pe.wait_ge(acc_free[u % 2], 2 * (u // 2))
                            products(0, 0, [1])
                            for k in range(1, end):
                                products(k, 0, range(2))
                            continue
                        if first == 0 and second is not None:
                            second(t)
                            for half in range(2):
                                u = g.u0 + half
                                pe.wait_ge(acc_free[u % 2], 2 * (u // 2) - 1 + t)
                        apart_at_end = t == 1 and g.c0 + end == CHUNKS
                        for halves in ([0], [1]) if apart_at_end else ([0, 1],):
                            for k in range(first, end):
                                last = products(k, t, halves)
                                if t == 1 and halves[-1] == 1:
                                    last.then_inc(chunk_used, 1)
                                    if between and k in between:
                                        between[k]()

            def up(layer, second):
                g, name = GEMMS[f"up{layer}"], f"h{layer}"
                g0 = TURNS[name][1]

                def turn_step(j, i=None):
                    u = g.u0 + j
                    pe.wait_ge(acc_free[u % 2], plus(2 * (u // 2 + 1), i, 2))
                    pe.wait_ge(turn_lo, plus(g0 + j - 1, i, 2))
                    for k in range(2):
                        for t in range(TT):
                            last = pe.transpose(turn_bank(name, g0 + j)[:, (k * TT + t) * P:(k * TT + t + 1) * P],
                                                h_tile[:, j % 2, t, k * P:(k + 1) * P], ident[:, :])
                    last.then_inc(turned, 1)

                cps = g.kc // g.kp

                def one(j, i=None):
                    between = {j * cps + 1: lambda: turn_step(j - 1, i)} if j else None
                    step(g, j, xt_hi, xt_lo, 0, f"f{layer}", between, i, 2, None if j else second)

                one(0)
                with pe.Fori(0, 4) as i:
                    for s in range(2):
                        one(1 + s, i)
                one(9)
                one(10)
                return lambda: turn_step(10)

            def slot(stream, s):
                lo_h, hi_h = STREAMS[stream]
                h = lo_h + s
                if lo_h <= h < hi_h and not (paired(h) and h % 2):
                    if h == 8:
                        pe.wait_ge(mla_ready, 1)
                        pe.wait_ge(*read("ukv", 2))
                    if 16 <= h < 32:
                        pe.wait_ge(*read("cd_in", -(-(FOX_AT + pair_columns(h - 16)[2]) // GEMMS["cd_in"].n)))
                    if h == 0 or h == 2:
                        pe.wait_ge(*read("ab_in", 2 if h == 0 else 3))
                    if h >= 1:
                        pe.wait_ge(qk_copied, turns_of(h) - 1)
                    if h < 8:
                        pe.wait_ge(key_twice, h // 4 + 1)
                    for n, src in enumerate(to_turn(h)):
                        last = pe.transpose(psum[0:src.shape[-1], QK_BANK, n * P:(n + 1) * P], src, ident[:, :])
                    last.then_inc(qk_turned, 1)
                h = lo_h + s - 3
                if lo_h <= h < hi_h:
                    hd = head_of(h)
                    pe.wait_ge(p_copied, h + 1)
                    if h >= 1:
                        pe.wait_ge(head_done, h)
                    if 16 <= h < 32:
                        pe.wait_ge(*read("cd_in", -(-(FOX_AT + pair_columns(h - 16)[2] + HD) // GEMMS["cd_in"].n)))
                    dv = hd.v(0).shape[-1]
                    for t in range(TT):
                        kts = range(TT) if hd.full or t else range(1)
                        for kt in kts:
                            n = (kt * TT + t) if hd.full else (t + kt)
                            last = pe.matmul(psum[:, O_BANK, t * dv:(t + 1) * dv],
                                             probs_t[:, h % 2, n * P:(n + 1) * P], hd.v(kt),
                                             start=(kt == 0), stop=(kt == kts[-1]))
                    last.then_inc(pv_ready, 1)
                h = lo_h + s - 2
                if lo_h <= h < hi_h:
                    hd = head_of(h)
                    pe.wait_ge(exp_ready, h + 1)
                    if h >= 1:
                        pe.wait_ge(p_copied, h)
                    n0 = keys0(hd)
                    pairs = ([(0, 0), (0, 1), (1, 0), (1, 1)] if hd.full else [(0, 0), (0, 1), (1, 1)])
                    for n, (kt, t) in enumerate(pairs):
                        at = t * n0 + kt * P
                        last = pe.transpose(psum[:, PT_BANK, n * P:(n + 1) * P], probs[:, h % 2, at:at + P],
                                            ident[:, :])
                    last.then_inc(p_turned, 1)
                h = lo_h + s - 1
                if lo_h <= h < hi_h:
                    hd = head_of(h)
                    pe.wait_ge(qk_copied, turns_of(h))
                    if h >= 1:
                        pe.wait_ge(max_ready, h)
                    n0 = keys0(hd)
                    for t in range(TT):
                        nk = S if t else n0
                        acc = psum[:, LOGIT_BANK, t * n0:t * n0 + nk]
                        p0, b = (h % 2 * HD if paired(h) else 0), qk_buffer(h)
                        last = pe.matmul(acc, qk_t[p0:p0 + hd.dim, b, t * P:(t + 1) * P],
                                         qk_t[p0:p0 + hd.dim, b, S:S + nk], start=True, stop=hd.fox is None)
                        if hd.fox is not None:
                            if h == STREAMS["l1"][0] and t == 0:
                                pe.wait_ge(cum_copied, 1)
                                pe.wait_ge(loaded["sel"], 16)
                            last = pe.matmul(acc, row_g[0:8, hd.fox * P:(hd.fox + 1) * P], cum_k[0:8, 0:nk],
                                             start=False, stop=True)
                    last.then_inc(logits_ready, 1)

            def slots(stream, *numbers):
                return lambda: [slot(stream, s) for s in numbers]

            tile_of = lambda m, at=0: (lambda k, t: m[:, t, at + k * P:at + (k + 1) * P])

            pe.wait_ge(loaded["ident"], 16)

            def heads_banks(name):
                pe.wait_ge(turn_lo, TURNS[name][1])

            def turn_queries():
                pe.wait_ge(*read("ab_in", 2))
                turn("cq", tile_of(proj0), [(rms_done, 4)])

            gemm("ab_in", xt_hi, xt_lo, 0, "x0",
                 {7: lambda: turn("mem", tile_of(mem_x), [(rms_done, 1)], [0]),
                  8: lambda: turn("mem", tile_of(mem_x), [(rms_done, 2)], [1]), 
                  9: turn_queries,
                  10: lambda: [heads_banks("cq"), slot("l0", 0), turn("ckv", tile_of(proj0, Q_RANK), [(rms_done, 6)])],
                  11: slots("l0", 1)},
                 second=lambda t: turn("x0", tile_of(x), [(loaded[f"x{t}"], 16)], [t]))
            pe.wait_ge(turn_lo, turned_at("ckv", 1, 1))
            gemm("uq", ht_hi, ht_lo, 8, "cq", {n: slots("l0", 2 + n) for n in range(3)})
            gemm("ukv", ht_hi, ht_lo, 11, "ckv", {n: slots("l0", 5 + n) for n in range(2)})
            gemm("mem_k", ht_hi, ht_lo, 0, None, {n: slots("l0", 7 + n) for n in range(4)})

            def first_results(name, src, heads, free):
                pe.wait_ge(*free)
                turn(name, tile_of(src), [(head_done, heads)])

            gemm("mem_v", ht_hi, ht_lo, 0, None,
                 {0: slots("l0", 11), 1: lambda: [slot("l0", 12), first_results("o0a", o0, 8, read("mem_k", 1))],
                  2: slots("l0", 13), 3: slots("l0", 14)})

            def after_norm(name, k):
                return lambda t: turn_tile(name, x, t, x_ready, 4 * k + 2 * t + 1)

            def last_results(name, src, stream, s):
                slots(stream, *s)()
                turn(name, tile_of(src, 4 * P), [(head_done, STREAMS[stream][1])])

            wide("ab_out", xt_hi, xt_lo, ("o0a", "o0b"),
                 between={0: slots("l0", 15), 1: slots("l0", 16), 2: slots("l0", 17),
                          3: lambda: last_results("o0b", o0, "l0", [18])})
            second = after_norm("f0", 0)
            wide("down0", ht_hi, ht_lo, "h0", between={1: up(0, second)})
            second = after_norm("x1", 1)

            def cumulate():
                pe.wait_ge(log_f_ready, 1)
                pe.wait_ge(loaded["cum"], 16)
                for t in range(TT):
                    last = pe.matmul(psum[0:FOX_H, O_BANK, 0:S], log_f[:, 3, t, :], cum_tri[:, t, :],
                                     start=(t == 0), stop=(t == TT - 1))
                last.then_inc(cum_ready, 1)

            gemm("cd_in", xt_hi, xt_lo, 0, "x1",
                 {7: lambda: [heads_banks("o1a"), cumulate()], **{n: slots("l1", s) for n, s in L1_SLOTS.items()},
                  24: lambda: first_results("o1a", o1, 24, read("cd_in", 6))},
                 second=second)
            wide("cd_out", ht_hi, ht_lo, ("o1a", "o1b"),
                 between={0: slots("l1", 14), 1: slots("l1", 15), 2: slots("l1", 16),
                          3: lambda: last_results("o1b", o1, "l1", [17, 18])})
            second = after_norm("f1", 2)
            wide("down1", ht_hi, ht_lo, "h1", between={1: up(1, second)})
            second = after_norm("x2", 3)
            gemm("in_a", xt_hi, xt_lo, 0, "x2", second=second)

            def moba_first():
                heads_banks("a")
                pe.wait_ge(moba_ready, 1)
                pe.wait_ge(*read("in_a", 6))
                slot("moba", 0)

            gemm("in_b", xt_hi, xt_lo, 0, None, {2: moba_first, **{2 + s: slots("moba", s) for s in range(1, 9)}})
            gemm("in_b_end", xt_hi, xt_lo)

            def mix(groups):
                for g in groups:
                    if g == 0:
                        pe.wait_ge(vn_ready, 1)
                        pe.wait_ge(wsp_ready, 1)
                    if g >= 2:
                        pe.wait_ge(gated_b, g - 1)
                    pe.matmul(psum[:, PT_BANK + g % 2, 0:S].rearrange("p (t n) -> p t n", t=TT), wsp[:, g, :],
                              b2[:, :, BW + g * P:BW + (g + 1) * P], start=True, stop=True).then_inc(mixed, 1)

            gemm("in_c", xt_hi, xt_lo, 0, None,
                 {0: lambda: turn("a", tile_of(a2), [(head_done, 38)], [0]),
                  1: lambda: turn("a", tile_of(a2), [(head_done, 38)], [1]),
                  **{2 + g: lambda g=g: mix([g]) for g in range(6)}})

            def xa_first():
                pe.wait_ge(*read("in_c", 2))
                heads_banks("b")
                pe.wait_ge(gated_b, 6)
                slot("xa", 0)

            gemm("gate_a", xt_hi, xt_lo, 0, None, {0: xa_first, **{s: slots("xa", s) for s in range(1, 7)}})
            gemm("branch_a", ht_hi, ht_lo, 0, "a",
                 {0: lambda: turn("b", tile_of(b2), [(gated_b, 6), (head_done, 42)], [0]),
                  1: lambda: turn("b", tile_of(b2), [], [1]),
                  2: lambda: turn("c", tile_of(c2), [(head_done, 42)])})
            gemm("gate_b", xt_hi, xt_lo)
            gemm("branch_b", ht_hi, ht_lo, 6, "b")
            gemm("gate_c", xt_hi, xt_lo)
            wide("branch_c", ht_hi, ht_lo, "c", 12)
            wide("out", xt_hi, xt_lo, "y", head=NS, 
                 second=lambda t: turn_tile("y", y2, t, y_ready, 5 + 2 * t))

        @block.scalar
        def _(act):
            done = {"chunks": 0, "steps": 0, "due": 0}

            def settle(ins):
                done["steps"] += 1
                ins.then_inc(act_step, 1)
                act.wait_ge(act_step, done["steps"])

            def split_hi(c, i=None, per_turn=0):
                s, w = c % NS, WIDTH[c]
                act.wait_ge(staged[s], plus(16 * (c // NS + 1), i, 16 * per_turn // NS))
                if c >= NS or i is not None:
                    act.wait_ge(chunk_used, plus(c - NS + 1, i, per_turn))
                act.copy(w_hi[:, s, 0:w], stage[:, s, 0:w]).then_inc(hi_done, 1)

            def split_to(c):
                while done["chunks"] < min(c, CHUNKS):
                    split_hi(done["chunks"])
                    done["chunks"] += 1

            def gemm(name, evacuate=None, between=None, after=()):
                g = GEMMS[name]
                cps = g.kc // g.kp
                for j in range(g.steps):
                    for n in range(j * cps, (j + 1) * cps):
                        done["due"] = g.c0 + n + 1 + LEAD
                        if evacuate is not None and n == (j + 1) * cps - 1:
                            for s, v in after if j == 0 else ():
                                act.wait_ge(s, v)
                            pair = (g.u0 + j) % 2
                            act.wait_ge(chunk_used, g.c0 + n + 1)
                            for t in range(TT):
                                evacuate(j, t, psum[:, 2 * pair + t, :]).then_inc(acc_free[pair], 1)
                        if between and n in between:
                            between[n]()
                        split_to(done["due"])

            def turn(name, hi, k0=0, tiles=range(TT)):
                for part in turn_parts(name, tiles):
                    turn_part(part, name, hi, k0)

            def turn_part(part, name, hi=xt_hi, k0=0):
                g, t, k, w = part
                act.wait_ge(turned, g + 1)
                act.copy(hi[:, k0 + k:k0 + k + w, t * P:(t + 1) * P],
                         turn_bank(name, g)[:, 0:w * P].rearrange("p (k n) -> p k n", k=w)).then_inc(turn_hi, 1)

            def turn_scaled(part, name="x2"):
                g, t, k, w = part
                act.wait_ge(loaded["norm_g"], 16)
                act.wait_ge(turned, g + 1)
                for n in range(w):
                    last = act.activation(xt_hi[:, k + n, t * P:(t + 1) * P], turn_bank(name, g)[:, n * P:(n + 1) * P],
                                          ACT.Copy, scale=norm_g[:, k + n:k + n + 1])
                last.then_inc(turn_hi, 1)

            def turn_hidden(layer, j, dst, i=None):
                name = f"h{layer}"
                g = TURNS[name][1] + j
                act.wait_ge(turned, plus(g + 1, i, 2))
                act.copy(dst, turn_bank(name, g).rearrange("p (k n) -> p k n", k=2)).then_inc(turn_hi, 1)

            def wide(name, between=None):
                g = GEMMS[name]
                for k in range(g.kc):
                    done["due"] = min(g.c0 + k + 1 + LEAD, g.c0 + g.kc)
                    if between and k in between:
                        between[k]()
                    split_to(done["due"])

            def slot(stream, s):
                lo_h, hi_h = STREAMS[stream]
                h = lo_h + s - 2
                if lo_h <= h < hi_h:
                    hd = head_of(h)
                    w = 4 * P if hd.full else 3 * P
                    act.wait_ge(p_turned, h + 1)
                    if h >= 2:
                        act.wait_ge(pv_ready, h - 1)
                    act.copy(probs_t[:, h % 2, 0:w], psum[:, PT_BANK, 0:w]).then_inc(p_copied, 1)
                split_to(done["due"])
                h = lo_h + s - 1
                if lo_h <= h < hi_h:
                    hd = head_of(h)
                    n0, b = keys0(hd), h % 4
                    act.wait_ge(max_ready, h + 1)
                    if hd.sink is not None:
                        act.activation(soft[:, b, 3, :], soft[:, b, 1, :], ACT.Exp,
                                       bias=head_par[:, 0, hd.sink:hd.sink + 1])
                    for t in range(TT):
                        p = probs[:, h % 2, t * n0:t * n0 + (S if t else n0)]
                        last = act.activation(p, p, ACT.Exp, bias=soft[:, b, 1, t:t + 1],
                                              accum_out=soft[:, b, 2, t:t + 1])
                    last.then_inc(exp_ready, 1)

            def slots(stream, *numbers):
                return lambda: [slot(stream, s) for s in numbers]

            def rms(k, src, junk, n, ready, tiles=range(TT)):
                for t in tiles:
                    for s, v in ready(t) if callable(ready) else ready:
                        act.wait_ge(s, v)
                    settle(act.activation(junk, src(t), ACT.Square, accum_out=rms_st[:, k, 0, t:t + 1]))
                    act.activation(rms_st[:, k, 1, t:t + 1], rms_st[:, k, 0, t:t + 1], ACT.Sqrt, scale=1.0 / n,
                                   bias=eps[:, 1:2]).then_inc(rms_sd, 1)

            def deviation(k, t, which_eps=0):
                act.wait_ge(ln_var, TT * k + t + 1)
                act.activation(ln_st[:, k, 28 + t:29 + t], ln_st[:, k, 25 + 2 * t:26 + 2 * t], ACT.Sqrt,
                               bias=eps[:, which_eps:which_eps + 1]).then_inc(ln_sd, 1)

            def norm_and_turn(k, name):
                end = done["chunks"]
                act.preload_act_table(ACT.Sqrt)
                deviation(k, 0)
                split_to(end + LEAD)
                first, last = turn_parts(name, [0])
                turn_part(first, name)
                split_to(end + NS)
                turn_part(last, name)
                deviation(k, 1)
                turn(name, xt_hi, 0, [1])

            def copy_to(dst):
                return lambda j, t, acc: act.copy(*dst(j, t, acc))

            def up(layer):
                g, name = GEMMS[f"up{layer}"], f"h{layer}"
                cps = g.kc // g.kp
                act.preload_act_table(ACT.Silu)

                def one(j, i=None):
                    for m in range(cps):
                        if i is None:
                            split_to(g.c0 + j * cps + m + 1 + LEAD)
                        else:
                            split_hi(g.c0 + j * cps + m + LEAD, i, 2 * cps)
                        if m == 1 and j:
                            k = 2 * (j - 1)
                            turn_hidden(layer, j - 1,
                                        ht_hi[:, k:k + 2, :] if i is None else ht_hi[:, bass.ds(i * 4 + k, 2), :], i)
                    pair = (g.u0 + j) % 2
                    act.wait_ge(chunk_used, plus(g.c0 + (j + 1) * cps, i, 2 * cps))
                    for t in range(TT):
                        act.activation(u_tile[:, j % 2, t, :], psum[:, 2 * pair + t, 0:256], ACT.Silu
                                       ).then_inc(silu_ready, 1)

                one(0)
                assert done["chunks"] == g.c0 + cps + LEAD
                with act.Fori(0, 4) as i:
                    for s in range(2):
                        one(1 + s, i)
                done["chunks"] += 8 * cps
                one(9)
                one(10)

            def down(layer):
                wide(f"down{layer}", {1: lambda: turn_hidden(layer, 10, ht_hi[:, 20:22, :])})

            act.preload_act_table(ACT.Sqrt)
            turn("x0", xt_hi, 0, [0])
            split_to(NS)
            turn("x0", xt_hi, 0, [1])

            def memory_norm():
                act.wait_ge(constants_set, 3)
                rms(0, lambda t: mem_x[:, t, :], arena[:, Q0:Q0 + D], D, [(loaded["mem"], 16)])

            def low_rank_norms():
                rms(1, lambda t: proj0[:, t, 0:Q_RANK], arena[:, K0:K0 + Q_RANK], Q_RANK, [read("ab_in", 2)])
                rms(2, lambda t: proj0[:, t, Q_RANK:Q_RANK + KV_RANK], arena[:, K0:K0 + KV_RANK], KV_RANK, [])

            def first_slot():
                act.wait_ge(loaded["heads"], 16)
                slot("l0", 0)

            gemm("ab_in", copy_to(lambda j, t, acc: (proj0[:, t, j * 480:(j + 1) * 480], acc[:, 0:480])),
                 {4: memory_norm, 7: lambda: [turn("mem", ht_hi, 0, [0]), low_rank_norms()],
                  8: lambda: turn("mem", ht_hi, 0, [1]),
                  9: lambda: [turn("cq", ht_hi, 8), act.preload_act_table(ACT.Exp)],
                  10: lambda: [first_slot(), turn("ckv", ht_hi, 11)], 11: slots("l0", 1)})
            gemm("uq", copy_to(lambda j, t, acc: (q0[:, t, j * 256:(j + 1) * 256], acc[:, 0:256])),
                 {n: slots("l0", 2 + n) for n in range(3)})

            def split_kv(j, t, acc):
                kv = acc.rearrange("p (h n) -> p h n", h=4)
                settle(act.copy(k0[:, t, 4 * j:4 * j + 4, 0:MLA_NOPE], kv[:, :, 0:MLA_NOPE]))
                return act.copy(v0[:, t, 4 * j:4 * j + 4, :], kv[:, :, MLA_NOPE:])

            gemm("ukv", split_kv, {n: slots("l0", 5 + n) for n in range(2)})
            gemm("mem_k", copy_to(lambda j, t, acc: (mem_k[:, t, :], acc)),
                 {n: slots("l0", 7 + n) for n in range(4)})
            gemm("mem_v", copy_to(lambda j, t, acc: (mem_v[:, t, :], acc)),
                 {0: slots("l0", 11), 1: lambda: [slot("l0", 12), turn("o0a", xt_hi)],
                  2: slots("l0", 13), 3: slots("l0", 14)})
            wide("ab_out", {0: slots("l0", 15), 1: slots("l0", 16), 2: slots("l0", 17),
                            3: lambda: [slot("l0", 18), turn("o0b", xt_hi, 4)]})
            norm_and_turn(0, "f0")
            up(0)
            down(0)
            norm_and_turn(1, "x1")

            def log_sigmoid():
                act.wait_ge(f_abs, 1)
                settle(act.activation(log_f[:, 2, :, :], log_f[:, 1, :, :], ACT.Exp, scale=-1.0))
                act.activation(log_f[:, 1, :, :], log_f[:, 2, :, :], ACT.Ln, bias=1.0).then_inc(f_ln, 1)

            gemm("cd_in", copy_to(lambda j, t, acc: (proj1[:, t, j * 440:(j + 1) * 440], acc[:, 0:440])),
                 {4: log_sigmoid, **{n: slots("l1", s) for n, s in L1_SLOTS.items()},
            24: lambda: turn("o1a", ht_hi)})
            wide("cd_out", {0: slots("l1", 14), 1: slots("l1", 15), 2: slots("l1", 16),
                            3: lambda: [slots("l1", 17, 18)(), turn("o1b", ht_hi, 4)]})
            norm_and_turn(2, "f1")
            up(1)
            down(1)
            act.preload_act_table(ACT.Sqrt)
            end = done["chunks"]
            deviation(3, 0)
            split_to(end + LEAD)
            first, last = turn_parts("x2", [0])
            turn_scaled(first)
            split_to(end + NS)
            turn_scaled(last)
            h_junk = arena[:, B2:B2 + D]
            rms(3, lambda t: x[:, t, :], h_junk, D, lambda t: [(x_ready, 14 + 2 * t)], [0])
            deviation(3, 1)
            for part in turn_parts("x2", [1]):
                turn_scaled(part)
            rms(3, lambda t: x[:, t, :], h_junk, D, lambda t: [(x_ready, 14 + 2 * t)], [1])
            root = lambda t: rms_st[:, 3, 2, t:t + 1]
            act.wait_ge(rms_done, 8)

            def pieces(dst, gate_from):
                def evacuate(j, t, acc, n=512):
                    at = j * 512
                    cut = min(max(gate_from - at, 0), n)
                    if 0 < cut < n:
                        settle(act.activation(dst[:, t, at:at + cut], acc[:, 0:cut], ACT.Copy, scale=root(t)))
                    if cut < n:
                        return act.activation(dst[:, t, at + cut:at + n], acc[:, cut:n], ACT.Silu,
                                              scale=root(t))
                    return act.activation(dst[:, t, at:at + n], acc[:, 0:n], ACT.Copy, scale=root(t))
                return evacuate

            gemm("in_a", pieces(a2, 3 * AW))
            gemm("in_b", pieces(b2, 2 * BW), {**{2 + s: slots("moba", s) for s in range(9)},
                                              14: lambda: [deviation(4, 0, 1), deviation(4, 1, 1)]})
            gemm("in_b_end", lambda j, t, acc: pieces(b2, 2 * BW)(4, t, acc, 256))
            gemm("in_c", pieces(c2, CW), {0: lambda: turn("a", ht_hi, 0, [0]), 1: lambda: turn("a", ht_hi, 0, [1])})

            def gate(j, t, acc):
                return act.activation(sig[:, t, j * 512:(j + 1) * 512], acc, ACT.Sigmoid, scale=root(t))

            act.wait_ge(x_ready, 16)
            gemm("gate_a", gate, {s: slots("xa", s) for s in range(7)})
            gemm("branch_a", None, {0: lambda: turn("b", ht_hi, 6, [0]), 1: lambda: turn("b", ht_hi, 6, [1]),
                                    2: lambda: turn("c", ht_hi, 12)})
            gemm("gate_b", gate, after=[read("branch_a", 2)])
            gemm("branch_b")
            gemm("gate_c", gate, after=[(y_ready, 4)])
            wide("branch_c")
            end = done["chunks"]
            split_to(end + LEAD)
            turn("y", xt_hi, 0, [0])
            split_to(end + NS)
            turn("y", xt_hi, 0, [1])
            wide("out")
            act.preload_act_table(ACT.Sqrt)
            for t in range(TT):
                for j, junk in enumerate((B2, B2 + 512)):
                    act.wait_ge(x_ready, 16 + 2 * t + j + 1)
                    act.activation(arena[:, junk:junk + 512], x[:, t, j * 512:(j + 1) * 512], ACT.Square,
                                   accum_out=rms_st[:, 4, j, t:t + 1]).then_inc(final_sum, 1)
                act.wait_ge(final_sum, 3 * t + 3)
                act.activation(rms_st[:, 4, 1, t:t + 1], rms_st[:, 4, 0, t:t + 1], ACT.Sqrt, scale=1.0 / D,
                               bias=eps[:, 1:2]).then_inc(rms_sd, 1)

        @block.vector
        def _(dve):
            done = {"chunks": 0, "steps": 0}

            def settle(ins):
                done["steps"] += 1
                ins.then_inc(dve_step, 1)
                dve.wait_ge(dve_step, done["steps"])

            def split_lo(c, i=None, per_turn=0):
                s, w = c % NS, WIDTH[c]
                dve.wait_ge(hi_done, plus(c + 1, i, per_turn))
                dve.tensor_tensor(w_lo[:, s, 0:w], stage[:, s, 0:w], w_hi[:, s, 0:w].bitcast(F32), ALU.subtract
                                  ).then_inc(lo_done, 1)

            def split_to(c):
                while done["chunks"] < min(c, CHUNKS):
                    split_lo(done["chunks"])
                    done["chunks"] += 1

            def gemm(name, evacuate=None, between=None):
                g = GEMMS[name]
                cps = g.kc // g.kp
                for j in range(g.steps):
                    for n in range(j * cps, (j + 1) * cps):
                        if evacuate is not None and n == (j + 1) * cps - 1:
                            u = g.u0 + j
                            dve.wait_ge(chunk_used, g.c0 + n + 1)
                            for t in range(TT):
                                evacuate(j, t, psum[:, 2 * (u % 2) + t, 0:g.n], acc_free[u % 2],
                                         2 * (u // 2) + t + 1)
                        if between and n in between:
                            between[n]()
                        split_to(g.c0 + n + 1 + LEAD)

            def turn(name, hi, lo, k0=0, tiles=range(TT)):
                for part in turn_parts(name, tiles):
                    turn_part(part, hi, lo, k0, name)

            def turn_part(part, hi, lo, k0, name):
                g, t, k, w = part
                dst = (slice(None), slice(k0 + k, k0 + k + w), slice(t * P, (t + 1) * P))
                dve.wait_ge(turn_hi, g + 1)
                if name == "x2":
                    for n in range(w):
                        dst = (slice(None), k + n, slice(t * P, (t + 1) * P))
                        last = dve.scalar_tensor_tensor(lo[dst], turn_bank(name, g)[:, n * P:(n + 1) * P],
                                                        norm_g[:, k + n:k + n + 1], hi[dst].bitcast(F32),
                                                        ALU.mult, ALU.subtract)
                    last.then_inc(turn_lo, 1)
                    return
                dve.tensor_tensor(lo[dst], turn_bank(name, g)[:, 0:w * P].rearrange("p (k n) -> p k n", k=w),
                                  hi[dst].bitcast(F32), ALU.subtract).then_inc(turn_lo, 1)

            def turn_hidden(layer, j, at, i=None):
                name = f"h{layer}"
                g = TURNS[name][1] + j
                dve.wait_ge(turn_hi, plus(g + 1, i, 2))
                dve.tensor_tensor(ht_lo[:, at, :], turn_bank(name, g).rearrange("p (k n) -> p k n", k=2),
                                  ht_hi[:, at, :].bitcast(F32), ALU.subtract).then_inc(turn_lo, 1)

            def wide(name, between=None):
                g = GEMMS[name]
                for k in range(g.kc):
                    if between and k in between:
                        between[k]()
                    split_to(min(g.c0 + k + 1 + LEAD, g.c0 + g.kc))

            def halves(name, t, evacuate):
                g = GEMMS[name]
                for j in range(2):
                    if (t, j) == (1, 1):
                        dve.wait_ge(chunk_used, g.c0 + g.kc)
                    else:
                        dve.wait_ge(half_done, 3 * WIDE.index(name) + 2 * t + j + 1)
                    u = g.u0 + j
                    evacuate(j, t, psum[:, 2 * (u % 2) + t, :], acc_free[u % 2], 2 * (u // 2) + t + 1)

            def slot(stream, s):
                lo_h, hi_h = STREAMS[stream]
                h = lo_h + s
                if lo_h <= h < hi_h and not (paired(h) and h % 2):
                    dim = P if paired(h) else head_of(h).dim
                    dve.wait_ge(qk_turned, turns_of(h))
                    if last_user(h) >= 0:
                        dve.wait_ge(logits_ready, last_user(h) + 1)
                    dve.tensor_copy(qk_t[0:dim, qk_buffer(h), :], psum[0:dim, QK_BANK, :]).then_inc(qk_copied, 1)
                h = lo_h + s - 3
                if lo_h <= h < hi_h:
                    hd = head_of(h)
                    dve.wait_ge(pv_ready, h + 1)
                    dv = hd.v(0).shape[-1]
                    for t in range(TT):
                        o, r = psum[:, O_BANK, t * dv:(t + 1) * dv], soft[:, h % 4, 4, t:t + 1]
                        if hd.gate is None:
                            last = dve.tensor_scalar(hd.out(t), o, r, None, ALU.mult)
                        else:
                            last = dve.scalar_tensor_tensor(hd.out(t), o, r, hd.gate(t), ALU.mult, ALU.mult)
                    last.then_inc(head_done, 1)
                h = lo_h + s - 2
                if lo_h <= h < hi_h:
                    hd = head_of(h)
                    b = h % 4
                    dve.wait_ge(exp_ready, h + 1)
                    if hd.sink is not None:
                        settle(dve.tensor_tensor(soft[:, b, 2, :], soft[:, b, 2, :], soft[:, b, 3, :], ALU.add))
                    settle(dve.reciprocal(soft[:, b, 4, :], soft[:, b, 2, :]))
                h = lo_h + s - 1
                if lo_h <= h < hi_h:
                    hd = head_of(h)
                    n0, b = keys0(hd), h % 4
                    if h == 24:
                        dve.wait_ge(rel_ready, 2)
                    dve.wait_ge(logits_ready, h + 1)
                    if h >= 2:
                        dve.wait_ge(p_turned, h - 1)
                    for t in range(TT):
                        at, nk = t * n0, S if t else n0
                        added = no_mask[:, 0:nk] if hd.mask is None else hd.mask[:, at:at + nk]
                        last = dve.tensor_tensor_reduce(probs[:, h % 2, at:at + nk], psum[:, LOGIT_BANK, at:at + nk],
                                                        added, hd.scale, -3e38, ALU.add, ALU.max,
                                                        soft[:, b, 0, t:t + 1])
                    settle(last)
                    if hd.sink is None:
                        last = dve.tensor_scalar(soft[:, b, 1, :], soft[:, b, 0, :], -1.0, None, ALU.mult)
                    else:
                        last = dve.tensor_scalar(soft[:, b, 1, :], soft[:, b, 0, :],
                                                 head_par[:, 0, hd.sink:hd.sink + 1], -1.0, ALU.max, ALU.mult)
                    last.then_inc(max_ready, 1)

            def slots(stream, *numbers):
                return lambda: [slot(stream, s) for s in numbers]

            def rms(k, src, dst, gain, tiles=range(TT)):
                for t in tiles:
                    dve.wait_ge(rms_sd, TT * k + t + 1)
                    settle(dve.reciprocal(rms_st[:, k, 2, t:t + 1], rms_st[:, k, 1, t:t + 1]))
                    dve.scalar_tensor_tensor(dst(t), src(t), rms_st[:, k, 2, t:t + 1], gain, ALU.mult, ALU.mult
                                             ).then_inc(rms_done, 1)

            def statistics(k, t, n, part):
                return dve.bn_stats(ln_st[:, k, 12 * t + 6 * n:12 * t + 6 * n + 6], part)

            def variance(k, t):
                dve.bn_aggr(ln_st[:, k, 24 + 2 * t:26 + 2 * t], ln_st[:, k, 12 * t:12 * t + 12]).then_inc(ln_var, 1)

            def deviate(k, t, m, gain, first=True):
                r = ln_st[:, k, 30 + t:31 + t]
                if first:
                    dve.wait_ge(ln_sd, TT * k + t + 1)
                    dve.reciprocal(r, ln_st[:, k, 28 + t:29 + t])
                settle(dve.scalar_tensor_tensor(m, m, ln_st[:, k, 24 + 2 * t:25 + 2 * t], gain,
                                                ALU.subtract, ALU.mult))
                return r

            def sum_tile(k, name, t):
                def evacuate(j, t, acc, freed, count):
                    part = x[:, t, j * 512:(j + 1) * 512]
                    dve.scalar_tensor_tensor(part, part, ALPHA, acc, ALU.mult, ALU.add).then_inc(freed, 1)

                halves(name, t, evacuate)
                for j in range(2):
                    u = GEMMS[name].u0 + j
                    dve.wait_ge(acc_free[u % 2], 2 * (u // 2) + t + 1)
                    last = statistics(k, t, j, x[:, t, j * 512:(j + 1) * 512])
                settle(last)
                variance(k, t)

            def norm_tile(k, t):
                dve.wait_ge(loaded[f"ln{k}"], 16)
                for j in range(2):
                    part = x[:, t, j * 512:(j + 1) * 512]
                    r = deviate(k, t, part, ln_par[:, 0, j * 512:(j + 1) * 512], j == 0)
                    dve.scalar_tensor_tensor(part, part, r, ln_par[:, 1, j * 512:(j + 1) * 512],
                                             ALU.mult, ALU.add).then_inc(x_ready, 1)

            def turn_and_split(name):
                for part in turn_parts(name, [0]):
                    split_to(done["chunks"] + 1)
                    turn_part(part, xt_hi, xt_lo, 0, name)

            def join_pool():
                for _ in range(2):
                    dve.wait_ge(*chunk_lo(done["chunks"]))
                    dve.nop().then_inc(lo_done, 1)
                    done["chunks"] += 1

            def norm_and_turn(k, projection, name):
                sum_tile(k, projection, 0)
                norm_tile(k, 0)
                turn_and_split(name)
                sum_tile(k, projection, 1)
                norm_tile(k, 1)
                turn(name, xt_hi, xt_lo, 0, [1])
                join_pool()

            def rotate(a, b, cos, sin, tmp):
                settle(dve.tensor_tensor(tmp(0), a, cos, ALU.mult))
                settle(dve.tensor_tensor(tmp(1), b, sin, ALU.mult))
                settle(dve.tensor_tensor(tmp(2), a, sin, ALU.mult))
                settle(dve.tensor_tensor(tmp(3), b, cos, ALU.mult))
                settle(dve.tensor_tensor(a, tmp(0), tmp(1), ALU.subtract))
                settle(dve.tensor_tensor(b, tmp(2), tmp(3), ALU.add))

            def angles(n, heads):
                return view(rope[:, n, :, :], 0, [[16, TT], [0, heads], [1, 16]])

            def up(layer):
                g, name = GEMMS[f"up{layer}"], f"h{layer}"
                cps = g.kc // g.kp
                silus = layer * 2 * g.steps

                def one(j, i=None):
                    for m in range(cps):
                        if i is None:
                            split_to(g.c0 + j * cps + m + 1 + LEAD)
                        else:
                            split_lo(g.c0 + j * cps + m + LEAD, i, 2 * cps)
                        if m == 1 and j:
                            k = 2 * (j - 1)
                            turn_hidden(layer, j - 1, slice(k, k + 2) if i is None else bass.ds(i * 4 + k, 2), i)
                    pair = (g.u0 + j) % 2
                    for t in range(TT):
                        dve.wait_ge(silu_ready, plus(silus + 2 * j + t + 1, i, 4))
                        dve.tensor_tensor(h_tile[:, j % 2, t, :], u_tile[:, j % 2, t, :],
                                          psum[:, 2 * pair + t, 256:512], ALU.mult).then_inc(acc_free[pair], 1)

                one(0)
                assert done["chunks"] == g.c0 + cps + LEAD
                with dve.Fori(0, 4) as i:
                    for s in range(2):
                        one(1 + s, i)
                done["chunks"] += 8 * cps
                one(9)
                one(10)

            def down(layer):
                wide(f"down{layer}", {1: lambda: turn_hidden(layer, 10, slice(20, 22))})

            dve.memset(eps[:, 0:1], LN_EPS).then_inc(constants_set, 1)
            dve.memset(eps[:, 1:2], RMS_EPS).then_inc(constants_set, 1)
            turn("x0", xt_hi, xt_lo, 0, [0])
            split_to(NS)
            turn("x0", xt_hi, xt_lo, 0, [1])

            def memory_norm():
                dve.wait_ge(loaded["mem_g"], 16)
                rms(0, lambda t: mem_x[:, t, :], lambda t: mem_x[:, t, :], row_g[:, :])

            def copy_key(g):
                dve.wait_ge(*read("ab_in", 2 + g))
                at = SWA_AT + g * SWA_GROUP
                dve.tensor_copy(twice_k[:, :, g, :].rearrange("p t (a n) -> p t a n", a=2),
                                view(proj0[:, 0, at:at + HD], 0, [[AB_W, TT], [0, 2], [1, HD]])
                                ).then_inc(key_twice, 1)

            def first_slot():
                dve.wait_ge(loaded["swa"], 16)
                dve.wait_ge(loaded["heads"], 16)
                slot("l0", 0)

            def low_rank_norms():
                dve.wait_ge(loaded["gains"], 16)
                rms(1, lambda t: proj0[:, t, 0:Q_RANK], lambda t: proj0[:, t, 0:Q_RANK], gains[:, 0:Q_RANK])
                rms(2, lambda t: proj0[:, t, Q_RANK:Q_RANK + KV_RANK], lambda t: proj0[:, t, Q_RANK:Q_RANK + KV_RANK],
                    gains[:, Q_RANK:])

            def mla_keys():
                dve.wait_ge(loaded["rope"], 16)
                tmp = lambda n: arena[:, K0 + 512 + n * 64:K0 + 512 + n * 64 + TT * 16].rearrange(
                    "p (t h n) -> p t h n", t=TT, h=1)
                kr = proj0[:, :, Q_RANK + KV_RANK:SWA_AT].rearrange("p t (h n) -> p t h n", h=1)
                rotate(kr[:, :, :, 0:16], kr[:, :, :, 16:32], angles(0, 1), angles(1, 1), tmp)
                settle(dve.tensor_copy(k0[:, :, :, MLA_NOPE:],
                                       view(proj0[:, 0, Q_RANK + KV_RANK:SWA_AT], 0,
                                            [[AB_W, TT], [0, MLA_H], [1, MLA_ROPE]])))

            gemm("ab_in", None, {4: memory_norm, 7: lambda: [turn("mem", ht_hi, ht_lo, 0, [0]), low_rank_norms()],
                                 8: lambda: turn("mem", ht_hi, ht_lo, 0, [1]),
                                 9: lambda: [turn("cq", ht_hi, ht_lo, 8), copy_key(0)],
                                 10: lambda: [first_slot(), turn("ckv", ht_hi, ht_lo, 11)],
                                 11: slots("l0", 1)})
            gemm("uq", None, {0: lambda: [copy_key(1), slot("l0", 2)], 1: lambda: [slot("l0", 3), mla_keys()],
                              2: slots("l0", 4)})

            def mla_queries():
                dve.wait_ge(*read("uq", 3))
                q = q0.rearrange("p t (h n) -> p t h n", h=MLA_H)
                rotate(q[:, :, :, 64:80], q[:, :, :, 80:96], angles(0, 8), angles(1, 8),
                       lambda n: proj0[:, :, n * P:(n + 1) * P].rearrange("p t (h n) -> p t h n", h=8))
                dve.nop().then_inc(mla_ready, 1)
                slot("l0", 5)

            gemm("ukv", None, {0: mla_queries, 1: slots("l0", 6)})

            dve.wait_ge(loaded["masks"], 16)
            gemm("mem_k", None, {n: slots("l0", 7 + n) for n in range(4)})
            gemm("mem_v", None, {0: slots("l0", 11), 1: lambda: [slot("l0", 12), turn("o0a", xt_hi, xt_lo)],
                                 2: slots("l0", 13), 3: slots("l0", 14)})
            wide("ab_out", {0: slots("l0", 15), 1: slots("l0", 16), 2: slots("l0", 17),
                            3: lambda: [slot("l0", 18), turn("o0b", xt_hi, xt_lo, 4)]})
            norm_and_turn(0, "ab_out", "f0")
            up(0)
            down(0)
            norm_and_turn(1, "down0", "x1")

            def forget_abs():
                dve.wait_ge(*read("cd_in", 1))
                f = proj1[:, :, 0:FOX_H]
                bias = view(head_par[:, 1, :], 0, [[0, TT], [1, 8]])
                settle(dve.tensor_tensor(log_f[:, 0, :, :], f, bias, ALU.add))
                dve.scalar_tensor_tensor(log_f[:, 1, :, :], log_f[:, 0, :, :], -1.0, log_f[:, 0, :, :],
                                         ALU.mult, ALU.max).then_inc(f_abs, 1)

            def forget_log():
                dve.wait_ge(f_ln, 1)
                dve.scalar_tensor_tensor(log_f[:, 3, :, :], log_f[:, 0, :, :], 0.0, log_f[:, 1, :, :],
                                         ALU.min, ALU.subtract).then_inc(log_f_ready, 1)

            def copy_cumulated():
                dve.wait_ge(cum_ready, 1)
                dve.tensor_copy(cum_k[0:FOX_H, :], psum[0:FOX_H, O_BANK, 0:S]).then_inc(cum_copied, 1)

            gemm("cd_in", None, {4: forget_abs, 5: forget_log, 7: copy_cumulated,
                                 **{n: slots("l1", s) for n, s in L1_SLOTS.items()},
            24: lambda: turn("o1a", ht_hi, ht_lo)})
            wide("cd_out", {0: slots("l1", 14), 1: slots("l1", 15), 2: slots("l1", 16),
                            3: lambda: [slots("l1", 17, 18)(), turn("o1b", ht_hi, ht_lo, 4)]})
            norm_and_turn(2, "cd_out", "f1")
            up(1)
            down(1)
            def second_root(t):
                dve.wait_ge(rms_sd, TT * 3 + t + 1)
                dve.reciprocal(rms_st[:, 3, 2, t:t + 1], rms_st[:, 3, 1, t:t + 1]).then_inc(rms_done, 1)

            sum_tile(3, "down1", 0)
            norm_tile(3, 0)
            turn_and_split("x2")
            second_root(0)
            sum_tile(3, "down1", 1)
            norm_tile(3, 1)
            for part in turn_parts("x2", [1]):
                turn_part(part, xt_hi, xt_lo, 0, "x2")
            second_root(1)
            join_pool()

            def moba_positions():
                dve.wait_ge(*read("in_a", 3))
                tmp = lambda n: region(12800, 4 * 96)[:, :, n * 96:(n + 1) * 96].rearrange(
                    "p t (h n) -> p t h n", h=MOBA_H)
                for at in (0, AW):
                    m = a2[:, :, at:at + AW].rearrange("p t (h n) -> p t h n", h=MOBA_H)
                    rotate(m[:, :, :, 0:ROT2], m[:, :, :, ROT2:2 * ROT2], angles(2, MOBA_H), angles(3, MOBA_H), tmp)
                dve.nop().then_inc(moba_ready, 1)

            gemm("in_a", None, {13: moba_positions})

            def gmlp_stats():
                dve.wait_ge(*read("in_b", 3))
                for t in range(TT):
                    for n in range(2):
                        last = statistics(4, t, n, b2[:, t, BW + n * 384:BW + (n + 1) * 384])
                settle(last)
                for t in range(TT):
                    variance(4, t)

            def gmlp_norm():
                dve.wait_ge(loaded["gmlp_g"], 16)
                for t in range(TT):
                    v = b2[:, t, BW:2 * BW]
                    last = dve.tensor_scalar(v, v, deviate(4, t, v, row_g[:, 0:BW]), None, ALU.mult)
                last.then_inc(vn_ready, 1)

            gemm("in_b", None, {**{2 + s: slots("moba", s) for s in range(9)}, 13: gmlp_stats, 15: gmlp_norm})
            gemm("in_b_end")

            def gate_b(groups):
                dve.wait_ge(*read("in_b_end", 1))
                for g in groups:
                    dve.wait_ge(mixed, g + 1)
                    u = b2[:, :, g * P:(g + 1) * P]
                    acc = psum[:, PT_BANK + g % 2, 0:S].rearrange("p (t n) -> p t n", t=TT)
                    settle(dve.scalar_tensor_tensor(u, acc, bsp[:, g:g + 1], u, ALU.add, ALU.mult))
                    dve.tensor_tensor(u, u, b2[:, :, 2 * BW + g * P:2 * BW + (g + 1) * P], ALU.mult
                                      ).then_inc(gated_b, 1)

            gemm("in_c", None, {0: lambda: turn("a", ht_hi, ht_lo, 0, [0]), 1: lambda: turn("a", ht_hi, ht_lo, 0, [1]),
                                **{2 + g: lambda g=g: gate_b([g]) for g in range(6)}})
            gemm("gate_a", None, {s: slots("xa", s) for s in range(7)})

            def branch(n):
                def evacuate(j, t, acc, freed, count):
                    y, s = y2[:, t, j * 512:(j + 1) * 512], sig[:, t, j * 512:(j + 1) * 512]
                    dve.tensor_tensor(s if n else y, acc, s, ALU.mult).then_inc(freed, 1)
                    if n:
                        dve.wait_ge(freed, count)
                        dve.tensor_tensor(y, y, s, ALU.add).then_inc(y_ready, 1)
                return evacuate

            dve.wait_ge(*read("gate_a", 2))
            gemm("branch_a", branch(0), {0: lambda: turn("b", ht_hi, ht_lo, 6, [0]),
                                         1: lambda: turn("b", ht_hi, ht_lo, 6, [1]),
                                         2: lambda: turn("c", ht_hi, ht_lo, 12)})
            gemm("gate_b")
            dve.wait_ge(*read("gate_b", 2))
            gemm("branch_b", branch(1))
            gemm("gate_c")
            dve.wait_ge(*read("gate_c", 2))
            wide("branch_c")
            end = done["chunks"]
            halves("branch_c", 0, branch(2))
            split_to(end + LEAD)
            turn("y", xt_hi, xt_lo, 0, [0])
            halves("branch_c", 1, branch(2))
            split_to(end + NS)
            turn("y", xt_hi, xt_lo, 0, [1])
            wide("out")

            def last_residual(j, t, acc, freed, count):
                part = x[:, t, j * 512:(j + 1) * 512]
                dve.tensor_tensor(part, part, acc, ALU.add).then_inc(x_ready, 1)

            dve.wait_ge(loaded["final_g"], 16)
            for t in range(TT):
                halves("out", t, last_residual)
                dve.wait_ge(final_sum, 3 * t + 2)
                dve.tensor_tensor(rms_st[:, 4, 0, t:t + 1], rms_st[:, 4, 0, t:t + 1], rms_st[:, 4, 1, t:t + 1],
                                  ALU.add).then_inc(final_sum, 1)
                dve.wait_ge(rms_sd, TT * 4 + t + 1)
                settle(dve.reciprocal(rms_st[:, 4, 2, t:t + 1], rms_st[:, 4, 1, t:t + 1]))
                for j in range(2):
                    cut = slice(j * 512, (j + 1) * 512)
                    dve.scalar_tensor_tensor(a2_out(t)[:, cut], x[:, t, cut], rms_st[:, 4, 2, t:t + 1],
                                             row_g[:, cut], ALU.mult, ALU.mult).then_inc(rms_done, 1)


def chunks_of(w, name):
    g = GEMMS[name]
    w = w.reshape(g.kc // g.kp, g.kp, P, g.steps, g.n).transpose(3, 0, 2, 1, 4)
    return np.ascontiguousarray(w.reshape(-1, P, g.kp * g.n))


def shape_constants():
    q, k = np.arange(S)[:, None], np.arange(S)[None, :]
    by_chunk = np.where(k // CH <= q // CH, 0.0, MASKED)
    causal = np.where(k <= q, 0.0, MASKED)
    window = np.where((k // CH <= q // CH) & (k // CH >= q // CH - 2), 0.0, MASKED)

    def tiles(m):
        return np.concatenate([m[0:P, 0:P], m[P:S, :]], 1)

    slopes = np.exp2(-8.0 * np.arange(1, SWA_H + 1) / SWA_H)
    swa = np.stack([tiles(np.where(window < 0, MASKED, -s * np.abs(q - k) * HD ** 0.5)) for s in slopes], 1)

    def angles(theta, width):
        inv = np.float32(theta) ** (-np.arange(0, width, 2, dtype=np.float32) / np.float32(width))
        a = (np.arange(S, dtype=np.float32)[:, None] * inv[None, :].astype(np.float32)).astype(np.float64)
        return [f(a).reshape(TT, P, width // 2).transpose(1, 0, 2) for f in (np.cos, np.sin)]

    c = {"ident": np.eye(P), "masks": np.stack([tiles(by_chunk), tiles(causal)], 1), "swa": swa,
         "rope": np.stack(angles(10000.0, MLA_ROPE) + angles(500000.0, 2 * ROT2), 1),
         "cum": np.where(q <= k, -HD ** 0.5, 0.0).reshape(TT, P, S).transpose(1, 0, 2),
         "sel": np.repeat(np.eye(FOX_H), P, 1)}
    return {n: np.ascontiguousarray(a, dtype=np.float32) for n, a in c.items()}


def kernel(**inputs):
    import concourse.bacc as bacc
    from concourse.bass_utils import run_bass_kernel_spmd

    a = {k: np.asarray(v) for k, v in inputs.items()}
    w2 = a["w_in_2"][0]
    cut = np.cumsum([0, 4 * AW, 3 * BW, 2 * CW, D, D, D])
    in_a, in_b, in_c, gate_a, gate_b, gate_c = (w2[:, cut[n]:cut[n + 1]] for n in range(6))

    ab = a["ab_w_in"][0]
    low = Q_RANK + KV_RANK + MLA_ROPE
    q, k, v = (ab[:, low + m:low + n].reshape(D, SWA_KV, -1) for m, n in ((0, 512), (512, 640), (640, 768)))
    ab = np.concatenate([ab[:, :low], np.concatenate([k, v, q], 2).reshape(D, -1)], 1)
    cd = a["cd_w_in"][0]
    n = FOX_H * HD

    def by_head(w):
        return w.reshape(D, 3, 4, 2 * HD).transpose(0, 2, 1, 3).reshape(D, 3 * 8 * HD)

    cd = np.concatenate([cd[:, 3 * n:3 * n + FOX_H], by_head(cd[:, :3 * n]), by_head(cd[:, 3 * n + FOX_H:])], 1)

    def up_of(layer):
        g, u = (a[n][layer].reshape(D, FF // 256, 256) for n in ("ffn_w_gate", "ffn_w_up"))
        return np.stack([g, u], 2).reshape(D, 2 * FF)

    weights = {"ab_in": ab, "mem_k": a["w_mem_kv_2"][0][:, :CW], "uq": a["ab_w_uq"][0],
               "ukv": a["ab_w_ukv"][0], "mem_v": a["w_mem_kv_2"][0][:, CW:],
               "ab_out": np.roll(a["ab_w_out"][0], SWA_H * HD, 0),
               "up0": up_of(0), "down0": a["ffn_w_down"][0], "cd_in": cd, "cd_out": a["cd_w_out"][0],
               "up1": up_of(1), "down1": a["ffn_w_down"][1], "in_a": in_a, "in_b": in_b[:, :2048],
               "in_b_end": in_b[:, 2048:], "in_c": in_c, "gate_a": gate_a, "branch_a": a["w_branch_a_2"][0],
               "gate_b": gate_b, "branch_b": a["w_branch_b_2"][0], "gate_c": gate_c,
               "branch_c": a["w_branch_c_2"][0], "out": a["w_out_2"][0]}
    arrays = {"w_" + n: chunks_of(w, n) for n, w in weights.items()}
    rel = np.zeros((CK_H, REL_PITCH), np.float32)
    rel[:, CH:] = a["cd_rel_bias"][0].T
    arrays.update(
        x=a["x"][0], mem=a["mem_2"][0], mem_norm_g=a["mem_norm_g_2"][0], norm_g=a["norm_g_2"][0].reshape(8, P).T,
        final_g=a["final_norm_g_2"], gmlp_g=a["gmlp_ln_g_2"][0],
        gains=np.concatenate([a["ab_q_norm"][0], a["ab_kv_norm"][0]]),
        head_par=np.concatenate([a["ab_sinks"][0], a["cd_b_forget"][0]]),
        ln=np.stack([np.stack([a[f"{n}_g"][k], a[f"{n}_b"][k]]) for k in range(2) for n in ("ln1", "ln2")]),
        wsp=a["w_spatial_2"][0].transpose(2, 0, 1), bsp=a["b_spatial_2"][0].T, rel=rel, **shape_constants())
    arrays = {n: np.ascontiguousarray(m) for n, m in arrays.items()}

    nc = bacc.Bacc("TRN2", target_bir_lowering=False, num_devices=1)
    d = {n: nc.dram_tensor(f"in_{n}", m.shape, mybir.dt.from_np(m.dtype), kind="ExternalInput").ap()
         for n, m in arrays.items()}
    out = nc.dram_tensor("out_x", (S, D), F32, kind="ExternalOutput").ap()
    build_program(nc, d, out)
    r = run_bass_kernel_spmd(nc, [{f"in_{n}": m for n, m in arrays.items()}], core_ids=[0])
    return r.results[0]["out_x"].reshape(1, S, D)
```
